# Optimizing a Trainium2 kernel written in Bass

```python
import jax, jax.numpy as jnp
from jax import lax
import numpy as np

D_MODEL = 1024
BATCH = 1
SEQ = 256
DEPTH = 1

N_HEADS_ATTN = 8
HEAD_DIM = 64
ROPE_DIM = HEAD_DIM // 4
ROPE_THETA = 500000.0
N_HEADS_IDX = 8
IDX_DIM = 64
TOPK_MAX = 256
Q_BLOCK = 128
N_POOL_GROUPS = 4
POOL_GROUP_DIM = 64
POOL_WINDOWS = (2, 4, 8, 16)
N_MEM = 256
N_HEADS_MEM = 4
N_BRANCHES = 3
N_EXPERTS = 32
TOP_K = 4
D_EXPERT = D_MODEL
SWIGLU_ALPHA = 1.702
SWIGLU_LIMIT = 7.0
MOE_BLOCK = 128
EPS = 1e-6

ATTN_W = N_HEADS_ATTN * HEAD_DIM
POOL_W = N_POOL_GROUPS * POOL_GROUP_DIM
MEM_W = N_HEADS_MEM * HEAD_DIM
IDXQ_W = N_HEADS_IDX * IDX_DIM
IN_SPLITS = (ATTN_W, ATTN_W, ATTN_W, IDXQ_W, IDX_DIM, N_HEADS_IDX, POOL_W, MEM_W)
IN_W = sum(IN_SPLITS)

kernel_name = "hybrid_dsa_pool_memory_moe_block"

def rmsnorm(x, g):
    xf = x.astype(jnp.float32)
    y = xf * lax.rsqrt(jnp.mean(xf * xf, axis=-1, keepdims=True) + EPS)
    return (y * g.astype(jnp.float32)).astype(x.dtype)

def partial_rope(x, pos):
    half = ROPE_DIM // 2
    inv = jnp.power(jnp.float32(ROPE_THETA), -jnp.arange(half, dtype=jnp.float32) / half)
    ang = pos.astype(jnp.float32)[:, None] * inv[None, :]
    cos = jnp.cos(ang)[None, :, None, :]
    sin = jnp.sin(ang)[None, :, None, :]
    xr = x[..., :ROPE_DIM].astype(jnp.float32)
    x1, x2 = xr[..., :half], xr[..., half:]
    rot = jnp.concatenate([x1 * cos - x2 * sin, x2 * cos + x1 * sin], axis=-1).astype(x.dtype)
    return jnp.concatenate([rot, x[..., ROPE_DIM:]], axis=-1)

def dsa_attention(q, k, v, iq, ik, iw):
    B, S = q.shape[0], q.shape[1]
    n_top = min(TOPK_MAX, S // 4)
    nb = S // Q_BLOCK
    key_pos = jnp.arange(S, dtype=jnp.int32)
    gather = jax.vmap(lambda a, i: a[i])
    ikf = ik.astype(jnp.float32)

    def to_blocks(a):
        return jnp.moveaxis(a.reshape((B, nb, Q_BLOCK) + a.shape[2:]), 1, 0)

    def block(args):
        qb, iqb, iwb, start = args
        q_pos = start + jnp.arange(Q_BLOCK, dtype=jnp.int32)
        causal = key_pos[None, :] <= q_pos[:, None]
        sc = jnp.einsum('bqhd,bsd->bqhs', iqb.astype(jnp.float32), ikf) * (IDX_DIM ** -0.5)
        sc = jnp.einsum('bqhs,bqh->bqs', jax.nn.relu(sc), iwb.astype(jnp.float32))
        sc = jnp.where(causal[None], sc, -jnp.inf)
        _, sel = lax.top_k(sc, n_top)
        k_sel = gather(k, sel)
        v_sel = gather(v, sel)
        logits = jnp.einsum('bqhd,bqkhd->bhqk', qb, k_sel).astype(jnp.float32) * (HEAD_DIM ** -0.5)
        valid = sel <= q_pos[None, :, None]
        logits = jnp.where(valid[:, None], logits, -jnp.inf)
        p = jax.nn.softmax(logits, axis=-1).astype(v.dtype)
        return jnp.einsum('bhqk,bqkhd->bqhd', p, v_sel)

    starts = jnp.arange(nb, dtype=jnp.int32) * Q_BLOCK
    out = lax.map(block, (to_blocks(q), to_blocks(iq), to_blocks(iw), starts))
    return jnp.moveaxis(out, 0, 1).reshape(B, S, -1)

def multiscale_pool(u, w_group, scale):
    B, S = u.shape[0], u.shape[1]
    ug = u.reshape(B, S, N_POOL_GROUPS, POOL_GROUP_DIM)
    cs = jnp.cumsum(ug.astype(jnp.float32), axis=1)
    cs = jnp.concatenate([jnp.zeros_like(cs[:, :1]), cs], axis=1)
    t = jnp.arange(S, dtype=jnp.int32)[:, None]
    win = jnp.array(POOL_WINDOWS, dtype=jnp.int32)[None, :]
    lo = jnp.maximum(t + 1 - win, 0)
    g_idx = jnp.arange(N_POOL_GROUPS, dtype=jnp.int32)[None, :]
    win_sum = cs[:, 1:] - cs[:, lo, g_idx]
    cnt = (t + 1 - lo).astype(jnp.float32)[None, :, :, None]
    pooled = (win_sum / cnt - ug.astype(jnp.float32)).astype(u.dtype)
    mixed = jnp.einsum('bsgc,gcd->bsgd', pooled, w_group)
    return mixed.reshape(B, S, POOL_W) * scale

def memory_attention(qm, mem_n, w_mem_kv):
    B, S = qm.shape[0], qm.shape[1]
    M = mem_n.shape[1]
    kv = mem_n @ w_mem_kv
    km = kv[..., :MEM_W].reshape(B, M, N_HEADS_MEM, HEAD_DIM)
    vm = kv[..., MEM_W:].reshape(B, M, N_HEADS_MEM, HEAD_DIM)
    q = qm.reshape(B, S, N_HEADS_MEM, HEAD_DIM)
    logits = jnp.einsum('bshd,bmhd->bhsm', q, km).astype(jnp.float32) * (HEAD_DIM ** -0.5)
    p = jax.nn.softmax(logits, axis=-1).astype(vm.dtype)
    return jnp.einsum('bhsm,bmhd->bshd', p, vm).reshape(B, S, MEM_W)

def moe(xn, w_router, b_router, w_up, b_up, w_down, b_down):
    B, S, D = xn.shape
    N = B * S
    A = N * TOP_K
    xt = xn.reshape(N, D)
    logits = (xt @ w_router + b_router).astype(jnp.float32)
    top_val, top_idx = lax.top_k(logits, TOP_K)
    gate = jax.nn.softmax(top_val, axis=-1)
    e_flat = top_idx.reshape(A).astype(jnp.int32)
    tok_flat = jnp.repeat(jnp.arange(N, dtype=jnp.int32), TOP_K)
    g_flat = gate.reshape(A)
    order = jnp.argsort(e_flat)
    e_sorted = e_flat[order]
    counts = jnp.bincount(e_flat, length=N_EXPERTS).astype(jnp.int32)
    padded = ((counts + MOE_BLOCK - 1) // MOE_BLOCK) * MOE_BLOCK
    start = jnp.cumsum(counts) - counts
    pend = jnp.cumsum(padded)
    pstart = pend - padded
    dest = pstart[e_sorted] + (jnp.arange(A, dtype=jnp.int32) - start[e_sorted])
    n_rows = A + N_EXPERTS * MOE_BLOCK
    n_blocks = n_rows // MOE_BLOCK
    row_tok = jnp.full((n_rows,), N, jnp.int32).at[dest].set(tok_flat[order])
    row_gate = jnp.zeros((n_rows,), jnp.float32).at[dest].set(g_flat[order])
    block_e = jnp.minimum(
        jnp.searchsorted(pend, jnp.arange(n_blocks, dtype=jnp.int32) * MOE_BLOCK, side='right'),
        N_EXPERTS - 1).astype(jnp.int32)
    x_pad = jnp.concatenate([xt, jnp.zeros((1, D), xt.dtype)], axis=0)

    def expert_block(args):
        rows, e = args
        hb = x_pad[rows] @ w_up[e] + b_up[e]
        glu = jnp.minimum(hb[:, :D_EXPERT], SWIGLU_LIMIT)
        lin = jnp.clip(hb[:, D_EXPERT:], -SWIGLU_LIMIT, SWIGLU_LIMIT)
        act = glu * jax.nn.sigmoid(SWIGLU_ALPHA * glu) * (lin + 1.0)
        return act @ w_down[e] + b_down[e]

    y_rows = lax.map(expert_block, (row_tok.reshape(n_blocks, MOE_BLOCK), block_e)).reshape(n_rows, D)
    y = jnp.zeros((N + 1, D), jnp.float32).at[row_tok].add(row_gate[:, None] * y_rows.astype(jnp.float32))
    return y[:N].reshape(B, S, D).astype(xn.dtype)

def setup_inputs(seed: int = 0) -> dict:
    key = jax.random.key(seed)
    ks = jax.random.split(key, 24)
    f32 = jnp.float32
    L = DEPTH

    def nrm(k, shape, fan_in):
        return jax.random.normal(k, shape, f32) * (fan_in ** -0.5)

    def gain(k, shape):
        return 1.0 + 0.05 * jax.random.normal(k, shape, f32)

    def bias(k, shape, s=0.02):
        return s * jax.random.normal(k, shape, f32)

    return {
        "x": jax.random.normal(ks[0], (BATCH, SEQ, D_MODEL), f32),
        "mem": jax.random.normal(ks[1], (BATCH, N_MEM, D_MODEL), f32),
        "norm_mix_g": gain(ks[2], (L, D_MODEL)),
        "w_in": nrm(ks[3], (L, D_MODEL, IN_W), D_MODEL),
        "w_gate": nrm(ks[4], (L, D_MODEL, N_BRANCHES * D_MODEL), D_MODEL),
        "b_gate": bias(ks[5], (L, N_BRANCHES * D_MODEL)),
        "w_proj_attn": nrm(ks[6], (L, ATTN_W, D_MODEL), ATTN_W),
        "w_proj_pool": nrm(ks[7], (L, POOL_W, D_MODEL), POOL_W),
        "w_proj_mem": nrm(ks[8], (L, MEM_W, D_MODEL), MEM_W),
        "pool_w_group": nrm(ks[9], (L, N_POOL_GROUPS, POOL_GROUP_DIM, POOL_GROUP_DIM), POOL_GROUP_DIM),
        "pool_scale": gain(ks[10], (L, POOL_W)),
        "mem_norm_g": gain(ks[11], (L, D_MODEL)),
        "w_mem_kv": nrm(ks[12], (L, D_MODEL, 2 * MEM_W), D_MODEL),
        "w_out": nrm(ks[13], (L, D_MODEL, D_MODEL), D_MODEL),
        "norm_ffn_g": gain(ks[14], (L, D_MODEL)),
        "w_router": nrm(ks[15], (L, D_MODEL, N_EXPERTS), D_MODEL),
        "b_router": bias(ks[16], (L, N_EXPERTS), 0.01),
        "w_up": nrm(ks[17], (L, N_EXPERTS, D_MODEL, 2 * D_EXPERT), D_MODEL),
        "b_up": bias(ks[18], (L, N_EXPERTS, 2 * D_EXPERT)),
        "w_down": nrm(ks[19], (L, N_EXPERTS, D_EXPERT, D_MODEL), D_EXPERT),
        "b_down": bias(ks[20], (L, N_EXPERTS, D_MODEL)),
        "norm_final_g": gain(ks[21], (D_MODEL,)),
    }

def reference(x, mem, norm_mix_g, w_in, w_gate, b_gate, w_proj_attn, w_proj_pool, w_proj_mem,
              pool_w_group, pool_scale, mem_norm_g, w_mem_kv, w_out, norm_ffn_g,
              w_router, b_router, w_up, b_up, w_down, b_down, norm_final_g):
    B, S, D = x.shape
    pos = jnp.arange(S, dtype=jnp.int32)
    split_points = tuple(int(p) for p in np.cumsum(IN_SPLITS)[:-1])
    h = x
    for l in range(DEPTH):
        xn = rmsnorm(h, norm_mix_g[l])
        proj = xn @ w_in[l]
        q, k, v, iq, ik, iw, u, qm = jnp.split(proj, split_points, axis=-1)
        q = partial_rope(q.reshape(B, S, N_HEADS_ATTN, HEAD_DIM), pos)
        k = partial_rope(k.reshape(B, S, N_HEADS_ATTN, HEAD_DIM), pos)
        v = v.reshape(B, S, N_HEADS_ATTN, HEAD_DIM)
        iq = partial_rope(iq.reshape(B, S, N_HEADS_IDX, IDX_DIM), pos)
        ik = partial_rope(ik.reshape(B, S, 1, IDX_DIM), pos)[:, :, 0]
        iw = iw * (N_HEADS_IDX ** -0.5)
        y_attn = dsa_attention(q, k, v, iq, ik, iw)
        y_pool = multiscale_pool(u, pool_w_group[l], pool_scale[l])
        y_mem = memory_attention(qm, rmsnorm(mem, mem_norm_g[l]), w_mem_kv[l])
        gates = jax.nn.sigmoid(xn @ w_gate[l] + b_gate[l]).reshape(B, S, N_BRANCHES, D)
        merged = (gates[:, :, 0] * (y_attn @ w_proj_attn[l])
                  + gates[:, :, 1] * (y_pool @ w_proj_pool[l])
                  + gates[:, :, 2] * (y_mem @ w_proj_mem[l]))
        h = h + merged @ w_out[l]
        h = h + moe(rmsnorm(h, norm_ffn_g[l]), w_router[l], b_router[l], w_up[l], b_up[l],
                    w_down[l], b_down[l])
    return rmsnorm(h, norm_final_g)


_drawn_inputs = setup_inputs


def setup_inputs(seed=0):
    import zlib

    import numpy as np

    out = dict(_drawn_inputs(seed))
    spreads = {}
    factors = {'b_gate': 3.714, 'mem_norm_g': 3.436, 'b_up': 5.587, 'b_down': 6.378}
    for name, (base, spread) in spreads.items():
        noise = np.random.default_rng([zlib.crc32(name.encode()), seed]).standard_normal(out[name].shape)
        drawn = base * np.exp(spread * noise) if base else spread * noise
        out[name] = __import__('jax').numpy.asarray(drawn.astype(out[name].dtype))
    for name, factor in factors.items():
        out[name] = (out[name] * factor).astype(out[name].dtype)
    return out
```

```python
from contextlib import ExitStack

import concourse.bass as bass
from concourse import mybir

F32 = mybir.dt.float32
BF16 = mybir.dt.bfloat16
I32 = mybir.dt.int32
ALU = mybir.AluOpType
ACT = mybir.ActivationFunctionType
AX = mybir.AxisListType

P = 128
S = 256
B = S // P
D = 1024
KC = D // P
M = 256
HEADS = 8
IHEADS = 8
MHEADS = 4
HD = 64
ROPE = 16
HALF = ROPE // 2
TOPK = S // 4
G = 4
NE = 32
TOP = 4
FE = 1024
EPS = 1e-6
ALPHA = 1.702
LIMIT = 7.0
SLOTS = 64
MAX_ROUNDS = S // SLOTS
BIG = 3.0e38
TAKEN = -3.4e38
UNSEL = -1.0e30

C_Q, C_K, C_V, C_IQ, C_IK, C_IW, C_U, C_QM = 0, 512, 1024, 1536, 2048, 2112, 2120, 2376
IN_W = 2632
A_W = C_QM - C_IK

GB = 2 * KC + 2
N_CONST = 9

RING_SLOTS = 6
RS = 4096
FRONT = ["A", "IQ", "Q", "K", "V", "QM", "KV", "G0", "G1", "G2", "G3", "G4", "G5", "PA", "PPM", "O0", "O1"]
UP_W = 2 * FE
UP_CHUNKS = D // P
DOWN_W = 2 * D
DOWN_SLOTS = FE // P // 2
DOWN0 = UP_CHUNKS * UP_W


def psum_jobs():
    jobs = [("gains", "dve")]
    jobs += [(("xT", j), "act") for j in range(4)]
    jobs += [(("A", b), "dve") for b in range(B)]
    jobs += [(("IQ", b), "act") for b in range(B)]
    jobs += [(("memT", j), "dve") for j in range(4)]
    jobs += [(("Q", b), "act") for b in range(B)]
    jobs += [(("iqT", j), "act") for j in range(2)] + [("ikT", "act")]
    jobs += [(("idx", h), "act") for h in range(IHEADS)]
    jobs += [(("K", b), "act") for b in range(B)]
    jobs += [(("V", b), "act") for b in range(B)]
    jobs += [("qmT", "act"), ("kmT", "act"), ("vm", "act")]
    jobs += [(("pool", j), "dve") for j in range(2)] + [("mix", "dve")]
    jobs += [(("qT", j), "act") for j in range(2)] + [(("kT", j), "act") for j in range(2)]
    nh = MHEADS + HEADS
    jobs += [(("sc", 0), "act")]
    for n in range(nh):
        jobs += [(("gate", 2 * n), "act")]
        if n + 1 < nh:
            jobs += [(("sc", n + 1), "act" if n + 1 < MHEADS else "dve")]
        jobs += [(("pT", n), "act"), (("gate", 2 * n + 1), "act"), (("o", n), "dve")]
    for f in range(KC):
        jobs += [(("br", f, i), "dve") for i in range(3)]
    jobs += [(("out", b, h), "dve") for b in range(B) for h in range(2)]
    jobs += [(("x2T", j), "act") for j in range(4)]
    jobs += [("logits", "dve"), ("pos", "dve"), ("gateT", "dve")]
    jobs += [(("bdown", b, h), "dve") for b in range(B) for h in range(2)]
    return jobs


JOBS = psum_jobs()
FILLED = {name: n + 1 for n, (name, _) in enumerate(JOBS)}
BANK = {name: n % 8 for n, (name, _) in enumerate(JOBS)}
OWNER = dict(JOBS)
EMPTIED = {}
for _o in ("act", "dve"):
    for _n, _name in enumerate([j for j, o in JOBS if o == _o]):
        EMPTIED[_name] = _n + 1


LAST_USE = {b: FILLED[b, 1] for b in ("A", "IQ", "Q", "K", "V")}
LAST_USE |= {"QM": FILLED["qmT"], "KV": FILLED["vm"]}
LAST_USE |= {f"G{g}": FILLED["gate", 4 * g + 3] for g in range(6)}
LAST_USE |= {b: FILLED["br", KC - 1, 2] for b in ("PA", "PPM")}
LAST_USE |= {b: FILLED["out", B - 1, 1] for b in ("O0", "O1")}


def hybrid_layer_kernel(nc, x, mem, w_in, w_gate, w_proj_attn, w_proj_pool, w_proj_mem, gains, pool_w_group,
                        w_mem_kv, w_out, norm_ffn_g, w_router, b_router, w_up, b_up, w_down, b_down,
                        norm_final_g, ident_c, iota_c, before_c, causal_c, rope_c, pool_c, expert_c, out):
    ctx = ExitStack()
    with ctx:
        def sb(name, shape, dt=F32):
            return ctx.enter_context(nc.sbuf_tensor(name, shape, dt))

        def sem(name):
            return ctx.enter_context(nc.semaphore(name))

        ring = sb("ring", [P, RING_SLOTS * RS])
        h_s = sb("h_s", [P, B, D])
        xn_area = sb("xn_area", [P, B, D])
        mem_s = sb("mem_s", [P, B, D])
        xT = sb("xT", [P, KC, S])
        memT = sb("memT", [P, KC, M])
        gate_area = sb("gate_area", [P, 3 * KC, S])
        qT = sb("qT", [P, HEADS // 2, S])
        kT = sb("kT", [P, HEADS // 2, S])
        ikT = sb("ikT", [P, S])
        v_s = sb("v_s", [P, B, HEADS * HD])
        misc = sb("misc", [P, 1024])
        idx = sb("idx", [P, P + S])
        bias = sb("bias", [P, P + S])
        lg_s = sb("lg_s", [P, 2, P + S])
        p_s = sb("p_s", [P, 2, B * S])
        pT_s = sb("pT_s", [P, 2, 2 * S])
        yT_area = sb("yT_area", [P, 6, S])
        wg_s = sb("wg_s", [HD, G, HD])
        wr_s = sb("wr_s", [P, KC, NE])
        br_s = sb("br_s", [P, B, NE])
        ident = sb("ident", [P, P])
        iota = sb("iota", [P, P])
        before = sb("before", [P, P])
        ones = sb("ones", [P, P])
        causal = sb("causal", [P, P])
        rope = sb("rope", [P, B, 2 * ROPE])
        rope_t = sb("rope_t", [P, 2, 8, ROPE])
        graw = sb("graw", [64, P])
        gT = sb("gT", [P, 64])
        gate_b = sb("gate_b", [P, 3 * KC])
        expert_f = sb("expert_f", [96, NE])
        expert_b = sb("expert_b", [96, NE], BF16)
        st = sb("st", [P, 32])
        eps_s = sb("eps_s", [P, 1])
        top8 = sb("top8", [P, 2, 8])
        sm = sb("sm", [P, 2, 8])
        rt = sb("rt", [P, B, 36])
        rt_m = sb("rt_m", [P, B, 36])
        rt8 = sb("rt8", [P, B, 8])
        sel = sb("sel", [P, B, NE])
        gex = sb("gex", [P, B, NE])
        gts = sb("gts", [P, B, NE])
        rsm = sb("rsm", [P, 8])
        posm = sb("posm", [P, B, NE + 1])
        gateT_s = sb("gateT_s", [NE, S])
        rounds_i = sb("rounds_i", [1, 1], I32)

        def view(area, start, *dims):
            n = 1
            for d in dims:
                n *= d
            flat = area[:].rearrange("p a b -> p (a b)") if len(area.shape) == 3 else area[:]
            flat = flat[:, start:start + n]
            if len(dims) == 2:
                return flat.rearrange("p (a b) -> p a b", a=dims[0])
            if len(dims) == 3:
                return flat.rearrange("p (a b c) -> p a b c", a=dims[0], b=dims[1])
            return flat

        iq_s = view(gate_area, 0, B, 512)
        q_s = view(gate_area, 1024, B, 512)
        k_s = view(gate_area, 2048, B, 512)
        iqT = view(gate_area, 3072, 4, S)
        pool_a = view(gate_area, 4096, B, G, S)
        gates = gate_area
        qmT = view(xn_area, 0, 2, S)
        kmT = view(xn_area, 512, 2, M)
        vm_s = view(xn_area, 1024, B, MHEADS * HD)
        ymT = view(xn_area, 1536, 2, S)
        xn2 = xn_area
        merged = view(mem_s, 0, KC, S)
        u_s = view(misc, 0, B, G * HD)
        ik_s = view(misc, 512, B, 2 * HD)
        iw_s = view(misc, 768, B, IHEADS)
        pooledT = view(pT_s, 0, G, S)
        relu_s = lg_s
        mix_t = view(lg_s, 0, 3, S)
        b_up_s = view(memT, 0, UP_W)
        b_rest = view(mem_s, 0, UP_W)
        b_part = misc[:, :].bitcast(BF16)
        b_mid = view(p_s, 0, 1024).bitcast(BF16)
        b_down_s = view(qT, 0, D)
        gf_bc = view(kT, 0, D)
        g2_bc = view(v_s, 0, D)
        glu = view(gate_area, 0, FE // 2)
        lin = view(gate_area, 512, FE // 2)
        sig = view(gate_area, 1024, FE // 2)
        act_s = view(gate_area, 1536, FE // 2)
        xeT = view(gate_area, 4096, KC, SLOTS)
        actT = view(gate_area, 4608, KC // 2, P)
        sel_slot = view(gate_area, 5120, B, SLOTS)
        put = view(gate_area, 5248, B, P)
        putT = view(gate_area, 5504, B, P)
        hot = view(gate_area, 5760, SLOTS // 2).bitcast(BF16)
        y_s = view(pT_s, 0, D)
        fin = mem_s

        psum = ctx.enter_context(nc.psum_tensor("psum", [P, 8, 512], F32))

        got_x = sem("got_x")
        got_mem = sem("got_mem")
        got_gains = sem("got_gains")
        got_ident = sem("got_ident")
        got_rope = sem("got_rope")
        got_const = sem("got_const")
        got_late = sem("got_late")
        got_bup = sem("got_bup")
        got_block = [sem(f"got_block{i}") for i in range(RING_SLOTS)]
        got_up = [sem(f"got_up{i}") for i in range(UP_CHUNKS)]
        got_down = [sem(f"got_down{i}") for i in range(DOWN_SLOTS)]
        bank_filled = sem("bank_filled")
        act_emptied = sem("act_emptied")
        dve_emptied = sem("dve_emptied")
        emptied = {"act": act_emptied, "dve": dve_emptied}
        ones_set = sem("ones_set")
        got_eps = sem("got_eps")
        inverse = sem("inverse")
        lin_ready = sem("lin_ready")
        squares = sem("squares")
        scaled = sem("scaled")
        roped = sem("roped")
        relu_ready = sem("relu_ready")
        relu_used = sem("relu_used")
        bias_ready = sem("bias_ready")
        max_ready = sem("max_ready")
        exp_ready = sem("exp_ready")
        p_ready = sem("p_ready")
        merged_ready = sem("merged_ready")
        parts_ready = sem("parts_ready")
        route_max = sem("route_max")
        route_exp = sem("route_exp")
        selected = sem("selected")
        weighted = sem("weighted")
        g_final = sem("g_final")
        route_done = sem("route_done")
        dve_own = sem("dve_own")
        act_own = sem("act_own")
        pool_own = sem("pool_own")
        slots_ready = sem("slots_ready")
        put_ready = sem("put_ready")
        gathered = sem("gathered")
        xe_ready = sem("xe_ready")
        put_turned = sem("put_turned")
        putT_ready = sem("putT_ready")
        up_done = sem("up_done")
        up_used = sem("up_used")
        down_used = sem("down_used")
        glu_ready = sem("glu_ready")
        sig_ready = sem("sig_ready")
        act_ready = sem("act_ready")
        act_turned = sem("act_turned")
        actT_ready = sem("actT_ready")
        y_ready = sem("y_ready")
        put_done = sem("put_done")
        added = sem("added")
        stored = sem("stored")

        block = ctx.enter_context(nc.Block())

        def ring_block(n, cols):
            s = (n % RING_SLOTS) * RS
            return ring[:, s:s + KC * cols].rearrange("p (k n) -> p k n", n=cols)

        def rows(w):
            return w.rearrange("(k p) n -> p k n", p=P)

        def block_arrived(eng, name):
            n = FRONT.index(name)
            eng.wait_ge(got_block[n % RING_SLOTS], 16 * (n // RING_SLOTS + 1))
            return n

        def bank(name):
            return psum[:, BANK[name], :]

        def rounds_of(eng):
            return nc.values_load(rounds_i[0:1, 0:1], engines=[eng.engine], min_val=1, max_val=MAX_ROUNDS)

        @block.sync
        def _(sp):
            sp.dma_start(h_s[:], x.rearrange("a (b p) d -> p (a b) d", p=P)).then_inc(got_x, 16)
            win = rows(w_in[0])
            wgt = rows(w_gate[0])
            src = {"A": [(win[:, :, C_IK:C_QM], 0)], "IQ": [(win[:, :, C_IQ:C_IK], 0)], "Q": [(win[:, :, C_Q:C_K], 0)],
                   "K": [(win[:, :, C_K:C_V], 0)], "V": [(win[:, :, C_V:C_IQ], 0)], "QM": [(win[:, :, C_QM:IN_W], 0)],
                   "KV": [(rows(w_mem_kv[0]), 0)], "PA": [(rows(w_proj_attn[0]), 0)],
                   "PPM": [(rows(w_proj_pool[0]), 0), (rows(w_proj_mem[0]), 2048)],
                   "O0": [(rows(w_out[0])[:, :, 0:512], 0)], "O1": [(rows(w_out[0])[:, :, 512:1024], 0)]}
            for g in range(6):
                src[f"G{g}"] = [(wgt[:, :, 512 * g:512 * (g + 1)], 0)]
            for n, name in enumerate(FRONT):
                if n >= RING_SLOTS:
                    sp.wait_ge(bank_filled, LAST_USE[FRONT[n - RING_SLOTS]])
                for ap, at in src[name]:
                    k, cols = ap.shape[1], ap.shape[2]
                    s = (n % RING_SLOTS) * RS + at
                    dst = ring[:, s:s + k * cols].rearrange("p (k n) -> p k n", n=cols)
                    sp.dma_start(dst, ap).then_inc(got_block[n % RING_SLOTS], 16)

            def load_up(e, k):
                sp.dma_start(ring[:, k * UP_W:(k + 1) * UP_W],
                             w_up[0][bass.ds(e, 1), k * P:(k + 1) * P, :].rearrange("a p n -> (a p) n"))\
                  .then_inc(got_up[k], 16)

            def load_down(e, j):
                s = DOWN0 + j * DOWN_W
                sp.dma_start(ring[:, s:s + DOWN_W].rearrange("p (t n) -> p t n", t=2),
                             w_down[0][bass.ds(e, 1), 2 * j * P:2 * (j + 1) * P, :]
                             .rearrange("a (t p) n -> p (a t) n", p=P)).then_inc(got_down[j], 16)

            last = {n % RING_SLOTS: LAST_USE[name] for n, name in enumerate(FRONT)}
            for k in range(UP_CHUNKS):
                sp.wait_ge(bank_filled, last[k // 2])
                load_up(0, k)
            for j in range(DOWN_SLOTS):
                sp.wait_ge(bank_filled, last[4 + j // 2])
                load_down(0, j)

            def expert_weights(e, i):
                for k in range(UP_CHUNKS):
                    sp.wait_ge(up_used, (i - 1) * UP_CHUNKS + k + 1)
                    load_up(e, k)
                for j in range(DOWN_SLOTS):
                    sp.wait_ge(down_used, (i - 1) * DOWN_SLOTS + j + 1)
                    load_down(e, j)

            with sp.Fori(1, NE) as e:
                expert_weights(e, e)
            sp.wait_ge(route_done, 1)
            rounds = rounds_of(sp)
            with sp.If(rounds > 1):
                with sp.Fori(1, rounds) as r:
                    with sp.Fori(0, NE) as e:
                        expert_weights(e, r * NE + e)
            sp.wait_ge(stored, 16 * B)

        @block.gpsimd
        def _(pool):
            own = [0]

            def link(ins):
                own[0] += 1
                ins.then_inc(pool_own, 1)
                pool.wait_ge(pool_own, own[0])

            nc.gpsimd.memset(ones[:], 1.0).then_inc(ones_set, 1)
            pool.wait_ge(got_rope, 16)

            def rotate(t, b, heads, last):
                v = t[:, b, :].rearrange("p (h d) -> p h d", h=heads)
                cc = rope[:, b:b + 1, 0:ROPE].to_broadcast([P, heads, ROPE])
                s1 = rope[:, b:b + 1, ROPE:ROPE + HALF].to_broadcast([P, heads, HALF])
                s2 = rope[:, b:b + 1, ROPE + HALF:2 * ROPE].to_broadcast([P, heads, HALF])
                c, s = rope_t[:, 0, 0:heads, :], rope_t[:, 1, 0:heads, :]
                nc.gpsimd.tensor_tensor(c, v[:, :, 0:ROPE], cc, ALU.mult)
                nc.gpsimd.tensor_tensor(s[:, :, 0:HALF], v[:, :, HALF:ROPE], s1, ALU.mult)
                link(nc.gpsimd.tensor_tensor(s[:, :, HALF:ROPE], v[:, :, 0:HALF], s2, ALU.mult))
                own[0] += 1
                nc.gpsimd.tensor_tensor(v[:, :, 0:ROPE], c, s, ALU.add).then_inc(roped, 1)
                last[0] += 1
                pool.wait_ge(roped, last[0])
                own[0] -= 1

            n = [0]
            for b in range(B):
                pool.wait_ge(dve_emptied, EMPTIED[("A", b)])
                rotate(ik_s, b, 2, n)
            for name, t in (("IQ", iq_s), ("Q", q_s), ("K", k_s)):
                for b in range(B):
                    pool.wait_ge(act_emptied, EMPTIED[(name, b)])
                    rotate(t, b, HEADS, n)
            pool.wait_ge(got_bup, 48)
            pool.wait_ge(bank_filled, FILLED["x2T", 3])
            link(nc.gpsimd.tensor_copy(b_part[0:96, :], b_up_s[0:96, :]))
            link(nc.gpsimd.tensor_tensor(b_rest[0:96, :], b_up_s[0:96, :], b_part[0:96, :], ALU.subtract))
            link(nc.gpsimd.tensor_copy(b_mid[0:96, :], b_rest[0:96, :]))
            link(nc.gpsimd.tensor_tensor(b_rest[0:96, :], b_rest[0:96, :], b_mid[0:96, :], ALU.subtract))
            nc.gpsimd.tensor_copy(b_part[32:64, :], b_mid[32:64, :])
            nc.gpsimd.tensor_copy(b_part[64:96, :], b_rest[64:96, :]).then_inc(parts_ready, 1)

        @block.scalar
        def _(act):
            own = [0]

            def link(ins):
                own[0] += 1
                ins.then_inc(act_own, 1)
                act.wait_ge(act_own, own[0])

            act.dma_start(ident[:], ident_c).then_inc(got_ident, 16)
            act.dma_start(graw[0:gains.shape[0], :], gains).then_inc(got_gains, 16)
            act.dma_start(mem_s[:], mem.rearrange("a (b p) d -> p (a b) d", p=P)).then_inc(got_mem, 16)
            act.dma_start(rope[:], rope_c.rearrange("(b p) c -> p b c", p=P)).then_inc(got_rope, 16)
            consts = [(iota[:], iota_c), (before[:], before_c), (causal[:], causal_c), (expert_f[:], expert_c),
                      (pool_a, pool_c.rearrange("(b p) g t -> p b g t", p=P)),
                      (wg_s[:], pool_w_group[0].rearrange("g c d -> c g d")),
                      (wr_s[:], rows(w_router[0])),
                      (br_s[:, 0, :], b_router.to_broadcast([P, NE])), (br_s[:, 1, :], b_router.to_broadcast([P, NE]))]
            for dst, s in consts:
                act.dma_start(dst, s).then_inc(got_const, 16)

            def rms_stats(src, at, sem_in, value):
                if sem_in is not None:
                    act.wait_ge(sem_in, value)
                for b in range(B):
                    ins = nc.scalar.activation(gates_scratch(b), src[:, b, :], ACT.Square,
                                               accum_out=st[:, at + b:at + b + 1])
                return ins

            def gates_scratch(b):
                return view(gate_area, 2048 + 1024 * b, D)

            act.wait_ge(got_eps, 1)
            link(rms_stats(h_s, 0, got_x, 16))
            nc.scalar.activation(st[:, 4:6], st[:, 0:2], ACT.Sqrt, bias=eps_s[:, 0:1], scale=1.0 / D)\
              .then_inc(squares, 1)
            link(rms_stats(mem_s, 8, got_mem, 16))
            nc.scalar.activation(st[:, 12:14], st[:, 8:10], ACT.Sqrt, bias=eps_s[:, 0:1], scale=1.0 / D)\
              .then_inc(squares, 1)

            def empty(name):
                act.wait_ge(bank_filled, FILLED[name])
                return bank(name)

            act.wait_ge(dve_emptied, EMPTIED["gains"])
            for j in range(4):
                t = empty(("xT", j))
                for c in range(2):
                    k = 2 * j + c
                    ins = nc.scalar.activation(xT[:, k, :], t[:, c * S:(c + 1) * S], ACT.Copy, scale=gT[:, k:k + 1])
                ins.then_inc(act_emptied, 1)

            def copy(name, dst, part=None):
                t = empty(name)
                src_ap = t if part is None else part(t)
                nc.scalar.activation(dst, src_ap, ACT.Copy).then_inc(act_emptied, 1)

            def pair(t):
                return t.rearrange("p (c s) -> p c s", c=2)

            for b in range(B):
                copy(("IQ", b), iq_s[:, b, :])
            for b in range(B):
                copy(("Q", b), q_s[:, b, :])
            for j in range(2):
                copy(("iqT", j), iqT[:, 2 * j:2 * j + 2, :], pair)
            copy("ikT", ikT[:, :], lambda t: t[:, 0:S])
            for h in range(IHEADS):
                if h >= 2:
                    act.wait_ge(relu_used, h - 1)
                t = empty(("idx", h))
                nc.scalar.activation(relu_s[:, h % 2, :], t[:, 0:P + S], ACT.Relu, scale=HD ** -0.5)\
                  .then_inc(act_emptied, 1)
            for b in range(B):
                copy(("K", b), k_s[:, b, :])
            for b in range(B):
                copy(("V", b), v_s[:, b, :])
            copy("qmT", qmT, pair)
            copy("kmT", kmT, pair)
            copy("vm", vm_s, pair)
            for c in range(3):
                act.dma_start(b_up_s[32 * c:32 * c + 32, :], b_up[0]).then_inc(got_bup, 16)
            for j in range(2):
                copy(("qT", j), qT[:, 2 * j:2 * j + 2, :], pair)
            for j in range(2):
                copy(("kT", j), kT[:, 2 * j:2 * j + 2, :], pair)

            link(nc.scalar.mul(gate_b[:], gT[:, GB:GB + 3 * KC], 0.5))

            def gate(m):
                t = empty(("gate", m))
                nc.scalar.activation(gates[:, m, :], t[:, 0:S], ACT.Tanh, bias=gate_b[:, m:m + 1], scale=0.5)\
                  .then_inc(act_emptied, 1)

            def exps(n):
                act.wait_ge(max_ready, n + 1)
                if n >= 2:
                    act.wait_ge(bank_filled, FILLED["pT", n - 2])
                for b in range(B):
                    if n < MHEADS:
                        src_ap, w = bank(("sc", n))[:, b * M:(b + 1) * M], M
                    else:
                        src_ap, w = lg_s[:, n % 2, b * P:P + b * S], P * (b + 1)
                    ins = nc.scalar.activation(p_s[:, n % 2, b * S:b * S + w], src_ap, ACT.Exp,
                                               bias=sm[:, n % 2, b:b + 1], scale=HD ** -0.5,
                                               accum_out=sm[:, n % 2, 2 + b:3 + b])
                    if n < MHEADS and b == B - 1:
                        ins.then_inc(act_emptied, 1)
                        act.wait_ge(act_emptied, EMPTIED["sc", n])
                        nc.scalar.copy(sm[:, n % 2, 6:7], sm[:, n % 2, 2:3]).then_inc(exp_ready, 1)
                    elif b == B - 1:
                        ins.then_inc(exp_ready, 1)

            def copy_pT(n):
                t = empty(("pT", n))
                if n >= 2:
                    act.wait_ge(bank_filled, FILLED["o", n - 2])
                if n < MHEADS:
                    nc.scalar.activation(pT_s[:, n % 2, :], t, ACT.Copy).then_inc(act_emptied, 1)
                else:
                    nc.scalar.activation(pT_s[:, n % 2, 0:S + P], t[:, 0:S + P], ACT.Copy).then_inc(act_emptied, 1)

            nh = MHEADS + HEADS
            act.wait_ge(dve_emptied, EMPTIED["mix"])
            exps(0)
            for n in range(nh):
                gate(2 * n)
                if n + 1 < nh:
                    exps(n + 1)
                copy_pT(n)
                gate(2 * n + 1)
            act.wait_ge(bank_filled, FILLED["o", nh - 1])
            act.dma_start(b_down_s[0:NE, :], b_down[0]).then_inc(got_late, 16)
            act.dma_start(gf_bc, norm_final_g.to_broadcast([P, D])).then_inc(got_late, 16)
            act.dma_start(g2_bc, norm_ffn_g.to_broadcast([P, D])).then_inc(got_late, 16)

            link(rms_stats(h_s, 16, dve_emptied, EMPTIED["out", B - 1, 1]))
            nc.scalar.activation(st[:, 20:22], st[:, 16:18], ACT.Sqrt, bias=eps_s[:, 0:1], scale=1.0 / D)\
              .then_inc(squares, 1)
            for j in range(4):
                copy(("x2T", j), xT[:, 2 * j:2 * j + 2, :], pair)
            act.wait_ge(route_max, 1)
            for b in range(B):
                ins = nc.scalar.activation(gex[:, b, :], rt[:, b, TOP:], ACT.Exp, bias=rsm[:, b:b + 1])
            ins.then_inc(route_exp, 1)

            def take_gathered(i):
                act.wait_ge(gathered, i + 1)
                nc.scalar.activation(xeT, psum[:, 2, :].rearrange("p (k c) -> p k c", k=KC), ACT.Copy)\
                  .then_inc(xe_ready, 1)

            take_gathered(0)
            act.wait_ge(route_done, 1)
            rounds = rounds_of(act)
            with act.Fori(0, rounds) as r:
                with act.Fori(0, NE) as e:
                    i = r * NE + e
                    act.wait_ge(glu_ready, i + 1)
                    nc.scalar.activation(sig, glu, ACT.Sigmoid, scale=ALPHA).then_inc(sig_ready, 1)
                    take_gathered(i + 1)
                    act.wait_ge(put_turned, i + 1)
                    nc.scalar.activation(putT, psum[:, 3, 0:B * P].rearrange("p (b c) -> p b c", b=B), ACT.Copy)\
                      .then_inc(putT_ready, 1)
                    act.wait_ge(act_turned, i + 1)
                    nc.scalar.activation(actT, psum[:, 2, :].rearrange("p (q c) -> p q c", c=P), ACT.Copy)\
                      .then_inc(actT_ready, 1)
                    act.wait_ge(down_used, DOWN_SLOTS * (i + 1))
                    nc.scalar.activation(y_s, psum[:, 5:7, :].rearrange("p a n -> p (a n)"), ACT.Copy)\
                      .then_inc(y_ready, 1)

            act.wait_ge(added, 2 + 4 * (NE * rounds + 1))
            link(rms_stats(h_s, 24, None, None))
            nc.scalar.activation(st[:, 28:30], st[:, 24:26], ACT.Sqrt, bias=eps_s[:, 0:1], scale=1.0 / D)\
              .then_inc(squares, 1)
            for b in range(B):
                act.wait_ge(g_final, b + 1)
                act.dma_start(out[0, b * P:(b + 1) * P, :], fin[:, b, :]).then_inc(stored, 16)

        @block.vector
        def _(dve):
            own = [0]

            def link(ins):
                own[0] += 1
                ins.then_inc(dve_own, 1)
                dve.wait_ge(dve_own, own[0])

            nc.vector.memset(eps_s[:], EPS).then_inc(got_eps, 1)

            def scale_rows(dst, src, at, count, gain=None):
                dve.wait_ge(squares, count)
                nc.vector.reciprocal(st[:, at + 6:at + 8], st[:, at + 4:at + 6]).then_inc(inverse, 1)
                dve.wait_ge(inverse, count)
                for b in range(B):
                    if gain is None:
                        ins = nc.vector.tensor_scalar(dst[:, b, :], src[:, b, :], st[:, at + 6 + b:at + 7 + b],
                                                      None, ALU.mult)
                    else:
                        ins = nc.vector.scalar_tensor_tensor(out=dst[:, b, :], in0=src[:, b, :],
                                                             scalar=st[:, at + 6 + b:at + 7 + b], in1=gain,
                                                             op0=ALU.mult, op1=ALU.mult)
                    if count < 4:
                        ins.then_inc(scaled, 1)
                    else:
                        ins.then_inc(g_final, 1)

            def empty(name):
                dve.wait_ge(bank_filled, FILLED[name])
                return bank(name)

            t = empty("gains")
            nc.vector.tensor_copy(gT[:, 0:gains.shape[0]], t[:, 0:gains.shape[0]]).then_inc(dve_emptied, 1)
            scale_rows(xn_area, h_s, 0, 1)
            scale_rows(mem_s, mem_s, 8, 2)
            for b in range(B):
                t = empty(("A", b))
                o = C_U - C_IK
                nc.vector.tensor_copy(u_s[:, b, :], t[:, o:o + G * HD])
                nc.vector.tensor_copy(ik_s[:, b, 0:HD], t[:, 0:HD])
                nc.vector.tensor_copy(ik_s[:, b, HD:2 * HD], t[:, 0:HD])
                o = C_IW - C_IK
                nc.vector.tensor_scalar(iw_s[:, b, :], t[:, o:o + IHEADS], IHEADS ** -0.5, None, ALU.mult)\
                  .then_inc(dve_emptied, 1)
            for j in range(4):
                t = empty(("memT", j))
                for c in range(2):
                    k = 2 * j + c
                    ins = nc.vector.tensor_scalar(memT[:, k, :], t[:, c * M:(c + 1) * M], gT[:, KC + k:KC + k + 1],
                                                  None, ALU.mult)
                ins.then_inc(dve_emptied, 1)
            for h in range(IHEADS):
                dve.wait_ge(act_emptied, EMPTIED["idx", h])
                for b in range(B):
                    cols = slice(b * P, P + b * S)
                    if h == 0:
                        ins = nc.vector.tensor_scalar(idx[:, cols], relu_s[:, h % 2, cols], iw_s[:, b, h:h + 1], None,
                                                      ALU.mult)
                    else:
                        ins = nc.vector.scalar_tensor_tensor(out=idx[:, cols], in0=relu_s[:, h % 2, cols],
                                                             scalar=iw_s[:, b, h:h + 1], in1=idx[:, cols],
                                                             op0=ALU.mult, op1=ALU.add)
                ins.then_inc(relu_used, 1)
                dve.wait_ge(relu_used, h + 1)
            dve.wait_ge(got_const, 16 * N_CONST)
            nc.vector.tensor_tensor(idx[:, 0:P], idx[:, 0:P], causal[:], ALU.add)
            link(nc.vector.tensor_tensor(idx[:, 2 * P:3 * P], idx[:, 2 * P:3 * P], causal[:], ALU.add))

            def take_top(b, first, n):
                cols = slice(b * P, P + b * S)
                for _ in range(first, first + n):
                    link(nc.vector.max(out=top8[:, b, :], in_=idx[:, cols]))
                    link(nc.vector.match_replace(out=idx[:, cols], in_to_replace=top8[:, b, :], in_values=idx[:, cols],
                                                 imm_value=TAKEN))
                if first + n == TOPK // 8:
                    link(nc.vector.tensor_scalar(bias[:, cols], idx[:, cols], (TAKEN - BIG) / 2, UNSEL, ALU.is_gt,
                                                 ALU.mult))
                    d = slice(2 * b * P, (2 * b + 1) * P)
                    link(nc.vector.tensor_tensor(bias[:, d], bias[:, d], causal[:], ALU.add))

            for j in range(2):
                t = empty(("pool", j))
                nc.vector.tensor_copy(pooledT[0:HD, 2 * j:2 * j + 2, :],
                                      t[0:HD, :].rearrange("p (g s) -> p g s", g=2)).then_inc(dve_emptied, 1)
            t = empty("mix")
            for c in range(2):
                ins = nc.vector.tensor_scalar(yT_area[:, 4 + c, :], t[:, c * S:(c + 1) * S],
                                              gT[:, 2 * KC + c:2 * KC + c + 1], None, ALU.mult)
            ins.then_inc(dve_emptied, 1)

            def maxima(n):
                if n < MHEADS:
                    t = empty(("sc", n))
                    if n >= 2:
                        dve.wait_ge(p_ready, n - 1)
                    link(nc.vector.reduce_max(sm[:, n % 2, 4:6], t.rearrange("p (b s) -> p b s", b=B), AX.X))
                else:
                    t = empty(("sc", n))
                    dve.wait_ge(exp_ready, n - 1)
                    for b in range(B):
                        cols = slice(b * P, P + b * S)
                        ins = nc.vector.tensor_tensor(lg_s[:, n % 2, cols], t[:, cols], bias[:, cols], ALU.add)
                    ins.then_inc(dve_emptied, 1)
                    dve.wait_ge(dve_emptied, EMPTIED["sc", n])
                    for b in range(B):
                        cols = slice(b * P, P + b * S)
                        ins = nc.vector.reduce_max(sm[:, n % 2, 4 + b:5 + b], lg_s[:, n % 2, cols], AX.X)
                    link(ins)
                nc.vector.tensor_scalar(sm[:, n % 2, 0:2], sm[:, n % 2, 4:6], -HD ** -0.5, None, ALU.mult)\
                  .then_inc(max_ready, 1)

            def normalise(n):
                dve.wait_ge(exp_ready, n + 1)
                link(nc.vector.reciprocal(sm[:, n % 2, 4:6], sm[:, n % 2, 2:4]))
                for b in range(B):
                    w = M if n < MHEADS else P * (b + 1)
                    ins = nc.vector.tensor_scalar(p_s[:, n % 2, b * S:b * S + w], p_s[:, n % 2, b * S:b * S + w],
                                                  sm[:, n % 2, 4 + b:5 + b], None, ALU.mult)
                ins.then_inc(p_ready, 1)

            def take_o(n):
                t = empty(("o", n))
                lo = HD * (n % 2)
                dst = ymT[lo:lo + HD, n // 2, :] if n < MHEADS else yT_area[lo:lo + HD, (n - MHEADS) // 2, :]
                nc.vector.tensor_copy(dst, t[lo:lo + HD, 0:S]).then_inc(dve_emptied, 1)

            nh = MHEADS + HEADS
            maxima(0)
            normalise(0)
            for n in range(nh):
                if n + 1 < nh:
                    maxima(n + 1)
                    normalise(n + 1)
                if n == 0:
                    take_top(0, 0, TOPK // 8)
                if n in (1, 2):
                    take_top(1, (n - 1) * (TOPK // 16), TOPK // 16)
                take_o(n)

            dve.wait_ge(act_emptied, EMPTIED["gate", 3 * KC - 1])
            for f in range(KC):
                for i in range(3):
                    t = empty(("br", f, i))
                    ins = nc.vector.scalar_tensor_tensor(out=mix_t[:, i, :], in0=gates[:, KC * i + f, :], scalar=1.0,
                                                         in1=t[:, 0:S], op0=ALU.add, op1=ALU.mult)
                    ins.then_inc(dve_emptied, 1)
                dve.wait_ge(dve_emptied, EMPTIED["br", f, 2])
                link(nc.vector.tensor_tensor(mix_t[:, 0, :], mix_t[:, 0, :], mix_t[:, 1, :], ALU.add))
                nc.vector.tensor_tensor(merged[:, f, :], mix_t[:, 0, :], mix_t[:, 2, :], ALU.add)\
                  .then_inc(merged_ready, 1)
                dve.wait_ge(merged_ready, f + 1)
            for b in range(B):
                for hf in range(2):
                    t = empty(("out", b, hf))
                    cols = slice(hf * 512, hf * 512 + 512)
                    nc.vector.scalar_tensor_tensor(out=h_s[:, b, cols], in0=t, scalar=0.5, in1=h_s[:, b, cols],
                                                   op0=ALU.mult, op1=ALU.add).then_inc(dve_emptied, 1)

            dve.wait_ge(got_late, 48)
            scale_rows(xn2, h_s, 16, 3, g2_bc)

            nc.vector.memset(rt[:, :, 0:TOP], BIG)
            nc.vector.tensor_copy(expert_b[:], expert_f[:])
            t = empty("logits")
            nc.vector.tensor_tensor(rt[:, :, TOP:], t[:, 0:B * NE].rearrange("p (b e) -> p b e", b=B), br_s[:],
                                    ALU.add).then_inc(dve_emptied, 1)
            dve.wait_ge(dve_emptied, EMPTIED["logits"])
            for b in range(B):
                ins = nc.vector.max(out=rt8[:, b, :], in_=rt[:, b, :])
            link(ins)
            nc.vector.tensor_scalar(rsm[:, 0:B], rt8[:, :, TOP:TOP + 1].rearrange("p b o -> p (b o)"), -1.0, None, ALU.mult)\
              .then_inc(route_max, 1)
            for b in range(B):
                ins = nc.vector.match_replace(out=rt_m[:, b, :], in_to_replace=rt8[:, b, :], in_values=rt[:, b, :],
                                              imm_value=TAKEN)
            link(ins)
            nc.vector.tensor_scalar(sel[:], rt_m[:, :, TOP:], (TAKEN - BIG) / 2, None, ALU.is_lt).then_inc(selected, 1)
            dve.wait_ge(selected, 1)
            dve.wait_ge(route_exp, 1)
            for b in range(B):
                ins = nc.vector.scalar_tensor_tensor(out=gex[:, b, :], in0=gex[:, b, :], scalar=1.0, in1=sel[:, b, :],
                                                     op0=ALU.mult, op1=ALU.mult, accum_out=rsm[:, 2 + b:3 + b])
            link(ins)
            link(nc.vector.reciprocal(rsm[:, 4:6], rsm[:, 2:4]))
            for b in range(B):
                ins = nc.vector.tensor_scalar(gts[:, b, :], gex[:, b, :], rsm[:, 4 + b:5 + b], None, ALU.mult)
            ins.then_inc(weighted, 1)

            t = empty("pos")
            pos = t[:, 0:B * NE].rearrange("p (b e) -> p b e", b=B)
            nc.vector.scalar_tensor_tensor(out=posm[:, :, 0:NE], in0=pos, scalar=1.0, in1=sel[:], op0=ALU.add,
                                           op1=ALU.mult)
            nc.vector.tensor_scalar(rt8[:, 0, 0:MAX_ROUNDS], iota[:, 0:MAX_ROUNDS], float(SLOTS), None, ALU.mult)
            nc.vector.reduce_max(rsm[:, 6:7], t[:, B * NE:(B + 1) * NE], AX.X).then_inc(dve_emptied, 1)
            dve.wait_ge(dve_emptied, EMPTIED["pos"])
            link(nc.vector.tensor_scalar(posm[:, :, 0:NE], posm[:, :, 0:NE], -1.0, None, ALU.add))
            nc.vector.tensor_scalar(posm[:, :, NE:NE + 1], posm[:, :, 0:1], -float(SLOTS), None, ALU.add)
            link(nc.vector.tensor_scalar(rt8[:, 1, 0:MAX_ROUNDS], rt8[:, 0, 0:MAX_ROUNDS], rsm[:, 6:7], None,
                                         ALU.is_lt))
            link(nc.vector.reduce_sum(rsm[:, 7:8], rt8[:, 1, 0:MAX_ROUNDS], AX.X))
            nc.vector.tensor_copy(rounds_i[:, :], rsm[0:1, 7:8]).then_inc(route_done, 1)

            def gather_columns(e, n):
                if n is not None:
                    dve.wait_ge(gathered, n)
                for b in range(B):
                    ins = nc.vector.tensor_scalar(sel_slot[:, b, :], iota[:, 0:SLOTS], posm[:, b, bass.ds(e, 1)], None,
                                                  ALU.is_equal)
                ins.then_inc(slots_ready, 1)

            gather_columns(0, None)
            t = empty("gateT")
            nc.vector.tensor_copy(gateT_s[:], t[0:NE, 0:S]).then_inc(dve_emptied, 1)
            for b in range(B):
                for hf in range(2):
                    t = empty(("bdown", b, hf))
                    cols = slice(hf * 512, hf * 512 + 512)
                    nc.vector.tensor_tensor(h_s[:, b, cols], t, h_s[:, b, cols], ALU.add).then_inc(dve_emptied, 1)
            nc.vector.engine_nop().then_inc(added, 2)

            def take_back(n):
                for j in range(4):
                    b, hf = j // 2, j % 2
                    cols = slice(hf * 512, hf * 512 + 512)
                    dve.wait_ge(put_done, 4 * n + j + 1)
                    nc.vector.tensor_tensor(h_s[:, b, cols], psum[:, 4 + 3 * (j % 2), :], h_s[:, b, cols],
                                            ALU.add).then_inc(added, 1)

            nc.vector.memset(putT, 0.0).then_inc(putT_ready, 1)
            nc.vector.memset(y_s, 0.0).then_inc(y_ready, 1)
            dve.wait_ge(route_done, 1)
            rounds = rounds_of(dve)
            link_base = own[0]
            with dve.Fori(0, rounds) as r:
                with dve.Fori(0, NE) as e:
                    i = r * NE + e
                    gather_columns(e + 1, i + 1)
                    take_back(i)
                    for b in range(B):
                        nc.vector.tensor_scalar(put[:, b, :], iota[:], posm[:, b, bass.ds(e, 1)],
                                                gts[:, b, bass.ds(e, 1)], ALU.is_equal, ALU.mult)
                    nc.vector.tensor_copy(hot[0:96, :], expert_b[:, bass.ds(e, 1)].to_broadcast([96, SLOTS]))\
                      .then_inc(put_ready, 1)
                    dve.wait_ge(up_done, i + 1)
                    nc.vector.tensor_scalar(glu, psum[:, 0, :], LIMIT, None, ALU.min).then_inc(glu_ready, 1)
                    nc.vector.tensor_scalar(lin, psum[:, 1, :], LIMIT, -LIMIT, ALU.min, ALU.max).then_inc(lin_ready, 1)
                    dve.wait_ge(lin_ready, 2 * i + 1)
                    nc.vector.scalar_tensor_tensor(out=lin, in0=lin, scalar=1.0, in1=glu, op0=ALU.add, op1=ALU.mult)\
                      .then_inc(lin_ready, 1)
                    dve.wait_ge(sig_ready, i + 1)
                    dve.wait_ge(lin_ready, 2 * i + 2)
                    nc.vector.tensor_tensor(act_s, lin, sig, ALU.mult).then_inc(act_ready, 1)
                nc.vector.tensor_scalar(posm[:], posm[:], -float(SLOTS), None, ALU.add).then_inc(dve_own, 1)
                dve.wait_ge(dve_own, link_base + r + 1)
            take_back(NE * rounds)
            scale_rows(fin, h_s, 24, 4, gf_bc)

        @block.tensor
        def _(pe):
            def fill(name):
                n = FILLED[name] - 1
                if n >= 8:
                    prev, who = JOBS[n - 8]
                    pe.wait_ge(emptied[who], EMPTIED[prev])
                return bank(name)

            def done(ins):
                ins.then_inc(bank_filled, 1)

            pe.wait_ge(got_ident, 16)
            pe.wait_ge(got_gains, 16)
            t = fill("gains")
            n = gains.shape[0]
            done(nc.tensor.transpose(t[:, 0:n], graw[0:n, :], ident[0:n, 0:n]))

            def transposes(kind, src, count_sem, count):
                for j in range(4):
                    t = fill((kind, j))
                    for c in range(2):
                        k = 2 * j + c
                        for b in range(B):
                            if j == 0 and c == 0 and count_sem is not None:
                                pe.wait_ge(count_sem, count + b)
                            ins = nc.tensor.transpose(t[:, c * S + b * P:c * S + (b + 1) * P],
                                                      src[:, b, k * P:(k + 1) * P], ident[:])
                    done(ins)

            transposes("xT", xn_area, scaled, 1)

            def project(name, cols, lhsT, jobs):
                n = block_arrived(pe, name)
                w = ring_block(n, cols)
                for b in range(B):
                    t = fill((jobs, b))
                    for k in range(KC):
                        ins = nc.tensor.matmul(t[:, 0:cols], lhsT[:, k, b * P:(b + 1) * P], w[:, k, :], start=(k == 0),
                                               stop=(k == KC - 1))
                    done(ins)

            pe.wait_ge(act_emptied, EMPTIED["xT", 3])
            project("A", A_W, xT, "A")
            project("IQ", 512, xT, "IQ")
            transposes("memT", mem_s, scaled, 3)
            project("Q", 512, xT, "Q")
            pe.wait_ge(roped, 4)
            for j in range(2):
                t = fill(("iqT", j))
                for c in range(2):
                    for b in range(B):
                        ins = nc.tensor.transpose(t[:, c * S + b * P:c * S + (b + 1) * P],
                                                  iq_s[:, b, (2 * j + c) * P:(2 * j + c + 1) * P], ident[:])
                done(ins)
            t = fill("ikT")
            for b in range(B):
                ins = nc.tensor.transpose(t[:, b * P:(b + 1) * P], ik_s[:, b, :], ident[:])
            done(ins)
            pe.wait_ge(act_emptied, EMPTIED["ikT"])

            def causal_scores(t, qt, kt, lo, c):
                nc.tensor.matmul(t[:, 0:P], qt[lo:lo + HD, c, 0:P], kt[lo:lo + HD, 0:P], start=True, stop=True)
                return nc.tensor.matmul(t[:, P:P + S], qt[lo:lo + HD, c, P:S], kt[lo:lo + HD, 0:S], start=True,
                                        stop=True)

            for h in range(IHEADS):
                t = fill(("idx", h))
                done(causal_scores(t, iqT, ikT, HD * (h % 2), h // 2))
            project("K", 512, xT, "K")
            project("V", 512, xT, "V")

            def project_T(t, w, col0, rhs, chunks):
                for c in range(chunks):
                    for k in range(KC):
                        ins = nc.tensor.matmul(t[:, c * S:(c + 1) * S], w[:, k, col0 + c * P:col0 + (c + 1) * P],
                                               rhs[:, k, :], start=(k == 0), stop=(k == KC - 1))
                return ins

            n = block_arrived(pe, "QM")
            done(project_T(fill("qmT"), ring_block(n, 256), 0, xT, 2))
            n = block_arrived(pe, "KV")
            pe.wait_ge(dve_emptied, EMPTIED["memT", 3])
            w = ring_block(n, 512)
            done(project_T(fill("kmT"), w, 0, memT, 2))
            t = fill("vm")
            for b in range(B):
                for k in range(KC):
                    ins = nc.tensor.matmul(t[:, b * 256:(b + 1) * 256], memT[:, k, b * P:(b + 1) * P], w[:, k, 256:512],
                                           start=(k == 0), stop=(k == KC - 1))
            done(ins)
            pe.wait_ge(got_const, 16 * N_CONST)
            for j in range(2):
                t = fill(("pool", j))
                for c in range(2):
                    g = 2 * j + c
                    for b in range(B):
                        ins = nc.tensor.matmul(t[0:HD, c * S:(c + 1) * S], u_s[:, b, g * HD:(g + 1) * HD],
                                               pool_a[:, b, g, :], start=(b == 0), stop=(b == B - 1))
                done(ins)
            t = fill("mix")
            pe.wait_ge(dve_emptied, EMPTIED["pool", 1])
            for g in range(G):
                lo = HD * (g % 2)
                ins = nc.tensor.matmul(t[lo:lo + HD, (g // 2) * S:(g // 2 + 1) * S], wg_s[:, g, :],
                                       pooledT[0:HD, g, :], start=True, stop=True)
            done(ins)
            for name, src_t, r in (("qT", q_s, 6), ("kT", k_s, 8)):
                pe.wait_ge(roped, r)
                for j in range(2):
                    t = fill((name, j))
                    for c in range(2):
                        for b in range(B):
                            ins = nc.tensor.transpose(t[:, c * S + b * P:c * S + (b + 1) * P],
                                                      src_t[:, b, (2 * j + c) * P:(2 * j + c + 1) * P], ident[:])
                    done(ins)

            def scores(n):
                t = fill(("sc", n))
                if n < MHEADS:
                    lo = HD * (n % 2)
                    for b in range(B):
                        ins = nc.tensor.matmul(t[:, b * M:(b + 1) * M], qmT[lo:lo + HD, n // 2, b * P:(b + 1) * P],
                                               kmT[lo:lo + HD, n // 2, :], start=True, stop=True)
                    done(ins)
                else:
                    m = n - MHEADS
                    done(causal_scores(t, qT, kT[:, m // 2, :], HD * (m % 2), m // 2))

            def turn_p(n):
                t = fill(("pT", n))
                pe.wait_ge(p_ready, n + 1)
                for s in range(2):
                    for b in range(B):
                        if n >= MHEADS and s > b:
                            continue
                        at = s * S + b * P if n < MHEADS or s == 0 else S
                        ins = nc.tensor.transpose(t[:, at:at + P], p_s[:, n % 2, b * S + s * P:b * S + (s + 1) * P],
                                                  ident[:])
                done(ins)

            def attend(n):
                t = fill(("o", n))
                pe.wait_ge(act_emptied, EMPTIED["pT", n])
                lo = HD * (n % 2)
                v = vm_s[:, :, n * HD:(n + 1) * HD] if n < MHEADS else v_s[:, :, (n - MHEADS) * HD:(n - MHEADS + 1) * HD]
                nc.tensor.matmul(t[lo:lo + HD, 0:S], v[:, 0, :], pT_s[:, n % 2, 0:S], start=True, stop=False)
                if n < MHEADS:
                    ins = nc.tensor.matmul(t[lo:lo + HD, 0:S], v[:, 1, :], pT_s[:, n % 2, S:2 * S], start=False,
                                           stop=True)
                else:
                    ins = nc.tensor.matmul(t[lo:lo + HD, P:S], v[:, 1, :], pT_s[:, n % 2, S:S + P], start=False,
                                           stop=True)
                done(ins)

            def gate(m):
                if m % 4 == 0:
                    block_arrived(pe, f"G{m // 4}")
                w = ring_block(FRONT.index(f"G{m // 4}"), 512)
                ins = project_T(fill(("gate", m)), w, (m % 4) * P, xT, 1)
                done(ins)
    
            nh = MHEADS + HEADS
            pe.wait_ge(act_emptied, EMPTIED["vm"])
            scores(0)
            for n in range(nh):
                gate(2 * n)
                if n + 1 == MHEADS:
                    pe.wait_ge(act_emptied, EMPTIED["kT", 1])
                if n + 1 < nh:
                    scores(n + 1)
                turn_p(n)
                gate(2 * n + 1)
                attend(n)

            na, np_ = block_arrived(pe, "PA"), FRONT.index("PPM")
            wa = ring_block(na, D)[:, 0:4, :]
            pe.wait_ge(got_block[np_ % RING_SLOTS], 16 * (np_ // RING_SLOTS + 2))
            wpm = ring[:, (np_ % RING_SLOTS) * RS:(np_ % RING_SLOTS + 1) * RS].rearrange("p (k n) -> p k n", n=D)
            pe.wait_ge(dve_emptied, EMPTIED["o", nh - 1])
            for f in range(KC):
                fc = slice(f * P, (f + 1) * P)
                for i, (w, y, ks) in enumerate(((wa, yT_area, range(4)), (wpm, yT_area, range(2)), (wpm, ymT, range(2)))):
                    t = fill(("br", f, i))
                    for k in ks:
                        ins = nc.tensor.matmul(t[:, 0:S], w[:, k + (2 if i == 2 else 0), fc],
                                               y[:, k + (4 if i == 1 else 0), :], start=(k == 0),
                                               stop=(k == len(ks) - 1))
                    done(ins)
            n0 = block_arrived(pe, "O0")
            n1 = block_arrived(pe, "O1")
            for b in range(B):
                for hf in range(2):
                    t = fill(("out", b, hf))
                    w = ring_block(n1 if hf else n0, 512)
                    for k in range(KC):
                        pe.wait_ge(merged_ready, k + 1)
                        ins = nc.tensor.matmul(t, merged[:, k, b * P:(b + 1) * P], w[:, k, :], start=(k == 0),
                                               stop=(k == KC - 1))
                    done(ins)

            transposes("x2T", xn2, scaled, 5)
            pe.wait_ge(act_emptied, EMPTIED["x2T", 3])
            t = fill("logits")
            for b in range(B):
                for k in range(KC):
                    ins = nc.tensor.matmul(t[:, b * NE:(b + 1) * NE], xT[:, k, b * P:(b + 1) * P], wr_s[:, k, :],
                                           start=(k == 0), stop=(k == KC - 1))
            done(ins)
            t = fill("pos")
            pe.wait_ge(selected, 1)
            pe.wait_ge(ones_set, 1)
            nc.tensor.matmul(t[:, 0:NE], before[:], sel[:, 0, :], start=True, stop=True)
            nc.tensor.matmul(t[:, NE:2 * NE], ones[:], sel[:, 0, :], start=True, stop=False)
            nc.tensor.matmul(t[:, NE:2 * NE], before[:], sel[:, 1, :], start=False, stop=True)
            nc.tensor.matmul(t[:, 2 * NE:3 * NE], ones[:], sel[:, 0, :], start=True, stop=False)
            done(nc.tensor.matmul(t[:, 2 * NE:3 * NE], ones[:], sel[:, 1, :], start=False, stop=True))
            t = fill("gateT")
            pe.wait_ge(weighted, 1)
            for b in range(B):
                ins = nc.tensor.transpose(t[0:NE, b * P:(b + 1) * P], gts[:, b, :], ident[:])
            done(ins)
            pe.wait_ge(dve_emptied, EMPTIED["gateT"])
            for b in range(B):
                for hf in range(2):
                    t = fill(("bdown", b, hf))
                    done(nc.tensor.matmul(t, gateT_s[:, b * P:(b + 1) * P], b_down_s[0:NE, hf * 512:hf * 512 + 512],
                                          start=True, stop=True))

            def gather(n):
                pe.wait_ge(slots_ready, n + 1)
                for k in range(KC):
                    for b in range(B):
                        ins = nc.tensor.matmul(psum[:, 2, k * SLOTS:(k + 1) * SLOTS], xn2[:, b, k * P:(k + 1) * P],
                                               sel_slot[:, b, :], start=(b == 0), stop=(b == B - 1))
                ins.then_inc(gathered, 1)

            def put_back(n):
                pe.wait_ge(y_ready, n + 1)
                pe.wait_ge(putT_ready, n + 1)
                for j in range(4):
                    b, hf = j // 2, j % 2
                    pe.wait_ge(added, 4 * n + j + 1)
                    nc.tensor.matmul(psum[:, 4 + 3 * (j % 2), :], putT[:, b, :], y_s[:, hf * 512:hf * 512 + 512],
                                     start=True, stop=True).then_inc(put_done, 1)

            pe.wait_ge(dve_emptied, EMPTIED["bdown", B - 1, 1])
            gather(0)
            pe.wait_ge(parts_ready, 1)
            pe.wait_ge(route_done, 1)
            rounds = rounds_of(pe)
            with pe.Fori(0, rounds) as r:
                with pe.Fori(0, NE) as e:
                    i = r * NE + e
                    pe.wait_ge(xe_ready, i + 1)
                    tiles = ((0, 0), (SLOTS, 512))
                    for k in range(UP_CHUNKS):
                        if k == 2:
                            put_back(i)
                        pe.wait_ge(got_up[k], 16 * (i + 1))
                        for c in range(2):
                            for lo, col in tiles:
                                at = k * UP_W + col + FE * c
                                ins = nc.tensor.matmul(psum[lo:lo + SLOTS, c, :], xeT[:, k, :], ring[:, at:at + 512],
                                                       start=(k == 0), stop=False)
                        ins.then_inc(up_used, 1)
                    pe.wait_ge(put_ready, i + 1)
                    for c in range(2):
                        for lo, col in tiles:
                            ins = nc.tensor.matmul(psum[lo:lo + SLOTS, c, :], hot[0:96, :],
                                                   b_part[0:96, col + FE * c:col + FE * c + 512], start=False, stop=True)
                    ins.then_inc(up_done, 1)
                    gather(i + 1)
                    for b in range(B):
                        ins = nc.tensor.transpose(psum[:, 3, b * P:(b + 1) * P], put[:, b, :], ident[:])
                    ins.then_inc(put_turned, 1)
                    pe.wait_ge(xe_ready, i + 2)
                    pe.wait_ge(act_ready, i + 1)
                    for q in range(KC // 2):
                        ins = nc.tensor.transpose(psum[:, 2, q * P:(q + 1) * P], act_s[:, q * P:(q + 1) * P], ident[:])
                    ins.then_inc(act_turned, 1)
                    pe.wait_ge(actT_ready, i + 1)
                    for j in range(DOWN_SLOTS):
                        pe.wait_ge(got_down[j], 16 * (i + 1))
                        for c in range(2):
                            for t_ in range(2):
                                at = DOWN0 + j * DOWN_W + t_ * D + 512 * c
                                f = 2 * j + t_
                                lhsT = actT[:, f % 4, (f // 4) * SLOTS:(f // 4 + 1) * SLOTS]
                                ins = nc.tensor.matmul(psum[t_ * SLOTS:(t_ + 1) * SLOTS, 5 + c, :], lhsT,
                                                       ring[:, at:at + 512], start=(j == 0), stop=(j == DOWN_SLOTS - 1))
                        ins.then_inc(down_used, 1)
            put_back(NE * rounds)


def shape_constants():
    import numpy as np
    f = np.float32
    iota = np.tile(np.arange(SLOTS, dtype=f), (P, P // SLOTS))
    before = np.triu(np.ones((P, P), f), 1)
    causal = np.where(np.arange(P)[None, :] <= np.arange(P)[:, None], f(0), f(-BIG)).astype(f)
    inv = np.power(f(500000.0), -np.arange(HALF, dtype=f) / f(HALF)).astype(f)
    ang = np.arange(S, dtype=f)[:, None] * inv[None, :]
    cos, sin = np.cos(ang).astype(f), np.sin(ang).astype(f)
    rope = np.concatenate([cos, cos, -sin, sin], axis=1)
    t = np.arange(S)
    pool = np.zeros((S, G, S), f)
    for g, w in enumerate((2, 4, 8, 16)):
        lo = np.maximum(t + 1 - w, 0)
        inside = (t[:, None] >= lo[None, :]) & (t[:, None] <= t[None, :])
        pool[:, g, :] = inside / (t + 1 - lo)[None, :] - (t[:, None] == t[None, :])
    expert = np.tile(np.eye(NE, dtype=f), (3, 1))
    return {"ident": np.eye(P, dtype=f), "iota": iota, "before": before, "causal": causal, "rope": rope,
            "pool": pool, "expert": expert}


_INS = ["x", "mem", "w_in", "w_gate", "w_proj_attn", "w_proj_pool", "w_proj_mem", "gains", "pool_w_group", "w_mem_kv",
        "w_out", "norm_ffn_g", "w_router", "b_router", "w_up", "b_up", "w_down", "b_down", "norm_final_g",
        "c_ident", "c_iota", "c_before", "c_causal", "c_rope", "c_pool", "c_expert"]


def kernel(**inputs):
    import numpy as np
    import concourse.bacc as bacc
    from concourse.bass_utils import run_bass_kernel_spmd

    nc = bacc.Bacc("TRN2", target_bir_lowering=False, num_devices=1)
    data = {k: np.ascontiguousarray(v) for k, v in inputs.items()}
    data["gains"] = np.concatenate([data[k].reshape(-1, P) for k in
                                    ("norm_mix_g", "mem_norm_g", "pool_scale", "b_gate")])
    data["norm_final_g"] = data["norm_final_g"].reshape(1, D)
    for k, v in shape_constants().items():
        data["c_" + k] = v
    arrays, args = {}, []
    for name in _INS:
        a = data[name]
        arrays[f"in_{name}"] = a
        args.append(nc.dram_tensor(f"in_{name}", a.shape, mybir.dt.from_np(a.dtype), kind="ExternalInput").ap())
    args.append(nc.dram_tensor("out_0", (1, S, D), F32, kind="ExternalOutput").ap())
    hybrid_layer_kernel(nc, *args)
    r = run_bass_kernel_spmd(nc, [arrays], core_ids=[0])
    return r.results[0]["out_0"]
```

```python
from contextlib import ExitStack

import concourse.bass as bass
from concourse import mybir

F32 = mybir.dt.float32
BF16 = mybir.dt.bfloat16
F32R = mybir.dt.float32r
I32 = mybir.dt.int32
ALU = mybir.AluOpType
ACT = mybir.ActivationFunctionType
AX = mybir.AxisListType

P = 128
S = 256
B = S // P
D = 1024
KC = D // P
M = 256
HEADS = 8
IHEADS = 8
MHEADS = 4
HD = 64
ROPE = 16
HALF = ROPE // 2
TOPK = S // 4
G = 4
NE = 32
TOP = 4
FE = 1024
EPS = 1e-6
ALPHA = 1.702
LIMIT = 7.0
SLOTS = 64
MAX_ROUNDS = S // SLOTS
BIG = 3.0e38
TAKEN = -3.4e38
UNSEL = -1.0e30

C_Q, C_K, C_V, C_IQ, C_IK, C_IW, C_U, C_QM = 0, 512, 1024, 1536, 2048, 2112, 2120, 2376
IN_W = 2632
A_W = C_QM - C_IK

GB = 2 * KC + 2
N_CONST = 8

RING_SLOTS = 4
RS = 4096
FRONT = ["A", "IQ", "Q", "K", "V", "QM", "KV", "G0", "G1", "G2", "G3", "G4", "G5", "PA", "PPM", "O0", "O1"]
UP_W = 2 * FE
UP_CHUNKS = D // P
DOWN_W = 2 * D
DOWN_SLOTS = FE // P // 2
DOWN0 = UP_CHUNKS * UP_W
RING_W = DOWN0 + DOWN_SLOTS * DOWN_W

UNITS = [(name, "rows", j) for name in ("A", "IQ", "Q", "K", "V") for j in range(KC // 2)]
UNITS += [("QM", "cols", c) for c in range(2)]
UNITS += [(f"G{g}", "cols", c) for g in range(6) for c in range(4)]
UNIT_SLOTS = 3
UNIT_W = 1024


def psum_jobs():
    jobs = [("gains", "dve")]
    jobs += [(("xT", j), "dve") for j in range(4)]
    jobs += [(("A", b), "dve") for b in range(B)]
    jobs += [(("IQ", b), "act") for b in range(B)]
    jobs += [(("memT", j), "dve") for j in range(4)]
    jobs += [(("Q", b), "act") for b in range(B)]
    jobs += [(("iqT", j), "act") for j in range(2)] + [("ikT", "act")]
    jobs += [(("idx", h), "act") for h in range(IHEADS)]
    jobs += [(("K", b), "act") for b in range(B)]
    jobs += [(("V", b), "act") for b in range(B)]
    jobs += [("qmT", "act"), ("kmT", "act"), ("vm", "act")]
    jobs += [(("pool", j), "dve") for j in range(2)] + [("mix", "dve")]
    jobs += [(("qT", j), "act") for j in range(2)] + [(("kT", j), "act") for j in range(2)]
    nh = MHEADS + HEADS
    jobs += [(("sc", 0), "act")]
    for n in range(nh):
        jobs += [(("gate", 2 * n), "act")]
        jobs += [(("pT", n), "act")]
        if n + 1 < nh:
            jobs += [(("sc", n + 1), "act" if n + 1 < MHEADS else "dve")]
        jobs += [(("gate", 2 * n + 1), "act"), (("o", n), "dve")]
    for f in range(KC):
        jobs += [(("br", f, i), "dve") for i in range(3)]
    jobs += [(("out", 0, 0), "dve"), (("out", 0, 1), "dve"), (("out", 1, 0), "dve")]
    jobs += [(("x2T", 0, 0), "act"), (("x2T", 0, 1), "act"), (("out", 1, 1), "dve")]
    jobs += [(("x2T", 1, 0), "act"), (("x2T", 1, 1), "act"), ("logits", "dve"), ("pos", "dve")]
    return jobs


JOBS = psum_jobs()
FILLED = {name: n + 1 for n, (name, _) in enumerate(JOBS)}
BANK = {name: n % 8 for n, (name, _) in enumerate(JOBS)}
OWNER = dict(JOBS)
EMPTIED = {}
for _o in ("act", "dve"):
    for _n, _name in enumerate([j for j, o in JOBS if o == _o]):
        EMPTIED[_name] = _n + 1


LAST_USE = {"KV": FILLED["vm"]}
LAST_USE |= {b: FILLED["br", KC - 1, 2] for b in ("PA", "PPM")}
LAST_USE |= {b: FILLED["out", B - 1, 1] for b in ("O0", "O1")}
LAST_SPLIT = {name: n + 1 for n, (name, _, _) in enumerate(UNITS)}


def unit_read(u):
    name, kind, j = UNITS[u]
    if kind == "rows":
        if j < KC // 2 - 1:
            return "unit_used", sum(1 for _, k, i in UNITS[:u + 1] if k == "rows" and i < KC // 2 - 1)
        return "bank_filled", FILLED[name, 1]
    if name == "QM":
        return ("bank_filled", FILLED["qmT"]) if j == 1 else ("unit_used", 5 * (KC // 2 - 1) + 1)
    return "bank_filled", FILLED["gate", 4 * int(name[1]) + j]


def hybrid_layer_kernel(nc, x, mem, w_in, w_gate, w_proj_attn, w_proj_pool, w_proj_mem, gains, pool_w_group,
                        w_mem_kv, w_out, norm_ffn_g, w_router, b_router, w_up, b_up, w_down, b_down,
                        norm_final_g, ident_c, iota_c, before_c, causal_c, rope_c, pool_c, expert_c, out):
    ctx = ExitStack()
    with ctx:
        def sb(name, shape, dt=F32):
            return ctx.enter_context(nc.sbuf_tensor(name, shape, dt))

        def sem(name):
            return ctx.enter_context(nc.semaphore(name))

        ring_at = nc.sbuf_base + (-nc.sbuf_base) % 32
        ring = sb("ring", [P, RING_W])
        unit_hi = nc.alloc_sbuf_tensor_at("unit_hi", [P, UNIT_SLOTS, UNIT_W], F32R, offset=ring_at + 4 * DOWN0)
        unit_lo = nc.alloc_sbuf_tensor_at("unit_lo", [P, UNIT_SLOTS, UNIT_W], F32R,
                                          offset=ring_at + 4 * (DOWN0 + UNIT_SLOTS * UNIT_W))
        xT_lo = nc.alloc_sbuf_tensor_at("xT_lo", [P, KC, S], F32R, offset=ring_at + 4 * (DOWN0 + 2 * UNIT_SLOTS * UNIT_W))
        h_s = sb("h_s", [P, B, D])
        xn_area = sb("xn_area", [P, B, D])
        mem_s = sb("mem_s", [P, B, D])
        xT_hi = sb("xT_hi", [P, KC, S], F32R)
        memT = sb("memT", [P, KC, M])
        gate_area = sb("gate_area", [P, 3 * KC, S])
        qT = sb("qT", [P, HEADS // 2, S])
        kT = sb("kT", [P, HEADS // 2, S])
        ikT = sb("ikT", [P, S])
        v_s = sb("v_s", [P, B, HEADS * HD])
        misc = sb("misc", [P, 1536])
        idx = sb("idx", [P, P + S])
        bias = sb("bias", [P, P + S])
        lg_s = sb("lg_s", [P, 2, P + S])
        p_s = sb("p_s", [P, 2, B * S])
        pT_s = sb("pT_s", [P, 2, 2 * S])
        yT_area = sb("yT_area", [P, 6, S])
        wg_s = sb("wg_s", [HD, G, HD])
        br_s = sb("br_s", [P, B, NE])
        ident = sb("ident", [P, P])
        iota = sb("iota", [P, P])
        before = sb("before", [P, P])
        ones = sb("ones", [P, P])
        causal = sb("causal", [P, P])
        rope = sb("rope", [P, B, 2 * ROPE])
        rope_t = sb("rope_t", [P, 2, 8, ROPE])
        graw = sb("graw", [64, P])
        gT = sb("gT", [P, 64])
        gate_b = sb("gate_b", [P, 3 * KC])
        expert_f = sb("expert_f", [96, NE])
        expert_b = sb("expert_b", [96, NE], BF16)
        st = sb("st", [P, 32])
        eps_s = sb("eps_s", [P, 1])
        top8 = sb("top8", [P, 2, 8])
        sm = sb("sm", [P, 2, 8])
        rt = sb("rt", [P, B, 36])
        rt_m = sb("rt_m", [P, B, 36])
        rt8 = sb("rt8", [P, B, 8])
        sel = sb("sel", [P, B, NE])
        gex = sb("gex", [P, B, NE])
        gts = sb("gts", [P, B, NE])
        rsm = sb("rsm", [P, 8])
        posm = sb("posm", [P, B, NE + 1])
        rounds_i = sb("rounds_i", [1, 1], I32)

        def view(area, start, *dims):
            n = 1
            for d in dims:
                n *= d
            flat = area[:].rearrange("p a b -> p (a b)") if len(area.shape) == 3 else area[:]
            flat = flat[:, start:start + n]
            if len(dims) == 2:
                return flat.rearrange("p (a b) -> p a b", a=dims[0])
            if len(dims) == 3:
                return flat.rearrange("p (a b c) -> p a b c", a=dims[0], b=dims[1])
            return flat

        iq_s = view(gate_area, 0, B, 512)
        q_s = view(gate_area, 1024, B, 512)
        k_s = view(gate_area, 2048, B, 512)
        iqT = view(gate_area, 3072, 4, S)
        pool_a = view(gate_area, 4096, B, G, S)
        gates = gate_area
        qmT = view(xn_area, 0, 2, S)
        kmT = view(xn_area, 512, 2, M)
        vm_s = view(xn_area, 1024, B, MHEADS * HD)
        ymT = view(xn_area, 1536, 2, S)
        xn2 = xn_area
        merged = view(mem_s, 0, KC, S)
        u_s = view(misc, 0, B, G * HD)
        ik_s = view(misc, 512, B, 2 * HD)
        iw_s = view(misc, 768, B, IHEADS)
        pooledT = view(pT_s, 0, G, S)
        relu_s = lg_s
        mix_t = view(lg_s, 0, 3, S)
        kT_odd = view(memT, 0, HEADS // 2, S)
        kmT_odd = view(memT, HEADS // 2 * S, MHEADS // 2, M)
        ikT_odd = view(pT_s, 0, S)
        x2T = memT
        b_up_s = view(mem_s, 0, UP_W)
        b_down_s = view(p_s, 0, D)
        b_mid = view(lg_s, 0, 512).bitcast(BF16)
        b_part = misc[:, :].bitcast(BF16)
        wr_s = view(qT, 0, KC, NE)
        gf_bc = view(kT, 0, D)
        g2_bc = view(v_s, 0, D)
        glu = view(gate_area, 0, FE // 2)
        lin = view(gate_area, 512, FE // 2)
        sig = view(gate_area, 1024, FE // 2)
        act_s = view(gate_area, 1536, FE // 2)
        xeT = view(gate_area, 4096, KC, SLOTS)
        actT = view(gate_area, 4608, KC // 2, P)
        sel_slot = view(gate_area, 5120, B, SLOTS)
        put = view(gate_area, 5248, B, P)
        putT = view(gate_area, 5504, B, P)
        hot = view(gate_area, 5760, SLOTS // 2).bitcast(BF16)
        y_s = view(pT_s, 0, D)
        fin = mem_s

        psum = ctx.enter_context(nc.psum_tensor("psum", [P, 8, 512], F32))

        got_x = [sem(f"got_x{b}") for b in range(B)]
        got_mem = sem("got_mem")
        got_gains = sem("got_gains")
        got_ident = sem("got_ident")
        got_rope = sem("got_rope")
        got_const = sem("got_const")
        got_late = sem("got_late")
        got_bup = sem("got_bup")
        got_block = [sem(f"got_block{i}") for i in range(RING_SLOTS)]
        got_up = [sem(f"got_up{i}") for i in range(UP_CHUNKS)]
        got_down = [sem(f"got_down{i}") for i in range(DOWN_SLOTS)]
        bank_filled = sem("bank_filled")
        act_emptied = sem("act_emptied")
        dve_emptied = sem("dve_emptied")
        emptied = {"act": act_emptied, "dve": dve_emptied}
        ones_set = sem("ones_set")
        zeros_set = sem("zeros_set")
        hi_ready = sem("hi_ready")
        lo_ready = sem("lo_ready")
        unit_used = sem("unit_used")
        xT_hi_ready = sem("xT_hi_ready")
        got_eps = sem("got_eps")
        inverse = sem("inverse")
        lin_ready = sem("lin_ready")
        squares = sem("squares")
        scaled = sem("scaled")
        roped = sem("roped")
        relu_ready = sem("relu_ready")
        relu_used = sem("relu_used")
        bias_ready = sem("bias_ready")
        max_ready = sem("max_ready")
        exp_ready = sem("exp_ready")
        p_ready = sem("p_ready")
        merged_ready = sem("merged_ready")
        parts_ready = sem("parts_ready")
        route_max = sem("route_max")
        route_exp = sem("route_exp")
        selected = sem("selected")
        weighted = sem("weighted")
        g_final = sem("g_final")
        route_done = sem("route_done")
        dve_own = sem("dve_own")
        act_own = sem("act_own")
        pool_own = sem("pool_own")
        slots_ready = sem("slots_ready")
        put_ready = sem("put_ready")
        gathered = sem("gathered")
        xe_ready = sem("xe_ready")
        put_turned = sem("put_turned")
        putT_ready = sem("putT_ready")
        up_done = sem("up_done")
        down_done = sem("down_done")
        up_used = sem("up_used")
        down_used = sem("down_used")
        glu_ready = sem("glu_ready")
        sig_ready = sem("sig_ready")
        act_ready = sem("act_ready")
        act_turned = sem("act_turned")
        actT_ready = sem("actT_ready")
        y_ready = sem("y_ready")
        put_done = sem("put_done")
        added = sem("added")
        stored = sem("stored")

        block = ctx.enter_context(nc.Block())

        def ring_block(n, cols):
            s = (n % RING_SLOTS) * RS
            return ring[:, s:s + KC * cols].rearrange("p (k n) -> p k n", n=cols)

        def rows(w):
            return w.rearrange("(k p) n -> p k n", p=P)

        def unit_views(u):
            name, kind, j = UNITS[u]
            cols = {"A": A_W, "QM": 256}.get(name, 512)
            w = ring_block(FRONT.index(name), cols)
            src = w[:, 2 * j:2 * j + 2, :] if kind == "rows" else w[:, :, j * P:(j + 1) * P]
            k, n = src.shape[1], src.shape[2]
            hi, lo = (t[:, u % UNIT_SLOTS, 0:k * n].rearrange("p (k n) -> p k n", n=n) for t in (unit_hi, unit_lo))
            return src, hi, lo

        def block_arrived(eng, name):
            n = FRONT.index(name)
            eng.wait_ge(got_block[n % RING_SLOTS], 16 * (n // RING_SLOTS + 1))
            return n

        def bank(name):
            return psum[:, BANK[name], :]

        def rounds_of(eng):
            return nc.values_load(rounds_i[0:1, 0:1], engines=[eng.engine], min_val=1, max_val=MAX_ROUNDS)

        @block.sync
        def _(sp):
            for b in range(B):
                sp.dma_start(h_s[:, b, :], x[0, b * P:(b + 1) * P, :]).then_inc(got_x[b], 16)
            win = rows(w_in[0])
            wgt = rows(w_gate[0])
            src = {"A": [(win[:, :, C_IK:C_QM], 0)], "IQ": [(win[:, :, C_IQ:C_IK], 0)], "Q": [(win[:, :, C_Q:C_K], 0)],
                   "K": [(win[:, :, C_K:C_V], 0)], "V": [(win[:, :, C_V:C_IQ], 0)], "QM": [(win[:, :, C_QM:IN_W], 0)],
                   "KV": [(rows(w_mem_kv[0]), 0)], "PA": [(rows(w_proj_attn[0]), 0)],
                   "PPM": [(rows(w_proj_pool[0]), 0), (rows(w_proj_mem[0]), 2048)],
                   "O0": [(rows(w_out[0])[:, :, 0:512], 0)], "O1": [(rows(w_out[0])[:, :, 512:1024], 0)]}
            for g in range(6):
                src[f"G{g}"] = [(wgt[:, :, 512 * g:512 * (g + 1)], 0)]
            for n, name in enumerate(FRONT):
                if n >= RING_SLOTS:
                    before_it = FRONT[n - RING_SLOTS]
                    if before_it in LAST_SPLIT:
                        sp.wait_ge(lo_ready, LAST_SPLIT[before_it])
                    else:
                        sp.wait_ge(bank_filled, LAST_USE[before_it])
                for ap, at in src[name]:
                    k, cols = ap.shape[1], ap.shape[2]
                    s = (n % RING_SLOTS) * RS + at
                    dst = ring[:, s:s + k * cols].rearrange("p (k n) -> p k n", n=cols)
                    sp.dma_start(dst, ap).then_inc(got_block[n % RING_SLOTS], 16)
                if name == "A":
                    sp.dma_start(mem_s[:], mem.rearrange("a (b p) d -> p (a b) d", p=P)).then_inc(got_mem, 16)

            def load_up(e, k):
                sp.dma_start(ring[:, k * UP_W:(k + 1) * UP_W],
                             w_up[0][bass.ds(e, 1), k * P:(k + 1) * P, :].rearrange("a p n -> (a p) n"))\
                  .then_inc(got_up[k], 16)

            def load_down(e, j):
                s = DOWN0 + j * DOWN_W
                sp.dma_start(ring[:, s:s + DOWN_W].rearrange("p (t n) -> p t n", t=2),
                             w_down[0][bass.ds(e, 1), 2 * j * P:2 * (j + 1) * P, :]
                             .rearrange("a (t p) n -> p (a t) n", p=P)).then_inc(got_down[j], 16)

            last = {n % RING_SLOTS: LAST_USE[name] for n, name in enumerate(FRONT) if name in LAST_USE}
            sp.wait_ge(bank_filled, FILLED["gate", 3 * KC - 1])
            for j in range(DOWN_SLOTS):
                load_down(0, j)
            order = sorted(range(UP_CHUNKS), key=lambda k: last[k // 2])
            for k in order:
                sp.wait_ge(bank_filled, last[k // 2])
                load_up(0, k)

            def expert_weights(e, i):
                for k in range(UP_CHUNKS):
                    sp.wait_ge(up_used, (i - 1) * UP_CHUNKS + k + 1)
                    load_up(e, k)
                for j in range(DOWN_SLOTS):
                    sp.wait_ge(down_used, (i - 1) * DOWN_SLOTS + j + 1)
                    load_down(e, j)

            with sp.Fori(1, NE) as e:
                expert_weights(e, e)
            sp.wait_ge(route_done, 1)
            rounds = rounds_of(sp)
            with sp.If(rounds > 1):
                with sp.Fori(1, rounds) as r:
                    with sp.Fori(0, NE) as e:
                        expert_weights(e, r * NE + e)
            sp.wait_ge(stored, 16 * B)

        @block.gpsimd
        def _(pool):
            nc.gpsimd.memset(ones[:], 1.0).then_inc(ones_set, 1)
            for u in range(len(UNITS)):
                src, hi, lo = unit_views(u)
                pool.wait_ge(hi_ready, u + 1)
                nc.gpsimd.tensor_tensor(lo, src, hi.bitcast(F32), ALU.subtract).then_inc(lo_ready, 1)

        @block.scalar
        def _(act):
            own = [0]

            def link(ins):
                own[0] += 1
                ins.then_inc(act_own, 1)
                act.wait_ge(act_own, own[0])

            act.dma_start(ident[:], ident_c).then_inc(got_ident, 16)
            act.dma_start(graw[0:gains.shape[0], :], gains).then_inc(got_gains, 16)
            act.dma_start(rope[:], rope_c.rearrange("(b p) c -> p b c", p=P)).then_inc(got_rope, 16)
            consts = [(iota[:], iota_c), (before[:], before_c), (causal[:], causal_c), (expert_f[:], expert_c),
                      (pool_a, pool_c.rearrange("(b p) g t -> p b g t", p=P)),
                      (wg_s[:], pool_w_group[0].rearrange("g c d -> c g d")),
                      (br_s[:, 0, :], b_router.to_broadcast([P, NE])), (br_s[:, 1, :], b_router.to_broadcast([P, NE]))]
            for dst, s in consts:
                act.dma_start(dst, s).then_inc(got_const, 16)

            def squares_of(src, at, b):
                return nc.scalar.activation(view(gate_area, 2048 + 1024 * b, D), src[:, b, :], ACT.Square,
                                            accum_out=st[:, at + b:at + b + 1])

            def root(at):
                nc.scalar.activation(st[:, at + 4:at + 6], st[:, at:at + 2], ACT.Sqrt, bias=eps_s[:, 0:1],
                                     scale=1.0 / D).then_inc(squares, 1)

            def split(u):
                if u >= UNIT_SLOTS:
                    which, value = unit_read(u - UNIT_SLOTS)
                    act.wait_ge({"unit_used": unit_used, "bank_filled": bank_filled}[which], value)
                if u == 0 or UNITS[u][0] != UNITS[u - 1][0]:
                    block_arrived(act, UNITS[u][0])
                src, hi, _ = unit_views(u)
                nc.scalar.activation(hi, src, ACT.Copy).then_inc(hi_ready, 1)

            act.wait_ge(got_eps, 1)
            nc.scalar.activation(st[:, 31:32], eps_s[:], ACT.Sqrt)
            for b in range(B):
                act.wait_ge(got_x[b], 16)
                ins = squares_of(h_s, 0, b)
            link(ins)
            root(0)
            for u in range(3):
                split(u)

            def empty(name):
                act.wait_ge(bank_filled, FILLED[name])
                return bank(name)

            act.wait_ge(dve_emptied, EMPTIED["gains"])
            for j in range(4):
                t = empty(("xT", j))
                for c in range(2):
                    k = 2 * j + c
                    ins = nc.scalar.activation(xT_hi[:, k, :], t[:, c * S:(c + 1) * S], ACT.Copy, scale=gT[:, k:k + 1])
                ins.then_inc(xT_hi_ready, 1)
            split(3)
            split(4)
            act.wait_ge(got_mem, 16)
            squares_of(mem_s, 8, 0)
            link(squares_of(mem_s, 8, 1))
            root(8)
            for u in range(5, 11):
                split(u)

            def copy(name, dst, part=None):
                t = empty(name)
                src_ap = t if part is None else part(t)
                nc.scalar.activation(dst, src_ap, ACT.Copy).then_inc(act_emptied, 1)

            def pair(t):
                return t.rearrange("p (c s) -> p c s", c=2)

            def copy_halves(name, even, odd, part):
                t = empty(name)
                nc.scalar.activation(even[0:HD], part(t)[0:HD], ACT.Copy)
                nc.scalar.activation(odd[HD:P], part(t)[HD:P], ACT.Copy).then_inc(act_emptied, 1)

            for b in range(B):
                copy(("IQ", b), iq_s[:, b, :])
            for u in range(11, 15):
                split(u)
            for b in range(B):
                copy(("Q", b), q_s[:, b, :])
            for j in range(2):
                copy(("iqT", j), iqT[:, 2 * j:2 * j + 2, :], pair)
            act.wait_ge(zeros_set, 1)
            copy_halves("ikT", ikT[:, :], ikT_odd, lambda t: t[:, 0:S])
            for h in range(IHEADS):
                if h >= 2:
                    act.wait_ge(relu_used, h - 1)
                t = empty(("idx", h))
                nc.scalar.activation(relu_s[:, h % 2, :], t[:, 0:P + S], ACT.Relu, scale=HD ** -0.5)\
                  .then_inc(act_emptied, 1)
            for u in range(15, 19):
                split(u)
            for b in range(B):
                copy(("K", b), k_s[:, b, :])
            act.wait_ge(bank_filled, FILLED["memT", 3])
            for c in range(3):
                act.dma_start(b_up_s[32 * c:32 * c + 32, :], b_up[0]).then_inc(got_bup, 16)
                act.dma_start(b_down_s[32 * c:32 * c + 32, :], b_down[0]).then_inc(got_bup, 16)
            for u in range(19, 23):
                split(u)
            for b in range(B):
                copy(("V", b), v_s[:, b, :])
            split(23)
            split(24)
            copy("qmT", qmT, pair)
            act.wait_ge(bank_filled, FILLED["vm"])
            act.wait_ge(zeros_set, 2)
            copy_halves("kmT", kmT, kmT_odd, pair)
            copy("vm", vm_s, pair)
            for j in range(2):
                copy(("qT", j), qT[:, 2 * j:2 * j + 2, :], pair)
            for j in range(2):
                copy_halves(("kT", j), kT[:, 2 * j:2 * j + 2, :], kT_odd[:, 2 * j:2 * j + 2, :], pair)

            link(nc.scalar.mul(gate_b[:], gT[:, GB:GB + 3 * KC], 0.5))

            def gate(m):
                t = empty(("gate", m))
                nc.scalar.activation(gates[:, m, :], t[:, 0:S], ACT.Tanh, bias=gate_b[:, m:m + 1], scale=0.5)\
                  .then_inc(act_emptied, 1)
                u = 22 + m + UNIT_SLOTS
                if u < len(UNITS):
                    split(u)

            def exps(n):
                act.wait_ge(max_ready, n + 1)
                if n >= 2:
                    act.wait_ge(bank_filled, FILLED["pT", n - 2])
                for b in range(B):
                    if n < MHEADS:
                        src_ap, w = bank(("sc", n))[:, b * M:(b + 1) * M], M
                    else:
                        src_ap, w = lg_s[:, n % 2, b * P:P + b * S], P * (b + 1)
                    ins = nc.scalar.activation(p_s[:, n % 2, b * S:b * S + w], src_ap, ACT.Exp,
                                               bias=sm[:, n % 2, b:b + 1], scale=HD ** -0.5,
                                               accum_out=sm[:, n % 2, 2 + b:3 + b])
                    if n < MHEADS and b == B - 1:
                        ins.then_inc(act_emptied, 1)
                        act.wait_ge(act_emptied, EMPTIED["sc", n])
                        nc.scalar.copy(sm[:, n % 2, 6:7], sm[:, n % 2, 2:3]).then_inc(exp_ready, 1)
                    elif b == B - 1:
                        ins.then_inc(exp_ready, 1)

            def copy_pT(n):
                t = empty(("pT", n))
                if n >= 2:
                    act.wait_ge(bank_filled, FILLED["o", n - 2])
                if n < MHEADS:
                    nc.scalar.activation(pT_s[:, n % 2, :], t, ACT.Copy).then_inc(act_emptied, 1)
                else:
                    nc.scalar.activation(pT_s[:, n % 2, 0:S + P], t[:, 0:S + P], ACT.Copy).then_inc(act_emptied, 1)

            nh = MHEADS + HEADS
            act.wait_ge(dve_emptied, EMPTIED["mix"])
            act.wait_ge(parts_ready, 1)
            exps(0)
            for n in range(nh):
                gate(2 * n)
                copy_pT(n)
                if n + 1 < nh:
                    exps(n + 1)
                gate(2 * n + 1)
            act.wait_ge(bank_filled, FILLED["o", nh - 1])
            act.dma_start(wr_s, rows(w_router[0])).then_inc(got_late, 16)
            act.dma_start(gf_bc, norm_final_g.to_broadcast([P, D])).then_inc(got_late, 16)
            act.dma_start(g2_bc, norm_ffn_g.to_broadcast([P, D])).then_inc(got_late, 16)

            act.wait_ge(dve_emptied, EMPTIED["out", 0, 1])
            squares_of(h_s, 16, 0)

            def copy_x2T(b, hf):
                t = empty(("x2T", b, hf))
                nc.scalar.activation(x2T[:, 4 * hf:4 * hf + 4, b * P:(b + 1) * P],
                                     t.rearrange("p (k s) -> p k s", k=4), ACT.Copy).then_inc(act_emptied, 1)

            copy_x2T(0, 0)
            copy_x2T(0, 1)
            act.wait_ge(dve_emptied, EMPTIED["out", 1, 1])
            link(squares_of(h_s, 16, 1))
            root(16)
            copy_x2T(1, 0)
            copy_x2T(1, 1)
            act.wait_ge(route_max, 1)
            for b in range(B):
                ins = nc.scalar.activation(gex[:, b, :], rt[:, b, TOP:], ACT.Exp, bias=rsm[:, b:b + 1])
            ins.then_inc(route_exp, 1)

            def take_gathered(i):
                act.wait_ge(gathered, i + 1)
                nc.scalar.activation(xeT, psum[:, 2, :].rearrange("p (k c) -> p k c", k=KC), ACT.Copy)\
                  .then_inc(xe_ready, 1)

            take_gathered(0)
            act.wait_ge(route_done, 1)
            rounds = rounds_of(act)
            with act.Fori(0, rounds) as r:
                with act.Fori(0, NE) as e:
                    i = r * NE + e
                    act.wait_ge(glu_ready, i + 1)
                    nc.scalar.activation(sig, glu, ACT.Sigmoid, scale=ALPHA).then_inc(sig_ready, 1)
                    take_gathered(i + 1)
                    act.wait_ge(put_turned, i + 1)
                    nc.scalar.activation(putT, psum[:, 3, 0:B * P].rearrange("p (b c) -> p b c", b=B), ACT.Copy)\
                      .then_inc(putT_ready, 1)
                    act.wait_ge(act_turned, i + 1)
                    nc.scalar.activation(actT, psum[:, 2, :].rearrange("p (q c) -> p q c", c=P), ACT.Copy)\
                      .then_inc(actT_ready, 1)
                    act.wait_ge(down_done, i + 1)
                    nc.scalar.activation(y_s, psum[:, 5:7, :].rearrange("p a n -> p (a n)"), ACT.Copy)\
                      .then_inc(y_ready, 1)

            act.wait_ge(added, 2 + 4 * (NE * rounds + 1))
            squares_of(h_s, 24, 0)
            link(squares_of(h_s, 24, 1))
            root(24)
            for b in range(B):
                act.wait_ge(g_final, b + 1)
                act.dma_start(out[0, b * P:(b + 1) * P, :], fin[:, b, :]).then_inc(stored, 16)

        @block.vector
        def _(dve):
            own = [0]

            def link(ins):
                own[0] += 1
                ins.then_inc(dve_own, 1)
                dve.wait_ge(dve_own, own[0])

            nc.vector.memset(eps_s[:], EPS).then_inc(got_eps, 1)
            nc.vector.memset(ikT[HD:P, :], 0.0)
            nc.vector.memset(ikT_odd[0:HD, :], 0.0).then_inc(zeros_set, 1)

            def inverse_rms(at, count):
                dve.wait_ge(squares, count)
                nc.vector.reciprocal(st[:, at + 6:at + 8], st[:, at + 4:at + 6]).then_inc(inverse, 1)
                dve.wait_ge(inverse, count)

            def scale_rows(dst, src, at, count):
                inverse_rms(at, count)
                for b in range(B):
                    nc.vector.tensor_scalar(dst[:, b, :], src[:, b, :], st[:, at + 6 + b:at + 7 + b], None, ALU.mult)\
                      .then_inc(scaled, 1)

            def empty(name):
                dve.wait_ge(bank_filled, FILLED[name])
                return bank(name)

            t = empty("gains")
            nc.vector.tensor_copy(gT[:, 0:gains.shape[0]], t[:, 0:gains.shape[0]]).then_inc(dve_emptied, 1)
            scale_rows(xn_area, h_s, 0, 1)
            for j in range(4):
                t = empty(("xT", j))
                dve.wait_ge(xT_hi_ready, j + 1)
                for c in range(2):
                    k = 2 * j + c
                    ins = nc.vector.scalar_tensor_tensor(out=xT_lo[:, k, :], in0=t[:, c * S:(c + 1) * S],
                                                         scalar=gT[:, k:k + 1], in1=xT_hi[:, k, :].bitcast(F32),
                                                         op0=ALU.mult, op1=ALU.subtract)
                ins.then_inc(dve_emptied, 1)
            scale_rows(mem_s, mem_s, 8, 2)
            for b in range(B):
                t = empty(("A", b))
                o = C_U - C_IK
                nc.vector.tensor_copy(u_s[:, b, :], t[:, o:o + G * HD])
                nc.vector.tensor_copy(ik_s[:, b, 0:HD], t[:, 0:HD])
                nc.vector.tensor_copy(ik_s[:, b, HD:2 * HD], t[:, 0:HD])
                o = C_IW - C_IK
                nc.vector.tensor_scalar(iw_s[:, b, :], t[:, o:o + IHEADS], IHEADS ** -0.5, None, ALU.mult)\
                  .then_inc(dve_emptied, 1)
                dve.wait_ge(dve_emptied, EMPTIED["A", b])

            rotated = [0]

            def rotate(t, b, heads):
                v = t[:, b, :].rearrange("p (h d) -> p h d", h=heads)
                cc = rope[:, b:b + 1, 0:ROPE].to_broadcast([P, heads, ROPE])
                s1 = rope[:, b:b + 1, ROPE:ROPE + HALF].to_broadcast([P, heads, HALF])
                s2 = rope[:, b:b + 1, ROPE + HALF:2 * ROPE].to_broadcast([P, heads, HALF])
                c, s = rope_t[:, 0, 0:heads, :], rope_t[:, 1, 0:heads, :]
                nc.vector.tensor_tensor(c, v[:, :, 0:ROPE], cc, ALU.mult)
                nc.vector.tensor_tensor(s[:, :, 0:HALF], v[:, :, HALF:ROPE], s1, ALU.mult)
                link(nc.vector.tensor_tensor(s[:, :, HALF:ROPE], v[:, :, 0:HALF], s2, ALU.mult))
                nc.vector.tensor_tensor(v[:, :, 0:ROPE], c, s, ALU.add).then_inc(roped, 1)
                rotated[0] += 1
                dve.wait_ge(roped, rotated[0])

            dve.wait_ge(got_rope, 16)
            for b in range(B):
                rotate(ik_s, b, 2)
            for b in range(B):
                dve.wait_ge(act_emptied, EMPTIED["IQ", b])
                rotate(iq_s, b, HEADS)
            for j in range(4):
                t = empty(("memT", j))
                for c in range(2):
                    k = 2 * j + c
                    ins = nc.vector.tensor_scalar(memT[:, k, :], t[:, c * M:(c + 1) * M], gT[:, KC + k:KC + k + 1],
                                                  None, ALU.mult)
                ins.then_inc(dve_emptied, 1)
            for b in range(B):
                dve.wait_ge(act_emptied, EMPTIED["Q", b])
                rotate(q_s, b, HEADS)
            for h in range(IHEADS):
                dve.wait_ge(act_emptied, EMPTIED["idx", h])
                for b in range(B):
                    cols = slice(b * P, P + b * S)
                    if h == 0:
                        ins = nc.vector.tensor_scalar(idx[:, cols], relu_s[:, h % 2, cols], iw_s[:, b, h:h + 1], None,
                                                      ALU.mult)
                    else:
                        ins = nc.vector.scalar_tensor_tensor(out=idx[:, cols], in0=relu_s[:, h % 2, cols],
                                                             scalar=iw_s[:, b, h:h + 1], in1=idx[:, cols],
                                                             op0=ALU.mult, op1=ALU.add)
                ins.then_inc(relu_used, 1)
                dve.wait_ge(relu_used, h + 1)
            dve.wait_ge(got_const, 16 * N_CONST)
            nc.vector.tensor_tensor(idx[:, 0:P], idx[:, 0:P], causal[:], ALU.add)
            link(nc.vector.tensor_tensor(idx[:, 2 * P:3 * P], idx[:, 2 * P:3 * P], causal[:], ALU.add))

            def take_top(b, first, n):
                cols = slice(b * P, P + b * S)
                for _ in range(first, first + n):
                    link(nc.vector.max(out=top8[:, b, :], in_=idx[:, cols]))
                    link(nc.vector.match_replace(out=idx[:, cols], in_to_replace=top8[:, b, :], in_values=idx[:, cols],
                                                 imm_value=TAKEN))
                if first + n == TOPK // 8:
                    link(nc.vector.tensor_scalar(bias[:, cols], idx[:, cols], (TAKEN - BIG) / 2, UNSEL, ALU.is_gt,
                                                 ALU.mult))
                    d = slice(2 * b * P, (2 * b + 1) * P)
                    link(nc.vector.tensor_tensor(bias[:, d], bias[:, d], causal[:], ALU.add))

            take_top(0, 0, TOPK // 8)
            take_top(1, 0, TOPK // 8)
            for b in range(B):
                dve.wait_ge(act_emptied, EMPTIED["K", b])
                rotate(k_s, b, HEADS)
            dve.wait_ge(bank_filled, FILLED["vm"])
            nc.vector.memset(kT[HD:P], 0.0)
            nc.vector.memset(kT_odd[0:HD], 0.0)
            nc.vector.memset(kmT[HD:P], 0.0)
            nc.vector.memset(kmT_odd[0:HD], 0.0).then_inc(zeros_set, 1)
            for j in range(2):
                t = empty(("pool", j))
                nc.vector.tensor_copy(pooledT[0:HD, 2 * j:2 * j + 2, :],
                                      t[0:HD, :].rearrange("p (g s) -> p g s", g=2)).then_inc(dve_emptied, 1)
            t = empty("mix")
            for c in range(2):
                ins = nc.vector.tensor_scalar(yT_area[:, 4 + c, :], t[:, c * S:(c + 1) * S],
                                              gT[:, 2 * KC + c:2 * KC + c + 1], None, ALU.mult)
            ins.then_inc(dve_emptied, 1)

            dve.wait_ge(got_bup, 96)
            for src_b, at in ((b_up_s[:, 0:D], 0), (b_up_s[:, D:2 * D], D), (b_down_s, 2 * D)):
                rest, part, mid = src_b[0:96, :], b_part[:, at:at + D], b_mid[0:96, :]
                link(nc.vector.tensor_copy(part[0:96, :], rest))
                link(nc.vector.tensor_tensor(rest, rest, part[0:96, :], ALU.subtract))
                link(nc.vector.tensor_copy(mid, rest))
                nc.vector.tensor_copy(part[32:64, :], mid[32:64, :])
                link(nc.vector.tensor_tensor(rest, rest, mid, ALU.subtract))
                link(nc.vector.tensor_copy(part[64:96, :], rest[64:96, :]))
            nc.vector.tensor_copy(expert_b[:], expert_f[:]).then_inc(parts_ready, 1)

            def maxima(n):
                if n < MHEADS:
                    t = empty(("sc", n))
                    if n >= 2:
                        dve.wait_ge(p_ready, n - 1)
                    link(nc.vector.reduce_max(sm[:, n % 2, 4:6], t.rearrange("p (b s) -> p b s", b=B), AX.X))
                else:
                    t = empty(("sc", n))
                    dve.wait_ge(exp_ready, n - 1)
                    for b in range(B):
                        cols = slice(b * P, P + b * S)
                        ins = nc.vector.tensor_tensor(lg_s[:, n % 2, cols], t[:, cols], bias[:, cols], ALU.add)
                    ins.then_inc(dve_emptied, 1)
                    dve.wait_ge(dve_emptied, EMPTIED["sc", n])
                    for b in range(B):
                        cols = slice(b * P, P + b * S)
                        ins = nc.vector.reduce_max(sm[:, n % 2, 4 + b:5 + b], lg_s[:, n % 2, cols], AX.X)
                    link(ins)
                nc.vector.tensor_scalar(sm[:, n % 2, 0:2], sm[:, n % 2, 4:6], -HD ** -0.5, None, ALU.mult)\
                  .then_inc(max_ready, 1)

            def normalise(n):
                dve.wait_ge(exp_ready, n + 1)
                link(nc.vector.reciprocal(sm[:, n % 2, 4:6], sm[:, n % 2, 2:4]))
                for b in range(B):
                    w = M if n < MHEADS else P * (b + 1)
                    ins = nc.vector.tensor_scalar(p_s[:, n % 2, b * S:b * S + w], p_s[:, n % 2, b * S:b * S + w],
                                                  sm[:, n % 2, 4 + b:5 + b], None, ALU.mult)
                ins.then_inc(p_ready, 1)

            def take_o(n):
                t = empty(("o", n))
                lo = HD * (n % 2)
                dst = ymT[lo:lo + HD, n // 2, :] if n < MHEADS else yT_area[lo:lo + HD, (n - MHEADS) // 2, :]
                nc.vector.tensor_copy(dst, t[lo:lo + HD, 0:S]).then_inc(dve_emptied, 1)

            nh = MHEADS + HEADS
            maxima(0)
            normalise(0)
            for n in range(nh):
                if n + 1 < nh:
                    maxima(n + 1)
                    normalise(n + 1)
                take_o(n)

            dve.wait_ge(act_emptied, EMPTIED["gate", 3 * KC - 1])
            for f in range(KC):
                for i in range(3):
                    t = empty(("br", f, i))
                    ins = nc.vector.scalar_tensor_tensor(out=mix_t[:, i, :], in0=gates[:, KC * i + f, :], scalar=1.0,
                                                         in1=t[:, 0:S], op0=ALU.add, op1=ALU.mult)
                    ins.then_inc(dve_emptied, 1)
                dve.wait_ge(dve_emptied, EMPTIED["br", f, 2])
                link(nc.vector.tensor_tensor(mix_t[:, 0, :], mix_t[:, 0, :], mix_t[:, 1, :], ALU.add))
                nc.vector.tensor_tensor(merged[:, f, :], mix_t[:, 0, :], mix_t[:, 2, :], ALU.add)\
                  .then_inc(merged_ready, 1)
                dve.wait_ge(merged_ready, f + 1)
            dve.wait_ge(got_late, 48)
            for b in range(B):
                for hf in range(2):
                    t = empty(("out", b, hf))
                    cols = slice(hf * 512, hf * 512 + 512)
                    nc.vector.scalar_tensor_tensor(out=h_s[:, b, cols], in0=t, scalar=0.5, in1=h_s[:, b, cols],
                                                   op0=ALU.mult, op1=ALU.add).then_inc(dve_emptied, 1)
                    dve.wait_ge(dve_emptied, EMPTIED["out", b, hf])
                    nc.vector.tensor_tensor(xn2[:, b, cols], h_s[:, b, cols], g2_bc[:, cols], ALU.mult)\
                      .then_inc(scaled, 1)
            nc.vector.memset(rt[:, :, 0:TOP], BIG)
            inverse_rms(16, 3)

            t = empty("logits")
            for b in range(B):
                ins = nc.vector.scalar_tensor_tensor(out=rt[:, b, TOP:], in0=t[:, b * NE:(b + 1) * NE],
                                                     scalar=st[:, 22 + b:23 + b], in1=br_s[:, b, :], op0=ALU.mult,
                                                     op1=ALU.add)
            ins.then_inc(dve_emptied, 1)
            dve.wait_ge(dve_emptied, EMPTIED["logits"])
            for b in range(B):
                ins = nc.vector.max(out=rt8[:, b, :], in_=rt[:, b, :])
            link(ins)
            nc.vector.tensor_scalar(rsm[:, 0:B], rt8[:, :, TOP:TOP + 1].rearrange("p b o -> p (b o)"), -1.0, None, ALU.mult)\
              .then_inc(route_max, 1)
            for b in range(B):
                ins = nc.vector.match_replace(out=rt_m[:, b, :], in_to_replace=rt8[:, b, :], in_values=rt[:, b, :],
                                              imm_value=TAKEN)
            link(ins)
            nc.vector.tensor_scalar(sel[:], rt_m[:, :, TOP:], (TAKEN - BIG) / 2, None, ALU.is_lt).then_inc(selected, 1)
            dve.wait_ge(selected, 1)
            dve.wait_ge(route_exp, 1)
            for b in range(B):
                ins = nc.vector.scalar_tensor_tensor(out=gex[:, b, :], in0=gex[:, b, :], scalar=1.0, in1=sel[:, b, :],
                                                     op0=ALU.mult, op1=ALU.mult, accum_out=rsm[:, 2 + b:3 + b])
            link(ins)
            link(nc.vector.reciprocal(rsm[:, 4:6], rsm[:, 2:4]))
            for b in range(B):
                ins = nc.vector.tensor_scalar(gts[:, b, :], gex[:, b, :], rsm[:, 4 + b:5 + b], None, ALU.mult)
            ins.then_inc(weighted, 1)

            t = empty("pos")
            pos = t[:, 0:B * NE].rearrange("p (b e) -> p b e", b=B)
            nc.vector.scalar_tensor_tensor(out=posm[:, :, 0:NE], in0=pos, scalar=1.0, in1=sel[:], op0=ALU.add,
                                           op1=ALU.mult)
            nc.vector.tensor_scalar(rt8[:, 0, 0:MAX_ROUNDS], iota[:, 0:MAX_ROUNDS], float(SLOTS), None, ALU.mult)
            nc.vector.reduce_max(rsm[:, 6:7], t[:, B * NE:(B + 1) * NE], AX.X).then_inc(dve_emptied, 1)
            dve.wait_ge(dve_emptied, EMPTIED["pos"])
            link(nc.vector.tensor_scalar(posm[:, :, 0:NE], posm[:, :, 0:NE], -1.0, None, ALU.add))
            nc.vector.tensor_scalar(posm[:, :, NE:NE + 1], posm[:, :, 0:1], -float(SLOTS), None, ALU.add)
            link(nc.vector.tensor_scalar(rt8[:, 1, 0:MAX_ROUNDS], rt8[:, 0, 0:MAX_ROUNDS], rsm[:, 6:7], None,
                                         ALU.is_lt))
            link(nc.vector.reduce_sum(rsm[:, 7:8], rt8[:, 1, 0:MAX_ROUNDS], AX.X))
            nc.vector.tensor_copy(rounds_i[:, :], rsm[0:1, 7:8]).then_inc(route_done, 1)

            def gather_columns(e, n):
                if n is not None:
                    dve.wait_ge(gathered, n)
                for b in range(B):
                    ins = nc.vector.tensor_scalar(sel_slot[:, b, :], iota[:, 0:SLOTS], posm[:, b, bass.ds(e, 1)],
                                                  st[:, 22 + b:23 + b], ALU.is_equal, ALU.mult)
                ins.then_inc(slots_ready, 1)

            gather_columns(0, None)
            nc.vector.engine_nop().then_inc(added, 2)

            def take_back(n):
                for j in range(4):
                    b, hf = j // 2, j % 2
                    cols = slice(hf * 512, hf * 512 + 512)
                    dve.wait_ge(put_done, 4 * n + j + 1)
                    nc.vector.tensor_tensor(h_s[:, b, cols], psum[:, 4 + 3 * (j % 2), :], h_s[:, b, cols],
                                            ALU.add).then_inc(added, 1)

            nc.vector.memset(putT, 0.0).then_inc(putT_ready, 1)
            nc.vector.memset(y_s, 0.0).then_inc(y_ready, 1)
            dve.wait_ge(route_done, 1)
            rounds = rounds_of(dve)
            link_base = own[0]
            with dve.Fori(0, rounds) as r:
                with dve.Fori(0, NE) as e:
                    i = r * NE + e
                    gather_columns(e + 1, i + 1)
                    take_back(i)
                    for b in range(B):
                        nc.vector.tensor_scalar(put[:, b, :], iota[:], posm[:, b, bass.ds(e, 1)],
                                                gts[:, b, bass.ds(e, 1)], ALU.is_equal, ALU.mult)
                    nc.vector.tensor_copy(hot[0:96, :], expert_b[:, bass.ds(e, 1)].to_broadcast([96, SLOTS]))\
                      .then_inc(put_ready, 1)
                    dve.wait_ge(up_done, i + 1)
                    nc.vector.tensor_scalar(glu, psum[:, 0, :], LIMIT, None, ALU.min).then_inc(glu_ready, 1)
                    nc.vector.tensor_scalar(lin, psum[:, 1, :], LIMIT, -LIMIT, ALU.min, ALU.max).then_inc(lin_ready, 1)
                    dve.wait_ge(lin_ready, 2 * i + 1)
                    nc.vector.scalar_tensor_tensor(out=lin, in0=lin, scalar=1.0, in1=glu, op0=ALU.add, op1=ALU.mult)\
                      .then_inc(lin_ready, 1)
                    dve.wait_ge(sig_ready, i + 1)
                    dve.wait_ge(lin_ready, 2 * i + 2)
                    nc.vector.tensor_tensor(act_s, lin, sig, ALU.mult).then_inc(act_ready, 1)
                nc.vector.tensor_scalar(posm[:], posm[:], -float(SLOTS), None, ALU.add).then_inc(dve_own, 1)
                dve.wait_ge(dve_own, link_base + r + 1)
            take_back(NE * rounds)
            inverse_rms(24, 4)
            for b in range(B):
                nc.vector.scalar_tensor_tensor(out=fin[:, b, :], in0=h_s[:, b, :], scalar=st[:, 30 + b:31 + b], in1=gf_bc,
                                               op0=ALU.mult, op1=ALU.mult).then_inc(g_final, 1)

        @block.tensor
        def _(pe):
            def fill(name):
                n = FILLED[name] - 1
                if n >= 8:
                    prev, who = JOBS[n - 8]
                    pe.wait_ge(emptied[who], EMPTIED[prev])
                return bank(name)

            def done(ins):
                ins.then_inc(bank_filled, 1)

            pe.wait_ge(got_ident, 16)
            pe.wait_ge(got_gains, 16)
            t = fill("gains")
            n = gains.shape[0]
            done(nc.tensor.transpose(t[:, 0:n], graw[0:n, :], ident[0:n, 0:n]))

            def transposes(kind, src, count_sem, count):
                for j in range(4):
                    t = fill((kind, j))
                    for c in range(2):
                        k = 2 * j + c
                        for b in range(B):
                            if j == 0 and c == 0 and count_sem is not None:
                                pe.wait_ge(count_sem, count + b)
                            ins = nc.tensor.transpose(t[:, c * S + b * P:c * S + (b + 1) * P],
                                                      src[:, b, k * P:(k + 1) * P], ident[:])
                    done(ins)

            transposes("xT", xn_area, scaled, 1)

            n_unit = [0]

            def next_unit():
                u = n_unit[0]
                n_unit[0] += 1
                pe.wait_ge(lo_ready, u + 1)
                return unit_views(u)[1:]

            def three_passes(t, lhs, rhs, first, last):
                for n, (a, b) in enumerate(((0, 0), (0, 1), (1, 0))):
                    ins = nc.tensor.matmul(t, lhs[a], rhs[b], start=(first and n == 0), stop=(last and n == 2))
                return ins

            def project(name, cols):
                t = [fill((name, b)) for b in range(B)]
                for j in range(KC // 2):
                    hi, lo = next_unit()
                    for i in range(2):
                        k = 2 * j + i
                        for b in range(B):
                            s = slice(b * P, (b + 1) * P)
                            ins = three_passes(t[b][:, 0:cols], (xT_hi[:, k, s], xT_lo[:, k, s]),
                                               (hi[:, i, :], lo[:, i, :]), k == 0, k == KC - 1)
                            if k == KC - 1:
                                done(ins)
                    if j < KC // 2 - 1:
                        ins.then_inc(unit_used, 1)

            pe.wait_ge(dve_emptied, EMPTIED["xT", 3])
            project("A", A_W)
            project("IQ", 512)
            transposes("memT", mem_s, scaled, 3)
            project("Q", 512)
            pe.wait_ge(roped, 4)
            for j in range(2):
                t = fill(("iqT", j))
                for c in range(2):
                    for b in range(B):
                        ins = nc.tensor.transpose(t[:, c * S + b * P:c * S + (b + 1) * P],
                                                  iq_s[:, b, (2 * j + c) * P:(2 * j + c + 1) * P], ident[:])
                done(ins)
            t = fill("ikT")
            for b in range(B):
                ins = nc.tensor.transpose(t[:, b * P:(b + 1) * P], ik_s[:, b, :], ident[:])
            done(ins)
            pe.wait_ge(act_emptied, EMPTIED["ikT"])

            def causal_scores(t, qt, kt):
                nc.tensor.matmul(t[:, 0:P], qt[:, 0:P], kt[:, 0:P], start=True, stop=True)
                return nc.tensor.matmul(t[:, P:P + S], qt[:, P:S], kt[:, 0:S], start=True, stop=True)

            for h in range(IHEADS):
                t = fill(("idx", h))
                done(causal_scores(t, iqT[:, h // 2, :], ikT_odd if h % 2 else ikT))
            project("K", 512)
            project("V", 512)

            def project_T(t, w, col0, rhs, chunks):
                for c in range(chunks):
                    for k in range(KC):
                        ins = nc.tensor.matmul(t[:, c * S:(c + 1) * S], w[:, k, col0 + c * P:col0 + (c + 1) * P],
                                               rhs[:, k, :], start=(k == 0), stop=(k == KC - 1))
                return ins

            def chunk_T(t, last_of_job):
                hi, lo = next_unit()
                for k in range(KC):
                    ins = three_passes(t, (hi[:, k, :], lo[:, k, :]), (xT_hi[:, k, :], xT_lo[:, k, :]), k == 0,
                                       k == KC - 1)
                ins.then_inc(bank_filled if last_of_job else unit_used, 1)

            t = fill("qmT")
            for c in range(2):
                chunk_T(t[:, c * S:(c + 1) * S], c == 1)
            n = block_arrived(pe, "KV")
            pe.wait_ge(dve_emptied, EMPTIED["memT", 3])
            w = ring_block(n, 512)
            done(project_T(fill("kmT"), w, 0, memT, 2))
            t = fill("vm")
            for b in range(B):
                for k in range(KC):
                    ins = nc.tensor.matmul(t[:, b * 256:(b + 1) * 256], memT[:, k, b * P:(b + 1) * P], w[:, k, 256:512],
                                           start=(k == 0), stop=(k == KC - 1))
            done(ins)
            pe.wait_ge(got_const, 16 * N_CONST)
            for j in range(2):
                t = fill(("pool", j))
                for c in range(2):
                    g = 2 * j + c
                    for b in range(B):
                        ins = nc.tensor.matmul(t[0:HD, c * S:(c + 1) * S], u_s[:, b, g * HD:(g + 1) * HD],
                                               pool_a[:, b, g, :], start=(b == 0), stop=(b == B - 1))
                done(ins)
            t = fill("mix")
            pe.wait_ge(dve_emptied, EMPTIED["pool", 1])
            for g in range(G):
                lo = HD * (g % 2)
                ins = nc.tensor.matmul(t[lo:lo + HD, (g // 2) * S:(g // 2 + 1) * S], wg_s[:, g, :],
                                       pooledT[0:HD, g, :], start=True, stop=True)
            done(ins)
            for name, src_t, r in (("qT", q_s, 6), ("kT", k_s, 8)):
                pe.wait_ge(roped, r)
                for j in range(2):
                    t = fill((name, j))
                    for c in range(2):
                        for b in range(B):
                            ins = nc.tensor.transpose(t[:, c * S + b * P:c * S + (b + 1) * P],
                                                      src_t[:, b, (2 * j + c) * P:(2 * j + c + 1) * P], ident[:])
                    done(ins)

            def scores(n):
                t = fill(("sc", n))
                if n < MHEADS:
                    km = kmT_odd if n % 2 else kmT
                    for b in range(B):
                        ins = nc.tensor.matmul(t[:, b * M:(b + 1) * M], qmT[:, n // 2, b * P:(b + 1) * P],
                                               km[:, n // 2, :], start=True, stop=True)
                    done(ins)
                else:
                    m = n - MHEADS
                    done(causal_scores(t, qT[:, m // 2, :], (kT_odd if m % 2 else kT)[:, m // 2, :]))

            def turn_p(n):
                t = fill(("pT", n))
                pe.wait_ge(p_ready, n + 1)
                for s in range(2):
                    for b in range(B):
                        if n >= MHEADS and s > b:
                            continue
                        at = s * S + b * P if n < MHEADS or s == 0 else S
                        ins = nc.tensor.transpose(t[:, at:at + P], p_s[:, n % 2, b * S + s * P:b * S + (s + 1) * P],
                                                  ident[:])
                done(ins)

            def attend(n):
                t = fill(("o", n))
                pe.wait_ge(act_emptied, EMPTIED["pT", n])
                lo = HD * (n % 2)
                v = vm_s[:, :, n * HD:(n + 1) * HD] if n < MHEADS else v_s[:, :, (n - MHEADS) * HD:(n - MHEADS + 1) * HD]
                nc.tensor.matmul(t[lo:lo + HD, 0:S], v[:, 0, :], pT_s[:, n % 2, 0:S], start=True, stop=False)
                if n < MHEADS:
                    ins = nc.tensor.matmul(t[lo:lo + HD, 0:S], v[:, 1, :], pT_s[:, n % 2, S:2 * S], start=False,
                                           stop=True)
                else:
                    ins = nc.tensor.matmul(t[lo:lo + HD, P:S], v[:, 1, :], pT_s[:, n % 2, S:S + P], start=False,
                                           stop=True)
                done(ins)

            def gate(m):
                chunk_T(fill(("gate", m))[:, 0:S], True)

            nh = MHEADS + HEADS
            pe.wait_ge(act_emptied, EMPTIED["kT", 1])
            scores(0)
            for n in range(nh):
                gate(2 * n)
                turn_p(n)
                if n + 1 < nh:
                    scores(n + 1)
                gate(2 * n + 1)
                attend(n)

            na, np_ = block_arrived(pe, "PA"), FRONT.index("PPM")
            wa = ring_block(na, D)[:, 0:4, :]
            pe.wait_ge(got_block[np_ % RING_SLOTS], 16 * (np_ // RING_SLOTS + 2))
            wpm = ring[:, (np_ % RING_SLOTS) * RS:(np_ % RING_SLOTS + 1) * RS].rearrange("p (k n) -> p k n", n=D)
            pe.wait_ge(dve_emptied, EMPTIED["o", nh - 1])
            for f in range(KC):
                fc = slice(f * P, (f + 1) * P)
                for i, (w, y, ks) in enumerate(((wa, yT_area, range(4)), (wpm, yT_area, range(2)), (wpm, ymT, range(2)))):
                    t = fill(("br", f, i))
                    for k in ks:
                        ins = nc.tensor.matmul(t[:, 0:S], w[:, k + (2 if i == 2 else 0), fc],
                                               y[:, k + (4 if i == 1 else 0), :], start=(k == 0),
                                               stop=(k == len(ks) - 1))
                    done(ins)
            n0 = block_arrived(pe, "O0")
            n1 = block_arrived(pe, "O1")

            def project_out(b, hf):
                t = fill(("out", b, hf))
                w = ring_block(n1 if hf else n0, 512)
                for k in range(KC):
                    if b == 0 and hf == 0:
                        pe.wait_ge(merged_ready, k + 1)
                    ins = nc.tensor.matmul(t, merged[:, k, b * P:(b + 1) * P], w[:, k, :], start=(k == 0),
                                           stop=(k == KC - 1))
                done(ins)

            def turn_h(b, hf):
                t = fill(("x2T", b, hf))
                pe.wait_ge(scaled, 2 * B + 2 * b + hf + 1)
                for c in range(4):
                    k = 4 * hf + c
                    ins = nc.tensor.transpose(t[:, c * P:(c + 1) * P], xn2[:, b, k * P:(k + 1) * P], ident[:])
                done(ins)

            project_out(0, 0)
            project_out(0, 1)
            project_out(1, 0)
            turn_h(0, 0)
            turn_h(0, 1)
            project_out(1, 1)
            turn_h(1, 0)
            turn_h(1, 1)
            pe.wait_ge(got_late, 48)
            t = fill("logits")
            for b in range(B):
                pe.wait_ge(act_emptied, EMPTIED["x2T", b, 1])
                for k in range(KC):
                    ins = nc.tensor.matmul(t[:, b * NE:(b + 1) * NE], x2T[:, k, b * P:(b + 1) * P], wr_s[:, k, :],
                                           start=(k == 0), stop=(k == KC - 1))
            done(ins)
            t = fill("pos")
            pe.wait_ge(selected, 1)
            pe.wait_ge(ones_set, 1)
            nc.tensor.matmul(t[:, 0:NE], before[:], sel[:, 0, :], start=True, stop=True)
            nc.tensor.matmul(t[:, NE:2 * NE], ones[:], sel[:, 0, :], start=True, stop=False)
            nc.tensor.matmul(t[:, NE:2 * NE], before[:], sel[:, 1, :], start=False, stop=True)
            nc.tensor.matmul(t[:, 2 * NE:3 * NE], ones[:], sel[:, 0, :], start=True, stop=False)
            done(nc.tensor.matmul(t[:, 2 * NE:3 * NE], ones[:], sel[:, 1, :], start=False, stop=True))
            def gather(n):
                pe.wait_ge(slots_ready, n + 1)
                for k in range(KC):
                    for b in range(B):
                        ins = nc.tensor.matmul(psum[:, 2, k * SLOTS:(k + 1) * SLOTS], xn2[:, b, k * P:(k + 1) * P],
                                               sel_slot[:, b, :], start=(b == 0), stop=(b == B - 1))
                ins.then_inc(gathered, 1)

            def put_back(n):
                pe.wait_ge(y_ready, n + 1)
                pe.wait_ge(putT_ready, n + 1)
                for j in range(4):
                    b, hf = j // 2, j % 2
                    pe.wait_ge(added, 4 * n + j + 1)
                    nc.tensor.matmul(psum[:, 4 + 3 * (j % 2), :], putT[:, b, :], y_s[:, hf * 512:hf * 512 + 512],
                                     start=True, stop=True).then_inc(put_done, 1)

            pe.wait_ge(dve_emptied, EMPTIED["pos"])
            pe.wait_ge(act_emptied, EMPTIED["x2T", 1, 1])
            gather(0)
            pe.wait_ge(parts_ready, 1)
            pe.wait_ge(route_done, 1)
            rounds = rounds_of(pe)
            with pe.Fori(0, rounds) as r:
                with pe.Fori(0, NE) as e:
                    i = r * NE + e
                    pe.wait_ge(xe_ready, i + 1)
                    tiles = ((0, 0), (SLOTS, 512))
                    for k in range(UP_CHUNKS):
                        if k == 2:
                            put_back(i)
                        pe.wait_ge(got_up[k], 16 * (i + 1))
                        for c in range(2):
                            for lo, col in tiles:
                                at = k * UP_W + col + FE * c
                                ins = nc.tensor.matmul(psum[lo:lo + SLOTS, c, :], xeT[:, k, :], ring[:, at:at + 512],
                                                       start=(k == 0), stop=False)
                        ins.then_inc(up_used, 1)
                    pe.wait_ge(put_ready, i + 1)
                    for c in range(2):
                        for lo, col in tiles:
                            ins = nc.tensor.matmul(psum[lo:lo + SLOTS, c, :], hot[0:96, :],
                                                   b_part[0:96, col + FE * c:col + FE * c + 512], start=False, stop=True)
                    ins.then_inc(up_done, 1)
                    gather(i + 1)
                    for b in range(B):
                        ins = nc.tensor.transpose(psum[:, 3, b * P:(b + 1) * P], put[:, b, :], ident[:])
                    ins.then_inc(put_turned, 1)
                    pe.wait_ge(xe_ready, i + 2)
                    pe.wait_ge(act_ready, i + 1)
                    for q in range(KC // 2):
                        ins = nc.tensor.transpose(psum[:, 2, q * P:(q + 1) * P], act_s[:, q * P:(q + 1) * P], ident[:])
                    ins.then_inc(act_turned, 1)
                    pe.wait_ge(actT_ready, i + 1)
                    for j in range(DOWN_SLOTS):
                        pe.wait_ge(got_down[j], 16 * (i + 1))
                        for c in range(2):
                            for t_ in range(2):
                                at = DOWN0 + j * DOWN_W + t_ * D + 512 * c
                                f = 2 * j + t_
                                lhsT = actT[:, f % 4, (f // 4) * SLOTS:(f // 4 + 1) * SLOTS]
                                ins = nc.tensor.matmul(psum[t_ * SLOTS:(t_ + 1) * SLOTS, 5 + c, :], lhsT,
                                                       ring[:, at:at + 512], start=(j == 0),
                                                       stop=(j == DOWN_SLOTS - 1 and t_ == 1))
                        ins.then_inc(down_used, 1)
                    for c in range(2):
                        at = UP_W + 512 * c
                        ins = nc.tensor.matmul(psum[0:SLOTS, 5 + c, :], hot[0:96, :], b_part[0:96, at:at + 512],
                                               start=False, stop=True)
                    ins.then_inc(down_done, 1)
            put_back(NE * rounds)


def shape_constants():
    import numpy as np
    f = np.float32
    iota = np.tile(np.arange(SLOTS, dtype=f), (P, P // SLOTS))
    before = np.triu(np.ones((P, P), f), 1)
    causal = np.where(np.arange(P)[None, :] <= np.arange(P)[:, None], f(0), f(-BIG)).astype(f)
    inv = np.power(f(500000.0), -np.arange(HALF, dtype=f) / f(HALF)).astype(f)
    ang = np.arange(S, dtype=f)[:, None] * inv[None, :]
    cos, sin = np.cos(ang).astype(f), np.sin(ang).astype(f)
    rope = np.concatenate([cos, cos, -sin, sin], axis=1)
    t = np.arange(S)
    pool = np.zeros((S, G, S), f)
    for g, w in enumerate((2, 4, 8, 16)):
        lo = np.maximum(t + 1 - w, 0)
        inside = (t[:, None] >= lo[None, :]) & (t[:, None] <= t[None, :])
        pool[:, g, :] = inside / (t + 1 - lo)[None, :] - (t[:, None] == t[None, :])
    expert = np.tile(np.eye(NE, dtype=f), (3, 1))
    return {"ident": np.eye(P, dtype=f), "iota": iota, "before": before, "causal": causal, "rope": rope,
            "pool": pool, "expert": expert}


_INS = ["x", "mem", "w_in", "w_gate", "w_proj_attn", "w_proj_pool", "w_proj_mem", "gains", "pool_w_group", "w_mem_kv",
        "w_out", "norm_ffn_g", "w_router", "b_router", "w_up", "b_up", "w_down", "b_down", "norm_final_g",
        "c_ident", "c_iota", "c_before", "c_causal", "c_rope", "c_pool", "c_expert"]


def kernel(**inputs):
    import numpy as np
    import concourse.bacc as bacc
    from concourse.bass_utils import run_bass_kernel_spmd

    nc = bacc.Bacc("TRN2", target_bir_lowering=False, num_devices=1)
    data = {k: np.ascontiguousarray(v) for k, v in inputs.items()}
    data["gains"] = np.concatenate([data[k].reshape(-1, P) for k in
                                    ("norm_mix_g", "mem_norm_g", "pool_scale", "b_gate")])
    data["norm_final_g"] = data["norm_final_g"].reshape(1, D)
    for k, v in shape_constants().items():
        data["c_" + k] = v
    arrays, args = {}, []
    for name in _INS:
        a = data[name]
        arrays[f"in_{name}"] = a
        args.append(nc.dram_tensor(f"in_{name}", a.shape, mybir.dt.from_np(a.dtype), kind="ExternalInput").ap())
    args.append(nc.dram_tensor("out_0", (1, S, D), F32, kind="ExternalOutput").ap())
    hybrid_layer_kernel(nc, *args)
    r = run_bass_kernel_spmd(nc, [arrays], core_ids=[0])
    return r.results[0]["out_0"]
```

```python
from contextlib import ExitStack

import concourse.bass as bass
from concourse import mybir

F32 = mybir.dt.float32
BF16 = mybir.dt.bfloat16
F32R = mybir.dt.float32r
I32 = mybir.dt.int32
ALU = mybir.AluOpType
ACT = mybir.ActivationFunctionType
AX = mybir.AxisListType

P = 128
S = 256
B = S // P
D = 1024
KC = D // P
M = 256
HEADS = 8
IHEADS = 8
MHEADS = 4
HD = 64
ROPE = 16
HALF = ROPE // 2
TOPK = S // 4
G = 4
NE = 32
TOP = 4
FE = 1024
EPS = 1e-6
ALPHA = 1.702
LIMIT = 7.0
SLOTS = 64
MAX_ROUNDS = S // SLOTS
BIG = 3.0e38
TAKEN = -3.4e38
UNSEL = -1.0e30

C_Q, C_K, C_V, C_IQ, C_IK, C_IW, C_U, C_QM = 0, 512, 1024, 1536, 2048, 2112, 2120, 2376
IN_W = 2632
A_W = C_QM - C_IK

GB = 2 * KC + 2
N_CONST = 8

RING_SLOTS = 4
RS = 4096
FRONT = ["A", "IQ", "Q", "K", "V", "QM", "KV", "G0", "G1", "G2", "G3", "G4", "G5", "PA", "PPM", "O0", "O1"]
UP_W = 2 * FE
UP_CHUNKS = D // P
DOWN_W = 2 * D
DOWN_SLOTS = FE // P // 2
DOWN0 = UP_CHUNKS * UP_W
RING_W = DOWN0 + DOWN_SLOTS * DOWN_W

PIECES = UP_CHUNKS + DOWN_SLOTS
WSLOTS = 19
GROUP = 8
SLOT_OF = [n % (WSLOTS - 1) + 1 for n in range(5 * (WSLOTS - 1))]
for _n in (0, 19, 37, 54, 69, 83):
    SLOT_OF.insert(_n, 0)
USES = [SLOT_OF.count(s) for s in range(WSLOTS)]
USE_OF = [SLOT_OF[:m].count(s) for m, s in enumerate(SLOT_OF)]
PIECE_BEFORE = [max(n for n in range(-GROUP * PIECES, m) if SLOT_OF[n] == s) for m, s in enumerate(SLOT_OF)]
assert UP_W == DOWN_W and len(SLOT_OF) == GROUP * PIECES and NE % GROUP == 0 and SLOT_OF[:WSLOTS] == list(range(WSLOTS))

UNITS = [(name, "rows", j) for name in ("A", "IQ", "Q", "K", "V") for j in range(KC // 2)]
UNITS += [("QM", "cols", c) for c in range(2)]
UNITS += [(f"G{g}", "cols", c) for g in range(6) for c in range(4)]
UNITS += [("P", "cols", f) for f in range(D // P)]
assert FRONT.index("PPM") == FRONT.index("PA") + 1 and FRONT.index("PA") % RING_SLOTS < RING_SLOTS - 1
UNIT_SLOTS = 3
UNIT_W = 1024


def psum_jobs():
    jobs = [("gains", "dve")]
    jobs += [(("xT", j), "dve") for j in range(4)]
    jobs += [(("A", b), "dve") for b in range(B)]
    jobs += [(("IQ", b), "act") for b in range(B)]
    jobs += [(("memT", j), "dve") for j in range(4)]
    jobs += [(("iqT", j), "act") for j in range(2)] + [("ikT", "act")]
    jobs += [(("Q", b), "act") for b in range(B)]
    jobs += [(("idx", h), "act") for h in range(IHEADS)]
    jobs += [(("pool", j), "dve") for j in range(2)]
    jobs += [(("K", b), "act") for b in range(B)] + [("mix", "dve")]
    jobs += [(("V", b), "act") for b in range(B)]
    jobs += [("qmT", "act"), ("kmT", "act"), ("vm", "act")]
    jobs += [(("qT", j), "act") for j in range(2)] + [(("kT", j), "act") for j in range(2)]
    nh = MHEADS + HEADS
    jobs += [(("sc", 0), "act")]
    for n in range(nh):
        jobs += [(("gate", 2 * n), "act")]
        jobs += [(("pT", n), "act")]
        if n + 1 < nh:
            jobs += [(("sc", n + 1), "act" if n + 1 < MHEADS else "dve")]
        jobs += [(("gate", 2 * n + 1), "act"), (("o", n), "dve")]
    for f in range(KC):
        jobs += [(("br", f, i), "dve") for i in range(3)]
    jobs += [(("out", 0, 0), "dve"), (("out", 0, 1), "dve"), (("out", 1, 0), "dve")]
    jobs += [(("x2T", 0, 0), "act"), (("x2T", 0, 1), "act"), (("out", 1, 1), "dve")]
    jobs += [(("x2T", 1, 0), "act"), (("x2T", 1, 1), "act"), ("logits", "dve")]
    jobs += [("pos", "dve"), ("total", "dve")]
    return jobs


JOBS = psum_jobs()
FILLED = {name: n + 1 for n, (name, _) in enumerate(JOBS)}
BANK = {name: n % 8 for n, (name, _) in enumerate(JOBS)}
OWNER = dict(JOBS)
EMPTIED = {}
for _o in ("act", "dve"):
    for _n, _name in enumerate([j for j, o in JOBS if o == _o]):
        EMPTIED[_name] = _n + 1


LAST_USE = {"KV": FILLED["vm"]}
LAST_USE |= {b: FILLED["out", B - 1, 1] for b in ("O0", "O1")}
LAST_SPLIT = {name: n + 1 for n, (name, _, _) in enumerate(UNITS)}


def unit_read(u):
    name, kind, j = UNITS[u]
    if kind == "rows":
        if j < KC // 2 - 1:
            return "unit_used", sum(1 for _, k, i in UNITS[:u + 1] if k == "rows" and i < KC // 2 - 1)
        return "bank_filled", FILLED[name, 1]
    if name == "QM":
        return ("bank_filled", FILLED["qmT"]) if j == 1 else ("unit_used", 5 * (KC // 2 - 1) + 1)
    return "bank_filled", FILLED["br", j, 2] if name == "P" else FILLED["gate", 4 * int(name[1]) + j]


def hybrid_layer_kernel(nc, x, mem, w_in, w_gate, w_proj_attn, w_proj_pool, w_proj_mem, gains, pool_w_group,
                        w_mem_kv, w_out, norm_ffn_g, w_router, b_router, w_up, b_up, w_down, b_down,
                        norm_final_g, ident_c, iota_c, before_c, causal_c, rope_c, pool_c, expert_c, out):
    ctx = ExitStack()
    with ctx:
        def sb(name, shape, dt=F32):
            return ctx.enter_context(nc.sbuf_tensor(name, shape, dt))

        def sem(name):
            return ctx.enter_context(nc.semaphore(name))

        ring_at = nc.sbuf_base + (-nc.sbuf_base) % 32
        ring = sb("ring", [P, RING_W])
        unit_hi = nc.alloc_sbuf_tensor_at("unit_hi", [P, UNIT_SLOTS, UNIT_W], F32R, offset=ring_at + 4 * DOWN0)
        unit_lo = nc.alloc_sbuf_tensor_at("unit_lo", [P, UNIT_SLOTS, UNIT_W], F32R,
                                          offset=ring_at + 4 * (DOWN0 + UNIT_SLOTS * UNIT_W))
        xT_lo = nc.alloc_sbuf_tensor_at("xT_lo", [P, KC, S], F32R, offset=ring_at + 4 * (DOWN0 + 2 * UNIT_SLOTS * UNIT_W))
        h_s = sb("h_s", [P, B, D])
        xn_at = nc.sbuf_base + (-nc.sbuf_base) % 32
        xn_area = sb("xn_area", [P, B, D])
        xn_parts = nc.alloc_sbuf_tensor_at("xn_parts", [P, 8, S], F32R, offset=xn_at)
        mem_at = nc.sbuf_base + (-nc.sbuf_base) % 32
        mem_s = sb("mem_s", [P, B, D])
        mem_parts = nc.alloc_sbuf_tensor_at("mem_parts", [P, 2, S], F32R, offset=mem_at)
        xT_at = nc.sbuf_base + (-nc.sbuf_base) % 32
        xT_area = sb("xT_area", [P, KC * S])
        xT_hi = nc.alloc_sbuf_tensor_at("xT_hi", [P, KC, S], F32R, offset=xT_at)
        memT_at = nc.sbuf_base + (-nc.sbuf_base) % 32
        memT = sb("memT", [P, KC, M])
        memT_parts = nc.alloc_sbuf_tensor_at("memT_parts", [P, 8, S], F32R, offset=memT_at)
        gate_area = sb("gate_area", [P, 3 * KC, S])
        qk_area = sb("qk_area", [P, 2 * HEADS // 2 * S])
        vp_area = sb("vp_area", [P, 2 * HEADS * HD + 2 * B * S])
        yT_at = nc.sbuf_base + (-nc.sbuf_base) % 32
        yl_area = sb("yl_area", [P, 6 * S + 2 * (P + S)])
        yT_parts = nc.alloc_sbuf_tensor_at("yT_parts", [P, 4, S], F32R, offset=yT_at)
        ib_area = sb("ib_area", [P, S + 2 * (P + S)])
        misc = sb("misc", [P, 1536])
        pT_s = sb("pT_s", [P, 2, 2 * S])
        wg_s = sb("wg_s", [HD, G, HD])
        br_s = sb("br_s", [P, B, NE])
        ident = sb("ident", [P, P])
        iota = sb("iota", [P, P])
        before = sb("before", [P, P])
        ones = sb("ones", [P, P])
        causal = sb("causal", [P, P])
        rope = sb("rope", [P, B, 2 * ROPE])
        rope_t = sb("rope_t", [P, 2, 8, ROPE])
        graw = sb("graw", [64, P])
        gT = sb("gT", [P, 64])
        gate_b = sb("gate_b", [P, 3 * KC])
        expert_f = sb("expert_f", [96, NE])
        expert_b = sb("expert_b", [96, NE], BF16)
        st = sb("st", [P, 32])
        eps_s = sb("eps_s", [P, 1])
        warm = sb("warm", [P, 1])
        top8 = sb("top8", [P, 2, 8])
        sm = sb("sm", [P, 2, 8])
        rt = sb("rt", [P, B, 36])
        rt_m = sb("rt_m", [P, B, 36])
        rt8 = sb("rt8", [P, B, 8])
        sel = sb("sel", [P, B, NE])
        gex = sb("gex", [P, B, NE])
        gts = sb("gts", [P, B, NE])
        rsm = sb("rsm", [P, 8])
        posm = sb("posm", [P, B, NE + 1])
        rounds_i = sb("rounds_i", [1, 1], I32)

        def view(area, start, *dims):
            n = 1
            for d in dims:
                n *= d
            flat = area[:].rearrange("p a b -> p (a b)") if len(area.shape) == 3 else area[:]
            flat = flat[:, start:start + n]
            if len(dims) == 2:
                return flat.rearrange("p (a b) -> p a b", a=dims[0])
            if len(dims) == 3:
                return flat.rearrange("p (a b c) -> p a b c", a=dims[0], b=dims[1])
            return flat

        iq_s = view(gate_area, 0, B, 512)
        q_s = view(gate_area, 1024, B, 512)
        k_s = view(gate_area, 2048, B, 512)
        iqT = view(gate_area, 3072, 4, S)
        pool_a = view(gate_area, 4096, B, G, S)
        gates = gate_area
        qmT = view(xn_area, 0, 2, S)
        kmT = view(xn_area, 512, 2, M)
        vm_s = view(xn_area, 1024, B, MHEADS * HD)
        xn2 = xn_area
        qT = view(qk_area, 0, HEADS // 2, S)
        kT = view(qk_area, HEADS // 2 * S, HEADS // 2, S)
        v_s = view(vp_area, 0, B, HEADS * HD)
        p_s = view(vp_area, B * HEADS * HD, 2, B * S)
        y_pool = view(yl_area, 4 * S, 2, S)
        lg_s = view(yl_area, 6 * S, 2, P + S)
        ikT = view(ib_area, 0, S)
        idx = view(ib_area, S, P + S)
        bias = view(ib_area, P + 2 * S, P + S)
        y_parts = {"attn": (yT_parts[:, :, :], xn_parts[:, 0:4, :]),
                   "pool": (xn_parts[:, 4:6, :], mem_parts[:, :, :]),
                   "mem": (xn_parts[:, 6:8, :], memT_parts[:, 6:8, :])}
        merged = view(xT_area, 0, KC, S)
        u_s = view(misc, 0, B, G * HD)
        ik_s = view(misc, 512, B, 2 * HD)
        iw_s = view(misc, 768, B, IHEADS)
        pooledT = view(pT_s, 0, G, S)
        relu_s = lg_s
        mix_t = view(yl_area, 6 * S, 3, S)
        kT_odd = view(memT, 0, HEADS // 2, S)
        kmT_odd = view(memT, HEADS // 2 * S, MHEADS // 2, M)
        ikT_odd = view(pT_s, 0, S)
        x2T = memT
        b_up_s = view(mem_s, 0, UP_W)
        b_down_s = view(gate_area, 2048, D)
        b_mid = view(ib_area, S, 256).bitcast(BF16)
        b_part = misc[:, :].bitcast(BF16)
        wr_s = view(yl_area, UP_W, KC, NE)
        gf_bc = view(ib_area, 0, D)
        g2_bc = view(vp_area, 0, D)
        glu = view(gate_area, 0, FE // 2)
        lin = view(gate_area, 512, FE // 2)
        sig = view(gate_area, 1024, FE // 2)
        act_s = view(gate_area, 1536, FE // 2)
        xeT = view(gate_area, 2048, KC, SLOTS)
        actT = view(gate_area, 2560, KC // 2, P)
        sel_slot = view(gate_area, 3072, B, SLOTS)
        put = view(gate_area, 3200, B, P)
        putT = view(gate_area, 3456, B, P)
        hot = view(gate_area, 3712, SLOTS // 2).bitcast(BF16)
        wslot = [ring[:, n * UP_W:(n + 1) * UP_W] for n in range(PIECES)]
        wslot += [xT_area[:, :], view(mem_s, 0, UP_W), view(gate_area, 4096, UP_W), view(memT, 0, UP_W)]
        wslot += [view(area, 0, UP_W) for area in (qk_area, vp_area, yl_area)]
        y_s = view(pT_s, 0, D)
        fin = mem_s

        psum = ctx.enter_context(nc.psum_tensor("psum", [P, 8, 512], F32))

        got_x = [sem(f"got_x{b}") for b in range(B)]
        got_mem = sem("got_mem")
        got_gains = sem("got_gains")
        got_ident = sem("got_ident")
        got_rope = sem("got_rope")
        got_const = sem("got_const")
        got_late = sem("got_late")
        got_router = sem("got_router")
        got_bup = sem("got_bup")
        got_bdown = sem("got_bdown")
        got_block = [sem(f"got_block{i}") for i in range(RING_SLOTS)]
        got_piece = [sem(f"got_piece{i}") for i in range(WSLOTS)]
        bank_filled = sem("bank_filled")
        act_emptied = sem("act_emptied")
        dve_emptied = sem("dve_emptied")
        emptied = {"act": act_emptied, "dve": dve_emptied}
        ones_set = sem("ones_set")
        zeros_set = sem("zeros_set")
        hi_ready = sem("hi_ready")
        lo_ready = sem("lo_ready")
        unit_used = sem("unit_used")
        xT_hi_ready = sem("xT_hi_ready")
        got_eps = sem("got_eps")
        inverse = sem("inverse")
        lin_ready = sem("lin_ready")
        squares = sem("squares")
        scaled = sem("scaled")
        roped = sem("roped")
        relu_used = sem("relu_used")
        max_ready = sem("max_ready")
        exp_ready = sem("exp_ready")
        p_ready = sem("p_ready")
        merged_ready = sem("merged_ready")
        parts_ready = sem("parts_ready")
        route_max = sem("route_max")
        route_exp = sem("route_exp")
        selected = sem("selected")
        weighted = sem("weighted")
        last_squares = sem("last_squares")
        g_final = sem("g_final")
        route_done = sem("route_done")
        dve_own = sem("dve_own")
        act_own = sem("act_own")
        slots_ready = sem("slots_ready")
        put_ready = sem("put_ready")
        gathered = sem("gathered")
        xe_ready = sem("xe_ready")
        put_turned = sem("put_turned")
        putT_ready = sem("putT_ready")
        up_done = sem("up_done")
        piece_used = sem("piece_used")
        glu_ready = sem("glu_ready")
        sig_ready = sem("sig_ready")
        act_ready = sem("act_ready")
        act_turned = sem("act_turned")
        actT_ready = sem("actT_ready")
        y_ready = sem("y_ready")
        put_done = sem("put_done")
        added = sem("added")
        stored = sem("stored")

        block = ctx.enter_context(nc.Block())

        def ring_block(n, cols):
            s = (n % RING_SLOTS) * RS
            return ring[:, s:s + KC * cols].rearrange("p (k n) -> p k n", n=cols)

        def rows(w):
            return w.rearrange("(k p) n -> p k n", p=P)

        def unit_views(u):
            name, kind, j = UNITS[u]
            cols = {"A": A_W, "QM": 256, "P": D}.get(name, 512)
            w = ring_block(FRONT.index("PA" if name == "P" else name), cols)
            src = w[:, 2 * j:2 * j + 2, :] if kind == "rows" else w[:, :, j * P:(j + 1) * P]
            k, n = src.shape[1], src.shape[2]
            hi, lo = (t[:, u % UNIT_SLOTS, 0:k * n].rearrange("p (k n) -> p k n", n=n) for t in (unit_hi, unit_lo))
            return src, hi, lo

        def block_arrived(eng, name):
            n = FRONT.index(name)
            eng.wait_ge(got_block[n % RING_SLOTS], 16 * (n // RING_SLOTS + 1))
            return n

        def both_arrived(eng):
            block_arrived(eng, "PA")
            n = FRONT.index("PPM")
            eng.wait_ge(got_block[n % RING_SLOTS], 16 * (n // RING_SLOTS + 2))

        def bank(name):
            return psum[:, BANK[name], :]

        def rounds_of(eng):
            return nc.values_load(rounds_i[0:1, 0:1], engines=[eng.engine], min_val=1, max_val=MAX_ROUNDS)

        @block.sync
        def _(sp):
            for b in range(B):
                sp.dma_start(h_s[:, b, :], x[0, b * P:(b + 1) * P, :]).then_inc(got_x[b], 16)
            win = rows(w_in[0])
            wgt = rows(w_gate[0])
            src = {"A": [(win[:, :, C_IK:C_QM], 0)], "IQ": [(win[:, :, C_IQ:C_IK], 0)], "Q": [(win[:, :, C_Q:C_K], 0)],
                   "K": [(win[:, :, C_K:C_V], 0)], "V": [(win[:, :, C_V:C_IQ], 0)], "QM": [(win[:, :, C_QM:IN_W], 0)],
                   "KV": [(rows(w_mem_kv[0]), 0)], "PA": [(rows(w_proj_attn[0]), 0)],
                   "PPM": [(rows(w_proj_pool[0]), 0), (rows(w_proj_mem[0]), 2048)],
                   "O0": [(rows(w_out[0])[:, :, 0:512], 0)], "O1": [(rows(w_out[0])[:, :, 512:1024], 0)]}
            for g in range(6):
                src[f"G{g}"] = [(wgt[:, :, 512 * g:512 * (g + 1)], 0)]
            for n, name in enumerate(FRONT):
                if n >= RING_SLOTS:
                    before_it = FRONT[n - RING_SLOTS]
                    if before_it in LAST_SPLIT:
                        sp.wait_ge(lo_ready, LAST_SPLIT[before_it])
                    else:
                        sp.wait_ge(bank_filled, LAST_USE[before_it])
                for ap, at in src[name]:
                    k, cols = ap.shape[1], ap.shape[2]
                    s = (n % RING_SLOTS) * RS + at
                    dst = ring[:, s:s + k * cols].rearrange("p (k n) -> p k n", n=cols)
                    sp.dma_start(dst, ap).then_inc(got_block[n % RING_SLOTS], 16)
                if name == "A":
                    sp.dma_start(mem_s[:], mem.rearrange("a (b p) d -> p (a b) d", p=P)).then_inc(got_mem, 16)

            def load(e, n, slot):
                if n < UP_CHUNKS:
                    src_w, dst = w_up[0][bass.ds(e, 1), n * P:(n + 1) * P, :].rearrange("a p n -> (a p) n"), wslot[slot]
                else:
                    j = 2 * (n - UP_CHUNKS)
                    src_w = w_down[0][bass.ds(e, 1), j * P:(j + 2) * P, :].rearrange("a (t p) n -> p (a t) n", p=P)
                    dst = wslot[slot].rearrange("p (t n) -> p t n", t=2)
                sp.dma_start(dst, src_w).then_inc(got_piece[slot], 16)

            last = {n % RING_SLOTS: name for n, name in enumerate(FRONT)}

            def load_over(name):
                for q in range(UP_CHUNKS):
                    if last[q // 2] == name:
                        load(0, q, q)

            sp.wait_ge(bank_filled, FILLED["gate", 3 * KC - 1])
            load(0, 11, 11)
            sp.wait_ge(bank_filled, FILLED["o", MHEADS + HEADS - 1])
            load(1, 4, 16)
            sp.wait_ge(lo_ready, LAST_SPLIT["P"])
            load_over("PA")
            load_over("PPM")
            sp.wait_ge(bank_filled, FILLED["br", KC - 1, 2])
            for q in range(8, 11):
                load(0, q, q)
            load(1, 1, 13)
            sp.wait_ge(merged_ready, KC)
            load(1, 2, 14)
            load(1, 6, 18)
            for name in ("O0", "O1"):
                sp.wait_ge(bank_filled, LAST_USE[name])
                load_over(name)
            load(1, 0, 12)
            sp.wait_ge(scaled, 4 * B)
            load(1, 5, 17)
            sp.wait_ge(bank_filled, FILLED["logits"])
            load(1, 3, 15)

            def load_group(g, first):
                e0, n_group = g
                for m in range(first, GROUP * PIECES):
                    sp.wait_ge(piece_used, n_group * (GROUP * PIECES) + PIECE_BEFORE[m] + 1)
                    load(e0 + m // PIECES, m % PIECES, SLOT_OF[m])

            load_group((0, 0), WSLOTS)
            with sp.Fori(1, NE // GROUP) as g:
                load_group((g * GROUP, g), 0)
            sp.wait_ge(route_done, 1)
            rounds = rounds_of(sp)
            with sp.If(rounds > 1):
                with sp.Fori(1, rounds) as r:
                    with sp.Fori(0, NE // GROUP) as g:
                        load_group((g * GROUP, r * (NE // GROUP) + g), 0)
            for n in range(2 * B):
                b, cols = n // 2, slice(n % 2 * 512, n % 2 * 512 + 512)
                sp.wait_ge(g_final, n + 1)
                sp.dma_start(out[0, b * P:(b + 1) * P, cols], fin[:, b, cols]).then_inc(stored, 16)
            sp.wait_ge(stored, 16 * 2 * B)

        @block.gpsimd
        def _(pool):
            nc.gpsimd.memset(ones[:], 1.0).then_inc(ones_set, 1)
            for u in range(len(UNITS)):
                src, hi, lo = unit_views(u)
                pool.wait_ge(hi_ready, u + 1)
                nc.gpsimd.tensor_tensor(lo, src, hi.bitcast(F32), ALU.subtract).then_inc(lo_ready, 1)

        @block.scalar
        def _(act):
            own = [0]

            def link(ins):
                own[0] += 1
                ins.then_inc(act_own, 1)
                act.wait_ge(act_own, own[0])

            act.dma_start(ident[:], ident_c).then_inc(got_ident, 16)
            act.dma_start(graw[0:gains.shape[0], :], gains).then_inc(got_gains, 16)
            def squares_of(src, at, b):
                return nc.scalar.activation(view(gate_area, 2048 + 1024 * b, D), src[:, b, :], ACT.Square,
                                            accum_out=st[:, at + b:at + b + 1])

            def root(at):
                nc.scalar.activation(st[:, at + 4:at + 6], st[:, at:at + 2], ACT.Sqrt, bias=eps_s[:, 0:1],
                                     scale=1.0 / D).then_inc(squares, 1)

            def split(u):
                if u >= UNIT_SLOTS:
                    which, value = unit_read(u - UNIT_SLOTS)
                    act.wait_ge({"unit_used": unit_used, "bank_filled": bank_filled}[which], value)
                if u == 0 or UNITS[u][0] != UNITS[u - 1][0]:
                    if UNITS[u][0] == "P":
                        both_arrived(act)
                    else:
                        block_arrived(act, UNITS[u][0])
                src, hi, _ = unit_views(u)
                nc.scalar.activation(hi, src, ACT.Copy).then_inc(hi_ready, 1)

            act.wait_ge(got_eps, 1)
            nc.scalar.activation(warm[:], eps_s[:], ACT.Sqrt)
            for b in range(B):
                act.wait_ge(got_x[b], 16)
                ins = squares_of(h_s, 0, b)
            link(ins)
            root(0)
            act.dma_start(rope[:], rope_c.rearrange("(b p) c -> p b c", p=P)).then_inc(got_rope, 16)
            consts = [(iota[:], iota_c), (before[:], before_c), (causal[:], causal_c), (expert_f[:], expert_c),
                      (pool_a, pool_c.rearrange("(b p) g t -> p b g t", p=P)),
                      (wg_s[:], pool_w_group[0].rearrange("g c d -> c g d")),
                      (br_s[:, 0, :], b_router.to_broadcast([P, NE])), (br_s[:, 1, :], b_router.to_broadcast([P, NE]))]
            for dst, s in consts:
                act.dma_start(dst, s).then_inc(got_const, 16)

            def empty(name):
                act.wait_ge(bank_filled, FILLED[name])
                return bank(name)

            act.wait_ge(dve_emptied, EMPTIED["gains"])
            for j in range(4):
                t = empty(("xT", j))
                for c in range(2):
                    k = 2 * j + c
                    ins = nc.scalar.activation(xT_hi[:, k, :], t[:, c * S:(c + 1) * S], ACT.Copy, scale=gT[:, k:k + 1])
                ins.then_inc(xT_hi_ready, 1)
                if j == 1:
                    split(0)
            for u in range(1, 4):
                split(u)
            split(4)
            act.wait_ge(got_mem, 16)
            squares_of(mem_s, 8, 0)
            link(squares_of(mem_s, 8, 1))
            root(8)
            for u in range(5, 11):
                split(u)

            def copy(name, dst, part=None):
                t = empty(name)
                src_ap = t if part is None else part(t)
                nc.scalar.activation(dst, src_ap, ACT.Copy).then_inc(act_emptied, 1)

            def pair(t):
                return t.rearrange("p (c s) -> p c s", c=2)

            def copy_halves(name, even, odd, part):
                t = empty(name)
                nc.scalar.activation(even[0:HD], part(t)[0:HD], ACT.Copy)
                nc.scalar.activation(odd[HD:P], part(t)[HD:P], ACT.Copy).then_inc(act_emptied, 1)

            for b in range(B):
                copy(("IQ", b), iq_s[:, b, :])
            split(11)
            for j in range(2):
                copy(("iqT", j), iqT[:, 2 * j:2 * j + 2, :], pair)
            act.wait_ge(zeros_set, 1)
            copy_halves("ikT", ikT[:, :], ikT_odd, lambda t: t[:, 0:S])
            for u in range(12, 15):
                split(u)
            for b in range(B):
                copy(("Q", b), q_s[:, b, :])
            for h in range(IHEADS):
                if h >= 2:
                    act.wait_ge(relu_used, h - 1)
                t = empty(("idx", h))
                nc.scalar.activation(relu_s[:, h % 2, :], t[:, 0:P + S], ACT.Relu, scale=HD ** -0.5)\
                  .then_inc(act_emptied, 1)
            nc.scalar.activation(warm[:], eps_s[:], ACT.Exp)
            for u in range(15, 19):
                split(u)
            for b in range(B):
                copy(("K", b), k_s[:, b, :])
            act.wait_ge(bank_filled, FILLED["memT", 3])
            for c in range(3):
                act.dma_start(b_up_s[32 * c:32 * c + 32, :], b_up[0]).then_inc(got_bup, 16)
            for u in range(19, 23):
                split(u)
            for b in range(B):
                copy(("V", b), v_s[:, b, :])
            split(23)
            split(24)
            copy("qmT", qmT, pair)
            act.wait_ge(bank_filled, FILLED["vm"])
            act.wait_ge(zeros_set, 2)
            copy_halves("kmT", kmT, kmT_odd, pair)
            copy("vm", vm_s, pair)
            for j in range(2):
                copy(("qT", j), qT[:, 2 * j:2 * j + 2, :], pair)
            act.wait_ge(zeros_set, 3)
            for j in range(2):
                copy_halves(("kT", j), kT[:, 2 * j:2 * j + 2, :], kT_odd[:, 2 * j:2 * j + 2, :], pair)

            link(nc.scalar.mul(gate_b[:], gT[:, GB:GB + 3 * KC], 0.5))

            def gate(m):
                t = empty(("gate", m))
                nc.scalar.activation(gates[:, m, :], t[:, 0:S], ACT.Tanh, bias=gate_b[:, m:m + 1], scale=0.5)\
                  .then_inc(act_emptied, 1)
                u = 22 + m + UNIT_SLOTS
                if u < len(UNITS):
                    split(u)

            def exps(n):
                act.wait_ge(max_ready, n + 1)
                if n >= 2:
                    act.wait_ge(bank_filled, FILLED["pT", n - 2])
                for b in range(B):
                    if n < MHEADS:
                        src_ap, w = bank(("sc", n))[:, b * M:(b + 1) * M], M
                    else:
                        src_ap, w = lg_s[:, n % 2, b * P:P + b * S], P * (b + 1)
                    ins = nc.scalar.activation(p_s[:, n % 2, b * S:b * S + w], src_ap, ACT.Exp,
                                               bias=sm[:, n % 2, b:b + 1], scale=HD ** -0.5,
                                               accum_out=sm[:, n % 2, 2 + b:3 + b])
                    if n < MHEADS and b == B - 1:
                        ins.then_inc(act_emptied, 1)
                        act.wait_ge(act_emptied, EMPTIED["sc", n])
                        nc.scalar.copy(sm[:, n % 2, 6:7], sm[:, n % 2, 2:3]).then_inc(exp_ready, 1)
                    elif b == B - 1:
                        ins.then_inc(exp_ready, 1)

            def copy_pT(n):
                t = empty(("pT", n))
                if n >= 2:
                    act.wait_ge(bank_filled, FILLED["o", n - 2])
                if n < MHEADS:
                    nc.scalar.activation(pT_s[:, n % 2, :], t, ACT.Copy).then_inc(act_emptied, 1)
                else:
                    nc.scalar.activation(pT_s[:, n % 2, 0:S + P], t[:, 0:S + P], ACT.Copy).then_inc(act_emptied, 1)

            nh = MHEADS + HEADS
            act.wait_ge(dve_emptied, EMPTIED["mix"])
            exps(0)
            for c in range(3):
                act.dma_start(b_down_s[32 * c:32 * c + 32, :], b_down[0]).then_inc(got_bdown, 16)
            for n in range(nh):
                gate(2 * n)
                copy_pT(n)
                if n + 1 < nh:
                    exps(n + 1)
                gate(2 * n + 1)
            act.wait_ge(bank_filled, FILLED["o", nh - 1])
            act.dma_start(gf_bc, norm_final_g.to_broadcast([P, D])).then_inc(got_late, 16)
            act.dma_start(g2_bc, norm_ffn_g.to_broadcast([P, D])).then_inc(got_late, 16)
            for u in range(22 + 3 * KC + UNIT_SLOTS, len(UNITS)):
                split(u)
            act.wait_ge(merged_ready, KC)
            act.dma_start(wr_s, rows(w_router[0])).then_inc(got_router, 16)

            nc.scalar.activation(warm[:], eps_s[:], ACT.Sqrt)
            act.wait_ge(dve_emptied, EMPTIED["out", 0, 1])
            squares_of(h_s, 16, 0)

            def copy_x2T(b, hf):
                t = empty(("x2T", b, hf))
                nc.scalar.activation(x2T[:, 4 * hf:4 * hf + 4, b * P:(b + 1) * P],
                                     t.rearrange("p (k s) -> p k s", k=4), ACT.Copy).then_inc(act_emptied, 1)

            copy_x2T(0, 0)
            copy_x2T(0, 1)
            act.wait_ge(dve_emptied, EMPTIED["out", 1, 1])
            link(squares_of(h_s, 16, 1))
            root(16)
            copy_x2T(1, 0)
            copy_x2T(1, 1)
            act.wait_ge(route_max, 1)
            for b in range(B):
                ins = nc.scalar.activation(gex[:, b, :], rt[:, b, TOP:], ACT.Exp, bias=rsm[:, b:b + 1])
            ins.then_inc(route_exp, 1)

            def take_gathered(i):
                act.wait_ge(gathered, i + 1)
                nc.scalar.activation(xeT, psum[:, 2, :].rearrange("p (k c) -> p k c", k=KC), ACT.Copy)\
                  .then_inc(xe_ready, 1)

            take_gathered(0)
            act.wait_ge(route_done, 1)
            rounds = rounds_of(act)
            with act.Fori(0, rounds) as r:
                with act.Fori(0, NE // GROUP) as g:
                    for u in range(GROUP):
                        e = g * GROUP + u
                        i = r * NE + e
                        act.wait_ge(glu_ready, i + 1)
                        nc.scalar.activation(sig, glu, ACT.Sigmoid, scale=ALPHA).then_inc(sig_ready, 1)
                        take_gathered(i + 1)
                        act.wait_ge(put_turned, i + 1)
                        nc.scalar.activation(putT, psum[:, 3, 0:B * P].rearrange("p (b c) -> p b c", b=B), ACT.Copy)\
                          .then_inc(putT_ready, 1)
                        act.wait_ge(act_turned, i + 1)
                        nc.scalar.activation(actT, psum[:, 2, :].rearrange("p (q c) -> p q c", c=P), ACT.Copy)\
                          .then_inc(actT_ready, 1)
                        act.wait_ge(piece_used, PIECES * (i + 1))
                        nc.scalar.activation(y_s, psum[:, 5:7, :].rearrange("p a n -> p (a n)"), ACT.Copy)\
                          .then_inc(y_ready, 1)

            nc.scalar.activation(warm[:], eps_s[:], ACT.Sqrt)
            for b in range(B):
                act.wait_ge(added, 2 + 4 * NE * rounds + 2 * (b + 1))
                squares_of(h_s, 24, b).then_inc(last_squares, 1)
                act.wait_ge(last_squares, b + 1)
                nc.scalar.activation(st[:, 28 + b:29 + b], st[:, 24 + b:25 + b], ACT.Sqrt, bias=eps_s[:, 0:1],
                                     scale=1.0 / D).then_inc(squares, 1)

        @block.vector
        def _(dve):
            own = [0]

            def link(ins):
                own[0] += 1
                ins.then_inc(dve_own, 1)
                dve.wait_ge(dve_own, own[0])

            nc.vector.memset(eps_s[:], EPS).then_inc(got_eps, 1)
            nc.vector.memset(ikT[HD:P, :], 0.0)
            nc.vector.memset(ikT_odd[0:HD, :], 0.0).then_inc(zeros_set, 1)

            def inverse_rms(at, count):
                dve.wait_ge(squares, count)
                nc.vector.reciprocal(st[:, at + 6:at + 8], st[:, at + 4:at + 6]).then_inc(inverse, 1)
                dve.wait_ge(inverse, count)

            def scale_rows(dst, src, at, count):
                inverse_rms(at, count)
                for b in range(B):
                    nc.vector.tensor_scalar(dst[:, b, :], src[:, b, :], st[:, at + 6 + b:at + 7 + b], None, ALU.mult)\
                      .then_inc(scaled, 1)

            def empty(name):
                dve.wait_ge(bank_filled, FILLED[name])
                return bank(name)

            t = empty("gains")
            nc.vector.tensor_copy(gT[:, 0:gains.shape[0]], t[:, 0:gains.shape[0]]).then_inc(dve_emptied, 1)
            scale_rows(xn_area, h_s, 0, 1)
            for j in range(4):
                t = empty(("xT", j))
                dve.wait_ge(xT_hi_ready, j + 1)
                for c in range(2):
                    k = 2 * j + c
                    ins = nc.vector.scalar_tensor_tensor(out=xT_lo[:, k, :], in0=t[:, c * S:(c + 1) * S],
                                                         scalar=gT[:, k:k + 1], in1=xT_hi[:, k, :].bitcast(F32),
                                                         op0=ALU.mult, op1=ALU.subtract)
                ins.then_inc(dve_emptied, 1)
            scale_rows(mem_s, mem_s, 8, 2)
            for b in range(B):
                t = empty(("A", b))
                o = C_U - C_IK
                nc.vector.tensor_copy(u_s[:, b, :], t[:, o:o + G * HD])
                nc.vector.tensor_copy(ik_s[:, b, 0:HD], t[:, 0:HD])
                nc.vector.tensor_copy(ik_s[:, b, HD:2 * HD], t[:, 0:HD])
                o = C_IW - C_IK
                nc.vector.tensor_scalar(iw_s[:, b, :], t[:, o:o + IHEADS], IHEADS ** -0.5, None, ALU.mult)\
                  .then_inc(dve_emptied, 1)
                dve.wait_ge(dve_emptied, EMPTIED["A", b])

            rotated = [0]

            def rotate(t, b, heads):
                v = t[:, b, :].rearrange("p (h d) -> p h d", h=heads)
                cc = rope[:, b:b + 1, 0:ROPE].to_broadcast([P, heads, ROPE])
                s1 = rope[:, b:b + 1, ROPE:ROPE + HALF].to_broadcast([P, heads, HALF])
                s2 = rope[:, b:b + 1, ROPE + HALF:2 * ROPE].to_broadcast([P, heads, HALF])
                c, s = rope_t[:, 0, 0:heads, :], rope_t[:, 1, 0:heads, :]
                nc.vector.tensor_tensor(c, v[:, :, 0:ROPE], cc, ALU.mult)
                nc.vector.tensor_tensor(s[:, :, 0:HALF], v[:, :, HALF:ROPE], s1, ALU.mult)
                link(nc.vector.tensor_tensor(s[:, :, HALF:ROPE], v[:, :, 0:HALF], s2, ALU.mult))
                nc.vector.tensor_tensor(v[:, :, 0:ROPE], c, s, ALU.add).then_inc(roped, 1)
                rotated[0] += 1
                dve.wait_ge(roped, rotated[0])

            dve.wait_ge(got_rope, 16)
            for b in range(B):
                rotate(ik_s, b, 2)
            for b in range(B):
                dve.wait_ge(act_emptied, EMPTIED["IQ", b])
                rotate(iq_s, b, HEADS)
            for j in range(4):
                t = empty(("memT", j))
                for c in range(2):
                    k = 2 * j + c
                    ins = nc.vector.tensor_scalar(memT[:, k, :], t[:, c * M:(c + 1) * M], gT[:, KC + k:KC + k + 1],
                                                  None, ALU.mult)
                ins.then_inc(dve_emptied, 1)
            for b in range(B):
                dve.wait_ge(act_emptied, EMPTIED["Q", b])
                rotate(q_s, b, HEADS)
            for h in range(IHEADS):
                dve.wait_ge(act_emptied, EMPTIED["idx", h])
                for b in range(B):
                    cols = slice(b * P, P + b * S)
                    if h == 0:
                        ins = nc.vector.tensor_scalar(idx[:, cols], relu_s[:, h % 2, cols], iw_s[:, b, h:h + 1], None,
                                                      ALU.mult)
                    else:
                        ins = nc.vector.scalar_tensor_tensor(out=idx[:, cols], in0=relu_s[:, h % 2, cols],
                                                             scalar=iw_s[:, b, h:h + 1], in1=idx[:, cols],
                                                             op0=ALU.mult, op1=ALU.add)
                ins.then_inc(relu_used, 1)
                dve.wait_ge(relu_used, h + 1)
            dve.wait_ge(got_const, 16 * N_CONST)
            nc.vector.tensor_tensor(idx[:, 0:P], idx[:, 0:P], causal[:], ALU.add)
            link(nc.vector.tensor_tensor(idx[:, 2 * P:3 * P], idx[:, 2 * P:3 * P], causal[:], ALU.add))

            def take_top(b, first, n):
                cols = slice(b * P, P + b * S)
                for _ in range(first, first + n):
                    link(nc.vector.max(out=top8[:, b, :], in_=idx[:, cols]))
                    link(nc.vector.match_replace(out=idx[:, cols], in_to_replace=top8[:, b, :], in_values=idx[:, cols],
                                                 imm_value=TAKEN))
                if first + n == TOPK // 8:
                    link(nc.vector.tensor_scalar(bias[:, cols], idx[:, cols], (TAKEN - BIG) / 2, UNSEL, ALU.is_gt,
                                                 ALU.mult))
                    d = slice(2 * b * P, (2 * b + 1) * P)
                    link(nc.vector.tensor_tensor(bias[:, d], bias[:, d], causal[:], ALU.add))

            for j in range(2):
                t = empty(("pool", j))
                nc.vector.tensor_copy(pooledT[0:HD, 2 * j:2 * j + 2, :],
                                      t[0:HD, :].rearrange("p (g s) -> p g s", g=2)).then_inc(dve_emptied, 1)
            take_top(0, 0, TOPK // 8)
            take_top(1, 0, TOPK // 8)
            t = empty("mix")
            for c in range(2):
                ins = nc.vector.tensor_scalar(y_pool[:, c, :], t[:, c * S:(c + 1) * S],
                                              gT[:, 2 * KC + c:2 * KC + c + 1], None, ALU.mult)
            ins.then_inc(dve_emptied, 1)

            for b in range(B):
                dve.wait_ge(act_emptied, EMPTIED["K", b])
                rotate(k_s, b, HEADS)
            nc.vector.memset(kT[HD:P], 0.0)
            nc.vector.memset(kmT[HD:P], 0.0)
            dve.wait_ge(bank_filled, FILLED["vm"])
            nc.vector.memset(kmT_odd[0:HD], 0.0).then_inc(zeros_set, 1)
            nc.vector.memset(kT_odd[0:HD], 0.0).then_inc(zeros_set, 1)

            def bias_parts(c):
                if c == 0:
                    dve.wait_ge(got_bdown, 48)
                if c == 2:
                    dve.wait_ge(got_bup, 48)
                rest = (b_down_s[0:96, 512 * c:512 * c + 512] if c < 2
                        else b_up_s[0:96, 512 * (c - 2):512 * (c - 2) + 512])
                at = UP_W + 512 * c if c < 2 else 512 * (c - 2)
                part, mid = b_part[:, at:at + 512], b_mid[0:96, :]
                link(nc.vector.tensor_copy(part[0:96, :], rest))
                link(nc.vector.tensor_tensor(rest, rest, part[0:96, :], ALU.subtract))
                link(nc.vector.tensor_copy(mid, rest))
                nc.vector.tensor_copy(part[32:64, :], mid[32:64, :])
                link(nc.vector.tensor_tensor(rest, rest, mid, ALU.subtract))
                link(nc.vector.tensor_copy(part[64:96, :], rest[64:96, :]))
                if c == 5:
                    nc.vector.tensor_copy(expert_b[:], expert_f[:]).then_inc(parts_ready, 1)

            def maxima(n):
                if n < MHEADS:
                    t = empty(("sc", n))
                    if n >= 2:
                        dve.wait_ge(p_ready, n - 1)
                    link(nc.vector.reduce_max(sm[:, n % 2, 4:6], t.rearrange("p (b s) -> p b s", b=B), AX.X))
                else:
                    t = empty(("sc", n))
                    dve.wait_ge(exp_ready, n - 1)
                    for b in range(B):
                        cols = slice(b * P, P + b * S)
                        ins = nc.vector.tensor_tensor(lg_s[:, n % 2, cols], t[:, cols], bias[:, cols], ALU.add)
                    ins.then_inc(dve_emptied, 1)
                    dve.wait_ge(dve_emptied, EMPTIED["sc", n])
                    for b in range(B):
                        cols = slice(b * P, P + b * S)
                        ins = nc.vector.reduce_max(sm[:, n % 2, 4 + b:5 + b], lg_s[:, n % 2, cols], AX.X)
                    link(ins)
                nc.vector.tensor_scalar(sm[:, n % 2, 0:2], sm[:, n % 2, 4:6], -HD ** -0.5, None, ALU.mult)\
                  .then_inc(max_ready, 1)

            def normalise(n):
                dve.wait_ge(exp_ready, n + 1)
                link(nc.vector.reciprocal(sm[:, n % 2, 4:6], sm[:, n % 2, 2:4]))
                for b in range(B):
                    w = M if n < MHEADS else P * (b + 1)
                    ins = nc.vector.tensor_scalar(p_s[:, n % 2, b * S:b * S + w], p_s[:, n % 2, b * S:b * S + w],
                                                  sm[:, n % 2, 4 + b:5 + b], None, ALU.mult)
                ins.then_inc(p_ready, 1)

            def take_o(n):
                t = empty(("o", n))
                part = slice(HD * (n % 2), HD * (n % 2 + 1))
                name, c = ("mem", n // 2) if n < MHEADS else ("attn", (n - MHEADS) // 2)
                hi, lo = (y[part, c, :] for y in y_parts[name])
                link(nc.vector.tensor_copy(hi, t[part, 0:S]))
                nc.vector.tensor_tensor(lo, t[part, 0:S], hi.bitcast(F32), ALU.subtract).then_inc(dve_emptied, 1)

            nh = MHEADS + HEADS
            maxima(0)
            normalise(0)
            for n in range(nh):
                if n + 1 < nh:
                    maxima(n + 1)
                    normalise(n + 1)
                take_o(n)
                if n < 6:
                    bias_parts(n)
                if n == 6:
                    hi, lo = y_parts["pool"]
                    link(nc.vector.tensor_copy(hi, y_pool))
                    link(nc.vector.tensor_tensor(lo, y_pool, hi.bitcast(F32), ALU.subtract))

            dve.wait_ge(act_emptied, EMPTIED["gate", 3 * KC - 1])
            for f in range(KC):
                for i in range(3):
                    t = empty(("br", f, i))
                    ins = nc.vector.scalar_tensor_tensor(out=mix_t[:, i, :], in0=gates[:, KC * i + f, :], scalar=1.0,
                                                         in1=t[:, 0:S], op0=ALU.add, op1=ALU.mult)
                    ins.then_inc(dve_emptied, 1)
                dve.wait_ge(dve_emptied, EMPTIED["br", f, 2])
                link(nc.vector.tensor_tensor(mix_t[:, 0, :], mix_t[:, 0, :], mix_t[:, 1, :], ALU.add))
                nc.vector.tensor_tensor(merged[:, f, :], mix_t[:, 0, :], mix_t[:, 2, :], ALU.add)\
                  .then_inc(merged_ready, 1)
                dve.wait_ge(merged_ready, f + 1)
            dve.wait_ge(got_late, 32)
            for b in range(B):
                for hf in range(2):
                    t = empty(("out", b, hf))
                    cols = slice(hf * 512, hf * 512 + 512)
                    nc.vector.scalar_tensor_tensor(out=h_s[:, b, cols], in0=t, scalar=0.5, in1=h_s[:, b, cols],
                                                   op0=ALU.mult, op1=ALU.add).then_inc(dve_emptied, 1)
                    dve.wait_ge(dve_emptied, EMPTIED["out", b, hf])
                    nc.vector.tensor_tensor(xn2[:, b, cols], h_s[:, b, cols], g2_bc[:, cols], ALU.mult)\
                      .then_inc(scaled, 1)
            nc.vector.memset(rt[:, :, 0:TOP], BIG)
            inverse_rms(16, 3)

            t = empty("logits")
            for b in range(B):
                ins = nc.vector.scalar_tensor_tensor(out=rt[:, b, TOP:], in0=t[:, b * NE:(b + 1) * NE],
                                                     scalar=st[:, 22 + b:23 + b], in1=br_s[:, b, :], op0=ALU.mult,
                                                     op1=ALU.add)
            ins.then_inc(dve_emptied, 1)
            dve.wait_ge(dve_emptied, EMPTIED["logits"])
            for b in range(B):
                ins = nc.vector.max(out=rt8[:, b, :], in_=rt[:, b, :])
            link(ins)
            nc.vector.tensor_scalar(rsm[:, 0:B], rt8[:, :, TOP:TOP + 1].rearrange("p b o -> p (b o)"), -1.0, None, ALU.mult)\
              .then_inc(route_max, 1)
            for b in range(B):
                ins = nc.vector.match_replace(out=rt_m[:, b, :], in_to_replace=rt8[:, b, :], in_values=rt[:, b, :],
                                              imm_value=TAKEN)
            link(ins)
            nc.vector.tensor_scalar(sel[:], rt_m[:, :, TOP:], (TAKEN - BIG) / 2, None, ALU.is_lt).then_inc(selected, 1)
            dve.wait_ge(selected, 1)
            dve.wait_ge(route_exp, 1)
            for b in range(B):
                ins = nc.vector.scalar_tensor_tensor(out=gex[:, b, :], in0=gex[:, b, :], scalar=1.0, in1=sel[:, b, :],
                                                     op0=ALU.mult, op1=ALU.mult, accum_out=rsm[:, 2 + b:3 + b])
            link(ins)
            link(nc.vector.reciprocal(rsm[:, 4:6], rsm[:, 2:4]))
            for b in range(B):
                ins = nc.vector.tensor_scalar(gts[:, b, :], gex[:, b, :], rsm[:, 4 + b:5 + b], None, ALU.mult)
            ins.then_inc(weighted, 1)

            def gather_columns(e, n):
                if n is not None:
                    dve.wait_ge(gathered, n)
                for b in range(B):
                    ins = nc.vector.tensor_scalar(sel_slot[:, b, :], iota[:, 0:SLOTS], posm[:, b, bass.ds(e, 1)],
                                                  st[:, 22 + b:23 + b], ALU.is_equal, ALU.mult)
                ins.then_inc(slots_ready, 1)

            t = empty("pos")
            pos = t[:, 0:B * NE].rearrange("p (b e) -> p b e", b=B)
            nc.vector.scalar_tensor_tensor(out=posm[:, :, 0:NE], in0=pos, scalar=1.0, in1=sel[:], op0=ALU.add,
                                           op1=ALU.mult).then_inc(dve_emptied, 1)
            dve.wait_ge(dve_emptied, EMPTIED["pos"])
            link(nc.vector.tensor_scalar(posm[:, :, 0:NE], posm[:, :, 0:NE], -1.0, None, ALU.add))
            gather_columns(0, None)
            nc.vector.tensor_scalar(rt8[:, 0, 0:MAX_ROUNDS], iota[:, 0:MAX_ROUNDS], float(SLOTS), None, ALU.mult)
            t = empty("total")
            nc.vector.reduce_max(rsm[:, 6:7], t[:, 0:NE], AX.X).then_inc(dve_emptied, 1)
            dve.wait_ge(dve_emptied, EMPTIED["total"])
            nc.vector.tensor_scalar(posm[:, :, NE:NE + 1], posm[:, :, 0:1], -float(SLOTS), None, ALU.add)
            link(nc.vector.tensor_scalar(rt8[:, 1, 0:MAX_ROUNDS], rt8[:, 0, 0:MAX_ROUNDS], rsm[:, 6:7], None,
                                         ALU.is_lt))
            link(nc.vector.reduce_sum(rsm[:, 7:8], rt8[:, 1, 0:MAX_ROUNDS], AX.X))
            nc.vector.tensor_copy(rounds_i[:, :], rsm[0:1, 7:8]).then_inc(route_done, 1)

            nc.vector.engine_nop().then_inc(added, 2)

            def take_back(n):
                for j in range(4):
                    b, hf = j // 2, j % 2
                    cols = slice(hf * 512, hf * 512 + 512)
                    dve.wait_ge(put_done, 4 * n + j + 1)
                    nc.vector.tensor_tensor(h_s[:, b, cols], psum[:, 4 + 3 * (j % 2), :], h_s[:, b, cols],
                                            ALU.add).then_inc(added, 1)

            nc.vector.memset(putT, 0.0).then_inc(putT_ready, 1)
            nc.vector.memset(y_s, 0.0).then_inc(y_ready, 1)
            dve.wait_ge(route_done, 1)
            rounds = rounds_of(dve)
            link_base = own[0]
            with dve.Fori(0, rounds) as r:
                with dve.Fori(0, NE // GROUP) as g:
                    for u in range(GROUP):
                        e = g * GROUP + u
                        i = r * NE + e
                        gather_columns(e + 1, i + 1)
                        take_back(i)
                        for b in range(B):
                            nc.vector.tensor_scalar(put[:, b, :], iota[:], posm[:, b, bass.ds(e, 1)],
                                                    gts[:, b, bass.ds(e, 1)], ALU.is_equal, ALU.mult)
                        nc.vector.tensor_copy(hot[0:96, :], expert_b[:, bass.ds(e, 1)].to_broadcast([96, SLOTS]))\
                          .then_inc(put_ready, 1)
                        dve.wait_ge(up_done, i + 1)
                        nc.vector.tensor_scalar(glu, psum[:, 0, :], LIMIT, None, ALU.min).then_inc(glu_ready, 1)
                        nc.vector.tensor_scalar(lin, psum[:, 1, :], LIMIT, -LIMIT, ALU.min, ALU.max).then_inc(lin_ready, 1)
                        dve.wait_ge(lin_ready, 2 * i + 1)
                        nc.vector.scalar_tensor_tensor(out=lin, in0=lin, scalar=1.0, in1=glu, op0=ALU.add, op1=ALU.mult)\
                          .then_inc(lin_ready, 1)
                        dve.wait_ge(sig_ready, i + 1)
                        dve.wait_ge(lin_ready, 2 * i + 2)
                        nc.vector.tensor_tensor(act_s, lin, sig, ALU.mult).then_inc(act_ready, 1)
                nc.vector.tensor_scalar(posm[:], posm[:], -float(SLOTS), None, ALU.add).then_inc(dve_own, 1)
                dve.wait_ge(dve_own, link_base + r + 1)
            take_back(NE * rounds)
            for b in range(B):
                dve.wait_ge(squares, 4 + b)
                nc.vector.reciprocal(st[:, 30 + b:31 + b], st[:, 28 + b:29 + b]).then_inc(inverse, 1)
                dve.wait_ge(inverse, 4 + b)
                dve.wait_ge(added, 2 + 4 * NE * rounds + 2 * (b + 1))
                for hf in range(2):
                    cols = slice(hf * 512, hf * 512 + 512)
                    nc.vector.scalar_tensor_tensor(out=fin[:, b, cols], in0=h_s[:, b, cols],
                                                   scalar=st[:, 30 + b:31 + b], in1=gf_bc[:, cols], op0=ALU.mult,
                                                   op1=ALU.mult).then_inc(g_final, 1)

        @block.tensor
        def _(pe):
            def fill(name):
                n = FILLED[name] - 1
                if n >= 8:
                    prev, who = JOBS[n - 8]
                    pe.wait_ge(emptied[who], EMPTIED[prev])
                return bank(name)

            def done(ins):
                ins.then_inc(bank_filled, 1)

            pe.wait_ge(got_ident, 16)
            pe.wait_ge(got_gains, 16)
            t = fill("gains")
            n = gains.shape[0]
            done(nc.tensor.transpose(t[:, 0:n], graw[0:n, :], ident[0:n, 0:n]))

            def transposes(kind, src, count_sem, count):
                for j in range(4):
                    t = fill((kind, j))
                    for c in range(2):
                        k = 2 * j + c
                        for b in range(B):
                            if j == 0 and c == 0 and count_sem is not None:
                                pe.wait_ge(count_sem, count + b)
                            ins = nc.tensor.transpose(t[:, c * S + b * P:c * S + (b + 1) * P],
                                                      src[:, b, k * P:(k + 1) * P], ident[:])
                    done(ins)

            transposes("xT", xn_area, scaled, 1)

            n_unit = [0]

            def next_unit():
                u = n_unit[0]
                n_unit[0] += 1
                pe.wait_ge(lo_ready, u + 1)
                return unit_views(u)[1:]

            def three_passes(t, lhs, rhs, first, last):
                for n, (a, b) in enumerate(((0, 0), (0, 1), (1, 0))):
                    ins = nc.tensor.matmul(t, lhs[a], rhs[b], start=(first and n == 0), stop=(last and n == 2))
                return ins

            def project(name, cols):
                t = [fill((name, b)) for b in range(B)]
                for j in range(KC // 2):
                    if name == "A":
                        pe.wait_ge(dve_emptied, EMPTIED["xT", j])
                    hi, lo = next_unit()
                    for i in range(2):
                        k = 2 * j + i
                        for b in range(B):
                            s = slice(b * P, (b + 1) * P)
                            ins = three_passes(t[b][:, 0:cols], (xT_hi[:, k, s], xT_lo[:, k, s]),
                                               (hi[:, i, :], lo[:, i, :]), k == 0, k == KC - 1)
                            if k == KC - 1:
                                done(ins)
                    if j < KC // 2 - 1:
                        ins.then_inc(unit_used, 1)

            project("A", A_W)
            project("IQ", 512)
            transposes("memT", mem_s, scaled, 3)
            pe.wait_ge(roped, 4)
            for j in range(2):
                t = fill(("iqT", j))
                for c in range(2):
                    for b in range(B):
                        ins = nc.tensor.transpose(t[:, c * S + b * P:c * S + (b + 1) * P],
                                                  iq_s[:, b, (2 * j + c) * P:(2 * j + c + 1) * P], ident[:])
                done(ins)
            t = fill("ikT")
            for b in range(B):
                ins = nc.tensor.transpose(t[:, b * P:(b + 1) * P], ik_s[:, b, :], ident[:])
            done(ins)
            project("Q", 512)
            pe.wait_ge(act_emptied, EMPTIED["ikT"])

            def causal_scores(t, qt, kt):
                nc.tensor.matmul(t[:, 0:P], qt[:, 0:P], kt[:, 0:P], start=True, stop=True)
                return nc.tensor.matmul(t[:, P:P + S], qt[:, P:S], kt[:, 0:S], start=True, stop=True)

            for h in range(IHEADS):
                t = fill(("idx", h))
                done(causal_scores(t, iqT[:, h // 2, :], ikT_odd if h % 2 else ikT))
            pe.wait_ge(got_const, 16 * N_CONST)
            for j in range(2):
                t = fill(("pool", j))
                for c in range(2):
                    g = 2 * j + c
                    for b in range(B):
                        ins = nc.tensor.matmul(t[0:HD, c * S:(c + 1) * S], u_s[:, b, g * HD:(g + 1) * HD],
                                               pool_a[:, b, g, :], start=(b == 0), stop=(b == B - 1))
                done(ins)
            project("K", 512)
            t = fill("mix")
            pe.wait_ge(dve_emptied, EMPTIED["pool", 1])
            for g in range(G):
                lo = HD * (g % 2)
                ins = nc.tensor.matmul(t[lo:lo + HD, (g // 2) * S:(g // 2 + 1) * S], wg_s[:, g, :],
                                       pooledT[0:HD, g, :], start=True, stop=True)
            done(ins)
            project("V", 512)

            def project_T(t, w, col0, rhs, chunks):
                for c in range(chunks):
                    for k in range(KC):
                        ins = nc.tensor.matmul(t[:, c * S:(c + 1) * S], w[:, k, col0 + c * P:col0 + (c + 1) * P],
                                               rhs[:, k, :], start=(k == 0), stop=(k == KC - 1))
                return ins

            def chunk_T(t, last_of_job):
                hi, lo = next_unit()
                for k in range(KC):
                    ins = three_passes(t, (hi[:, k, :], lo[:, k, :]), (xT_hi[:, k, :], xT_lo[:, k, :]), k == 0,
                                       k == KC - 1)
                ins.then_inc(bank_filled if last_of_job else unit_used, 1)

            t = fill("qmT")
            for c in range(2):
                chunk_T(t[:, c * S:(c + 1) * S], c == 1)
            n = block_arrived(pe, "KV")
            pe.wait_ge(dve_emptied, EMPTIED["memT", 3])
            w = ring_block(n, 512)
            done(project_T(fill("kmT"), w, 0, memT, 2))
            t = fill("vm")
            for b in range(B):
                for k in range(KC):
                    ins = nc.tensor.matmul(t[:, b * 256:(b + 1) * 256], memT[:, k, b * P:(b + 1) * P], w[:, k, 256:512],
                                           start=(k == 0), stop=(k == KC - 1))
            done(ins)
            for name, src_t, r in (("qT", q_s, 6), ("kT", k_s, 8)):
                pe.wait_ge(roped, r)
                for j in range(2):
                    t = fill((name, j))
                    for c in range(2):
                        for b in range(B):
                            ins = nc.tensor.transpose(t[:, c * S + b * P:c * S + (b + 1) * P],
                                                      src_t[:, b, (2 * j + c) * P:(2 * j + c + 1) * P], ident[:])
                    done(ins)

            def scores(n):
                t = fill(("sc", n))
                if n < MHEADS:
                    km = kmT_odd if n % 2 else kmT
                    for b in range(B):
                        ins = nc.tensor.matmul(t[:, b * M:(b + 1) * M], qmT[:, n // 2, b * P:(b + 1) * P],
                                               km[:, n // 2, :], start=True, stop=True)
                    done(ins)
                else:
                    m = n - MHEADS
                    done(causal_scores(t, qT[:, m // 2, :], (kT_odd if m % 2 else kT)[:, m // 2, :]))

            def turn_p(n):
                t = fill(("pT", n))
                pe.wait_ge(p_ready, n + 1)
                for s in range(2):
                    for b in range(B):
                        if n >= MHEADS and s > b:
                            continue
                        at = s * S + b * P if n < MHEADS or s == 0 else S
                        ins = nc.tensor.transpose(t[:, at:at + P], p_s[:, n % 2, b * S + s * P:b * S + (s + 1) * P],
                                                  ident[:])
                done(ins)

            def attend(n):
                t = fill(("o", n))
                pe.wait_ge(act_emptied, EMPTIED["pT", n])
                lo = HD * (n % 2)
                v = vm_s[:, :, n * HD:(n + 1) * HD] if n < MHEADS else v_s[:, :, (n - MHEADS) * HD:(n - MHEADS + 1) * HD]
                nc.tensor.matmul(t[lo:lo + HD, 0:S], v[:, 0, :], pT_s[:, n % 2, 0:S], start=True, stop=False)
                if n < MHEADS:
                    ins = nc.tensor.matmul(t[lo:lo + HD, 0:S], v[:, 1, :], pT_s[:, n % 2, S:2 * S], start=False,
                                           stop=True)
                else:
                    ins = nc.tensor.matmul(t[lo:lo + HD, P:S], v[:, 1, :], pT_s[:, n % 2, S:S + P], start=False,
                                           stop=True)
                done(ins)

            def gate(m):
                chunk_T(fill(("gate", m))[:, 0:S], True)

            nh = MHEADS + HEADS
            pe.wait_ge(act_emptied, EMPTIED["vm"])
            scores(0)
            for n in range(nh):
                gate(2 * n)
                turn_p(n)
                if n + 1 == MHEADS:
                    pe.wait_ge(act_emptied, EMPTIED["kT", 1])
                if n + 1 < nh:
                    scores(n + 1)
                gate(2 * n + 1)
                attend(n)

            pe.wait_ge(dve_emptied, EMPTIED["o", nh - 1])
            for f in range(KC):
                hi, lo = next_unit()
                k0 = 0
                for i, name in enumerate(("attn", "pool", "mem")):
                    t = fill(("br", f, i))
                    y_hi, y_lo = y_parts[name]
                    chunks = y_hi.shape[1]
                    for k in range(chunks):
                        ins = three_passes(t[:, 0:S], (hi[:, k0 + k, :], lo[:, k0 + k, :]),
                                           (y_hi[:, k, :], y_lo[:, k, :]), k == 0, k == chunks - 1)
                    k0 += chunks
                    done(ins)
            n0 = block_arrived(pe, "O0")
            n1 = block_arrived(pe, "O1")

            def project_out(b, hf):
                t = fill(("out", b, hf))
                w = ring_block(n1 if hf else n0, 512)
                for k in range(KC):
                    if b == 0 and hf == 0:
                        pe.wait_ge(merged_ready, k + 1)
                    ins = nc.tensor.matmul(t, merged[:, k, b * P:(b + 1) * P], w[:, k, :], start=(k == 0),
                                           stop=(k == KC - 1))
                done(ins)

            def turn_h(b, hf):
                t = fill(("x2T", b, hf))
                pe.wait_ge(scaled, 2 * B + 2 * b + hf + 1)
                for c in range(4):
                    k = 4 * hf + c
                    ins = nc.tensor.transpose(t[:, c * P:(c + 1) * P], xn2[:, b, k * P:(k + 1) * P], ident[:])
                done(ins)

            project_out(0, 0)
            project_out(0, 1)
            project_out(1, 0)
            turn_h(0, 0)
            turn_h(0, 1)
            project_out(1, 1)
            t_logits = fill("logits")
            pe.wait_ge(got_router, 16)

            def logits(b):
                pe.wait_ge(act_emptied, EMPTIED["x2T", b, 1])
                for k in range(KC):
                    ins = nc.tensor.matmul(t_logits[:, b * NE:(b + 1) * NE], x2T[:, k, b * P:(b + 1) * P], wr_s[:, k, :],
                                           start=(k == 0), stop=(k == KC - 1))
                return ins

            logits(0)
            turn_h(1, 0)
            turn_h(1, 1)
            done(logits(1))
            t = fill("pos")
            pe.wait_ge(selected, 1)
            pe.wait_ge(ones_set, 1)
            nc.tensor.matmul(t[:, 0:NE], before[:], sel[:, 0, :], start=True, stop=True)
            nc.tensor.matmul(t[:, NE:2 * NE], ones[:], sel[:, 0, :], start=True, stop=False)
            done(nc.tensor.matmul(t[:, NE:2 * NE], before[:], sel[:, 1, :], start=False, stop=True))
            t = fill("total")
            nc.tensor.matmul(t[:, 0:NE], ones[:], sel[:, 0, :], start=True, stop=False)
            done(nc.tensor.matmul(t[:, 0:NE], ones[:], sel[:, 1, :], start=False, stop=True))
            def gather(n):
                pe.wait_ge(slots_ready, n + 1)
                for k in range(KC):
                    for b in range(B):
                        ins = nc.tensor.matmul(psum[:, 2, k * SLOTS:(k + 1) * SLOTS], xn2[:, b, k * P:(k + 1) * P],
                                               sel_slot[:, b, :], start=(b == 0), stop=(b == B - 1))
                ins.then_inc(gathered, 1)

            def put_back(n):
                pe.wait_ge(y_ready, n + 1)
                pe.wait_ge(putT_ready, n + 1)
                for j in range(4):
                    b, hf = j // 2, j % 2
                    pe.wait_ge(added, 4 * n + j + 1)
                    nc.tensor.matmul(psum[:, 4 + 3 * (j % 2), :], putT[:, b, :], y_s[:, hf * 512:hf * 512 + 512],
                                     start=True, stop=True).then_inc(put_done, 1)

            last = [name for name, _ in JOBS if BANK[name] == 2][-1]
            pe.wait_ge(emptied[OWNER[last]], EMPTIED[last])
            gather(0)
            pe.wait_ge(dve_emptied, EMPTIED["total"])
            pe.wait_ge(act_emptied, EMPTIED["x2T", 1, 1])
            pe.wait_ge(parts_ready, 1)
            pe.wait_ge(route_done, 1)
            rounds = rounds_of(pe)

            def piece(u, n, n_group):
                m = u * PIECES + n
                s = SLOT_OF[m]
                pe.wait_ge(got_piece[s], 16 * (n_group * USES[s] + USE_OF[m] + 1))
                return wslot[s]

            with pe.Fori(0, rounds) as r:
                with pe.Fori(0, NE // GROUP) as g:
                    n_group = r * (NE // GROUP) + g
                    for u in range(GROUP):
                        e = g * GROUP + u
                        i = r * NE + e
                        pe.wait_ge(xe_ready, i + 1)
                        tiles = ((0, 0), (SLOTS, 512))
                        for k in range(UP_CHUNKS):
                            if k == 2:
                                put_back(i)
                            w = piece(u, k, n_group)
                            for c in range(2):
                                for lo, col in tiles:
                                    at = col + FE * c
                                    ins = nc.tensor.matmul(psum[lo:lo + SLOTS, c, :], xeT[:, k, :], w[:, at:at + 512],
                                                           start=(k == 0), stop=False)
                            ins.then_inc(piece_used, 1)
                        pe.wait_ge(put_ready, i + 1)
                        for c in range(2):
                            for lo, col in tiles:
                                ins = nc.tensor.matmul(psum[lo:lo + SLOTS, c, :], hot[0:96, :],
                                                       b_part[0:96, col + FE * c:col + FE * c + 512], start=False, stop=True)
                        ins.then_inc(up_done, 1)
                        gather(i + 1)
                        for b in range(B):
                            ins = nc.tensor.transpose(psum[:, 3, b * P:(b + 1) * P], put[:, b, :], ident[:])
                        ins.then_inc(put_turned, 1)
                        pe.wait_ge(xe_ready, i + 2)
                        pe.wait_ge(act_ready, i + 1)
                        for q in range(KC // 2):
                            ins = nc.tensor.transpose(psum[:, 2, q * P:(q + 1) * P], act_s[:, q * P:(q + 1) * P], ident[:])
                        ins.then_inc(act_turned, 1)
                        pe.wait_ge(actT_ready, i + 1)
                        for j in range(DOWN_SLOTS):
                            w = piece(u, UP_CHUNKS + j, n_group)
                            for c in range(2):
                                for t_ in range(2):
                                    at = t_ * D + 512 * c
                                    f = 2 * j + t_
                                    lhsT = actT[:, f % 4, (f // 4) * SLOTS:(f // 4 + 1) * SLOTS]
                                    ins = nc.tensor.matmul(psum[t_ * SLOTS:(t_ + 1) * SLOTS, 5 + c, :], lhsT,
                                                           w[:, at:at + 512], start=(j == 0),
                                                           stop=(j == DOWN_SLOTS - 1))
                            ins.then_inc(piece_used, 1)
                            if j == 0:
                                for c in range(2):
                                    at = UP_W + 512 * c
                                    nc.tensor.matmul(psum[0:SLOTS, 5 + c, :], hot[0:96, :], b_part[0:96, at:at + 512],
                                                     start=False, stop=False)
            put_back(NE * rounds)


def shape_constants():
    import numpy as np
    f = np.float32
    iota = np.tile(np.arange(SLOTS, dtype=f), (P, P // SLOTS))
    before = np.triu(np.ones((P, P), f), 1)
    causal = np.where(np.arange(P)[None, :] <= np.arange(P)[:, None], f(0), f(-BIG)).astype(f)
    inv = np.power(f(500000.0), -np.arange(HALF, dtype=f) / f(HALF)).astype(f)
    ang = np.arange(S, dtype=f)[:, None] * inv[None, :]
    cos, sin = np.cos(ang).astype(f), np.sin(ang).astype(f)
    rope = np.concatenate([cos, cos, -sin, sin], axis=1)
    t = np.arange(S)
    pool = np.zeros((S, G, S), f)
    for g, w in enumerate((2, 4, 8, 16)):
        lo = np.maximum(t + 1 - w, 0)
        inside = (t[:, None] >= lo[None, :]) & (t[:, None] <= t[None, :])
        pool[:, g, :] = inside / (t + 1 - lo)[None, :] - (t[:, None] == t[None, :])
    expert = np.tile(np.eye(NE, dtype=f), (3, 1))
    return {"ident": np.eye(P, dtype=f), "iota": iota, "before": before, "causal": causal, "rope": rope,
            "pool": pool, "expert": expert}


_INS = ["x", "mem", "w_in", "w_gate", "w_proj_attn", "w_proj_pool", "w_proj_mem", "gains", "pool_w_group", "w_mem_kv",
        "w_out", "norm_ffn_g", "w_router", "b_router", "w_up", "b_up", "w_down", "b_down", "norm_final_g",
        "c_ident", "c_iota", "c_before", "c_causal", "c_rope", "c_pool", "c_expert"]


def kernel(**inputs):
    import numpy as np
    import concourse.bacc as bacc
    from concourse.bass_utils import run_bass_kernel_spmd

    nc = bacc.Bacc("TRN2", target_bir_lowering=False, num_devices=1)
    data = {k: np.ascontiguousarray(v) for k, v in inputs.items()}
    data["gains"] = np.concatenate([data[k].reshape(-1, P) for k in
                                    ("norm_mix_g", "mem_norm_g", "pool_scale", "b_gate")])
    data["norm_final_g"] = data["norm_final_g"].reshape(1, D)
    for k, v in shape_constants().items():
        data["c_" + k] = v
    arrays, args = {}, []
    for name in _INS:
        a = data[name]
        arrays[f"in_{name}"] = a
        args.append(nc.dram_tensor(f"in_{name}", a.shape, mybir.dt.from_np(a.dtype), kind="ExternalInput").ap())
    args.append(nc.dram_tensor("out_0", (1, S, D), F32, kind="ExternalOutput").ap())
    hybrid_layer_kernel(nc, *args)
    r = run_bass_kernel_spmd(nc, [arrays], core_ids=[0])
    return r.results[0]["out_0"]
```
